# Optimizing a Trainium2 kernel written in Bass

```python
import math
import jax, jax.numpy as jnp
from jax import lax
import numpy as np

D_MODEL = 1024
BATCH = 1
SEQ = 256
DEPTH = 2

N_MIXERS = 2
N_A_LAYERS = (DEPTH + 1) // 2
N_B_LAYERS = DEPTH // 2

HGRN_EXPAND = 128
HGRN_HEADS = D_MODEL // HGRN_EXPAND
HGRN_FDIM = HGRN_HEADS * HGRN_EXPAND
HGRN_IDIM = D_MODEL // HGRN_HEADS
HGRN_CHUNK = 64

ATTN_HEADS = 8
ATTN_HEAD_DIM = D_MODEL // ATTN_HEADS
MOBA_BLOCK = 256
MOBA_TOPK = 3
MOBA_QCHUNK = 32

REL_BUCKETS = 32
REL_MAX_DISTANCE = 1024

D_FF = -(-(8 * D_MODEL) // (3 * 256)) * 256
RMS_EPS = 1e-6


def rms_norm(x, g):
    xf = x.astype(jnp.float32)
    y = xf * lax.rsqrt(jnp.mean(xf * xf, axis=-1, keepdims=True) + RMS_EPS)
    return (y * g.astype(jnp.float32)).astype(x.dtype)

def t5_bucket(dist):
    n = jnp.maximum(dist, 0)
    max_exact = REL_BUCKETS // 2
    nf = jnp.maximum(n, max_exact).astype(jnp.float32)
    large = max_exact + (jnp.log(nf / max_exact) / math.log(REL_MAX_DISTANCE / max_exact)
                         * (REL_BUCKETS - max_exact)).astype(jnp.int32)
    large = jnp.minimum(large, REL_BUCKETS - 1)
    return jnp.where(n < max_exact, n, large)

def hgrn2_mixer(h, w_in, w_out, lb, out_norm):
    b_, s_, _ = h.shape
    f32 = jnp.float32
    proj = h @ w_in
    q, fz, inp, og = jnp.split(proj, [HGRN_FDIM, 2 * HGRN_FDIM, 2 * HGRN_FDIM + D_MODEL], axis=-1)
    q = jax.nn.silu(q.astype(f32))
    lbf = lb.astype(f32)
    f = lbf + (1.0 - lbf) * jax.nn.sigmoid(fz.astype(f32))
    k = 1.0 - f
    logf = jnp.log(f)
    nc = s_ // HGRN_CHUNK

    def to_chunks(t, d):
        return t.reshape(b_, nc, HGRN_CHUNK, HGRN_HEADS, d).transpose(1, 0, 3, 2, 4)

    qc = to_chunks(q, HGRN_EXPAND)
    kc = to_chunks(k, HGRN_EXPAND)
    gc = to_chunks(logf, HGRN_EXPAND)
    ic = to_chunks(inp.astype(f32), HGRN_IDIM)
    causal = jnp.tril(jnp.ones((HGRN_CHUNK, HGRN_CHUNK), dtype=bool))

    def step(state, xs):
        qb, kb, gb, ib = xs
        cum = jnp.cumsum(gb, axis=2)
        diff = cum[:, :, :, None, :] - cum[:, :, None, :, :]
        decay = jnp.exp(jnp.where(causal[:, :, None], diff, -jnp.inf))
        scores = jnp.einsum('bhtn,bhsn,bhtsn->bhts', qb, kb, decay)
        o = (jnp.einsum('bhts,bhsd->bhtd', scores, ib)
             + jnp.einsum('bhtn,bhnd->bhtd', qb * jnp.exp(cum), state))
        last = cum[:, :, -1:, :]
        state = (state * jnp.exp(last[:, :, 0, :, None])
                 + jnp.einsum('bhsn,bhsd->bhnd', kb * jnp.exp(last - cum), ib))
        return state, o

    s0 = jnp.zeros((b_, HGRN_HEADS, HGRN_EXPAND, HGRN_IDIM), f32)
    _, o = lax.scan(step, s0, (qc, kc, gc, ic))
    o = o.transpose(1, 0, 3, 2, 4).reshape(b_, s_, D_MODEL)
    o = rms_norm(o, out_norm) * jax.nn.sigmoid(og.astype(f32))
    return (o.astype(h.dtype) @ w_out).astype(h.dtype)

def moba_mixer(h, w_in, w_out, rel_table):
    b_, s_, _ = h.shape
    f32 = jnp.float32
    nh, dh = ATTN_HEADS, ATTN_HEAD_DIM
    q, k, v = jnp.split(h @ w_in, 3, axis=-1)
    heads = lambda t: t.reshape(b_, s_, nh, dh).transpose(0, 2, 1, 3)
    q, k, v = heads(q), heads(k), heads(v)
    nb = -(-s_ // MOBA_BLOCK)
    pad = nb * MOBA_BLOCK - s_
    kp = jnp.pad(k, ((0, 0), (0, 0), (0, pad), (0, 0)))
    vp = jnp.pad(v, ((0, 0), (0, 0), (0, pad), (0, 0)))
    kb = kp.reshape(b_, nh, nb, MOBA_BLOCK, dh)
    vb = vp.reshape(b_, nh, nb, MOBA_BLOCK, dh)
    kmean = jnp.mean(kb.astype(f32), axis=3)
    scale = dh ** -0.5
    nqc = s_ // MOBA_QCHUNK
    qch = q.reshape(b_, nh, nqc, MOBA_QCHUNK, dh).transpose(2, 0, 1, 3, 4)
    bi = jnp.arange(b_)[:, None, None, None]
    hi = jnp.arange(nh)[None, :, None, None]
    table_t = rel_table.T
    topk = min(MOBA_TOPK, nb)
    kk = topk * MOBA_BLOCK

    def chunk(args):
        c, qb = args
        q0 = c * MOBA_QCHUNK
        qpos = q0 + jnp.arange(MOBA_QCHUNK)
        j = q0 // MOBA_BLOCK
        gate = jnp.einsum('bhqd,bhnd->bhqn', qb.astype(f32), kmean)
        gate = jnp.where(jnp.arange(nb) < j, gate, -jnp.inf)
        _, sel = lax.top_k(gate, topk)
        sel_ok = jnp.arange(topk) < j
        ks = kb[bi, hi, sel]
        vs = vb[bi, hi, sel]
        s_sel = jnp.einsum('bhqd,bhqkpd->bhqkp', qb, ks).astype(f32) * scale
        kpos_sel = sel[..., None] * MOBA_BLOCK + jnp.arange(MOBA_BLOCK)
        bias_sel = table_t[hi[..., None], t5_bucket(qpos[:, None, None] - kpos_sel)]
        s_sel = jnp.where(sel_ok[:, None], s_sel + bias_sel.astype(f32), -jnp.inf)
        kown = lax.dynamic_slice_in_dim(kp, j * MOBA_BLOCK, MOBA_BLOCK, axis=2)
        vown = lax.dynamic_slice_in_dim(vp, j * MOBA_BLOCK, MOBA_BLOCK, axis=2)
        dist_own = qpos[:, None] - (j * MOBA_BLOCK + jnp.arange(MOBA_BLOCK))[None, :]
        bias_own = rel_table[t5_bucket(dist_own)].transpose(2, 0, 1).astype(f32)
        s_own = jnp.einsum('bhqd,bhpd->bhqp', qb, kown).astype(f32) * scale + bias_own
        s_own = jnp.where(dist_own >= 0, s_own, -jnp.inf)
        logits = jnp.concatenate([s_sel.reshape(b_, nh, MOBA_QCHUNK, kk), s_own], axis=-1)
        p = jax.nn.softmax(logits, axis=-1).astype(vb.dtype)
        p_sel = p[..., :kk].reshape(b_, nh, MOBA_QCHUNK, topk, MOBA_BLOCK)
        p_own = p[..., kk:]
        return (jnp.einsum('bhqkp,bhqkpd->bhqd', p_sel, vs)
                + jnp.einsum('bhqp,bhpd->bhqd', p_own, vown))

    o = lax.map(chunk, (jnp.arange(nqc), qch))
    o = o.transpose(1, 0, 3, 2, 4).reshape(b_, s_, D_MODEL)
    return (o @ w_out).astype(h.dtype)

def swiglu(h, w13, w2):
    g, u = jnp.split(h @ w13, 2, axis=-1)
    return ((jax.nn.silu(g) * u) @ w2).astype(h.dtype)

def first_inputs(seed: int = 0) -> dict:
    key = jax.random.key(seed)
    ks = jax.random.split(key, 14)
    nrm = lambda k, shape, fan_in: jax.random.normal(k, shape, jnp.float32) * (fan_in ** -0.5)
    gain = lambda k, shape: 1.0 + 0.02 * jax.random.normal(k, shape, jnp.float32)
    return {
        "x": jax.random.normal(ks[0], (BATCH, SEQ, D_MODEL), jnp.float32),
        "norm_mix": gain(ks[1], (DEPTH, D_MODEL)),
        "norm_ffn": gain(ks[2], (DEPTH, D_MODEL)),
        "hgrn_w_in": nrm(ks[3], (N_A_LAYERS, D_MODEL, 2 * HGRN_FDIM + 2 * D_MODEL), D_MODEL),
        "hgrn_lb_logits": 1.0 + 0.1 * jax.random.normal(ks[4], (N_A_LAYERS + 1, HGRN_FDIM), jnp.float32),
        "hgrn_out_norm": gain(ks[5], (N_A_LAYERS, D_MODEL)),
        "hgrn_w_out": nrm(ks[6], (N_A_LAYERS, D_MODEL, D_MODEL), D_MODEL),
        "moba_w_in": nrm(ks[7], (N_B_LAYERS, D_MODEL, 3 * D_MODEL), D_MODEL),
        "moba_w_out": nrm(ks[8], (N_B_LAYERS, D_MODEL, D_MODEL), D_MODEL),
        "rel_bias_table": 0.5 * jax.random.normal(ks[9], (REL_BUCKETS, ATTN_HEADS), jnp.float32),
        "ffn_w13": nrm(ks[10], (DEPTH, D_MODEL, 2 * D_FF), D_MODEL),
        "ffn_w2": nrm(ks[11], (DEPTH, D_FF, D_MODEL), D_FF),
        "final_norm": gain(ks[12], (D_MODEL,)),
    }

def first_block(x, norm_mix, norm_ffn, hgrn_w_in, hgrn_lb_logits, hgrn_out_norm, hgrn_w_out,
              moba_w_in, moba_w_out, rel_bias_table, ffn_w13, ffn_w2, final_norm):
    lb_all = jnp.cumsum(jax.nn.softmax(hgrn_lb_logits.astype(jnp.float32), axis=0), axis=0)[:N_A_LAYERS]
    h = x
    for layer in range(DEPTH):
        y = rms_norm(h, norm_mix[layer])
        idx = layer // N_MIXERS
        if layer % N_MIXERS == 0:
            y = hgrn2_mixer(y, hgrn_w_in[idx], hgrn_w_out[idx], lb_all[idx], hgrn_out_norm[idx])
        else:
            y = moba_mixer(y, moba_w_in[idx], moba_w_out[idx], rel_bias_table)
        h = h + y
        h = h + swiglu(rms_norm(h, norm_ffn[layer]), ffn_w13[layer], ffn_w2[layer])
    return rms_norm(h, final_norm)


N_A_LAYERS_2 = DEPTH // 2
N_B_LAYERS_2 = DEPTH - N_A_LAYERS_2
D_FF_2 = 2816
CONV_WIDTH = 3
N_HEADS = 16
HEAD_DIM = D_MODEL // N_HEADS
N_KV_GROUPS = 4
HEADS_PER_GROUP = N_HEADS // N_KV_GROUPS
CMP_BLOCK = 32
CMP_STRIDE = 16
CMP_HIDDEN = 4 * HEAD_DIM
SEL_BLOCK = 64
N_SELECT = 16
WINDOW = 512
N_BRANCH = 3
N_KV_SLOTS = 6
QUERY_CHUNK = 32
EPS = 1e-6
FORCE_SCORE = 1e9
MASK_SCORE = -1e30


def _rmsnorm(x, g):
    xf = x.astype(jnp.float32)
    y = xf * lax.rsqrt(jnp.mean(xf * xf, axis=-1, keepdims=True) + EPS)
    return (y * g.astype(jnp.float32)).astype(x.dtype)

def _swiglu(x, w_gate_up, w_down):
    a, b = jnp.split(x @ w_gate_up, 2, axis=-1)
    return (jax.nn.silu(a) * b) @ w_down

def _short_conv(x, w_in, conv_w, w_out):
    b_gate, c_gate, u = jnp.split(x @ w_in, 3, axis=-1)
    v = c_gate * u
    conv = lax.conv_general_dilated(
        v, conv_w[:, None, :], window_strides=(1,), padding=[(CONV_WIDTH - 1, 0)],
        dimension_numbers=("NWC", "WIO", "NWC"), feature_group_count=D_MODEL)
    return (b_gate * conv) @ w_out

def _compress(x_raw, pos, w1, b1, w2):
    s = x_raw.shape[2]
    n_cmp = (s - CMP_BLOCK) // CMP_STRIDE + 1
    idx = np.arange(n_cmp)[:, None] * CMP_STRIDE + np.arange(CMP_BLOCK)[None, :]
    blocks = x_raw[:, :, idx] + pos
    flat = blocks.reshape(blocks.shape[:3] + (CMP_BLOCK * HEAD_DIM,))
    return jax.nn.gelu(flat @ w1 + b1) @ w2

def _shared_kv(h, kv_norm, kv_w, cmp_pos, cmp_w1, cmp_b1, cmp_w2, k_norm):
    b, s, _ = h.shape
    kv = (_rmsnorm(h, kv_norm) @ kv_w).reshape(b, s, N_KV_SLOTS, N_KV_GROUPS, HEAD_DIM)
    kv = jnp.transpose(kv, (2, 0, 3, 1, 4))
    k_cmp = _rmsnorm(_compress(kv[0], cmp_pos[0], cmp_w1[0], cmp_b1[0], cmp_w2[0]), k_norm[0])
    v_cmp = _compress(kv[1], cmp_pos[1], cmp_w1[1], cmp_b1[1], cmp_w2[1])
    n_blk = s // SEL_BLOCK
    k_sel = _rmsnorm(kv[2], k_norm[1]).reshape(b, N_KV_GROUPS, n_blk, SEL_BLOCK, HEAD_DIM)
    v_sel = kv[3].reshape(b, N_KV_GROUPS, n_blk, SEL_BLOCK, HEAD_DIM)
    pad = ((0, 0), (0, 0), (WINDOW, 0), (0, 0))
    k_win = jnp.pad(_rmsnorm(kv[4], k_norm[2]), pad)
    v_win = jnp.pad(kv[5], pad)
    return (k_cmp, v_cmp, k_sel, v_sel, k_win, v_win)

def _softmax_f32(logits, mask):
    return jax.nn.softmax(jnp.where(mask, logits, MASK_SCORE), axis=-1)

def _nsa(x, w_qg, q_norm, w_o, k_cmp, v_cmp, k_sel, v_sel, k_win, v_win):
    b, s, _ = x.shape
    n_chunk = s // QUERY_CHUNK
    n_cmp = k_cmp.shape[2]
    n_blk = k_sel.shape[2]
    n_sel = min(N_SELECT, n_blk)
    scale = HEAD_DIM ** -0.5

    proj = x @ w_qg
    q = _rmsnorm(proj[..., :N_HEADS * HEAD_DIM].reshape(b, s, N_HEADS, HEAD_DIM), q_norm)
    gate = jax.nn.sigmoid(proj[..., N_HEADS * HEAD_DIM:].astype(jnp.float32))
    q = q.reshape(b, n_chunk, QUERY_CHUNK, N_KV_GROUPS, HEADS_PER_GROUP, HEAD_DIM)
    q = q.transpose(1, 0, 3, 4, 2, 5)
    gate = gate.reshape(b, n_chunk, QUERY_CHUNK, N_KV_GROUPS, HEADS_PER_GROUP, N_BRANCH)
    gate = gate.transpose(1, 0, 3, 4, 2, 5)

    cmp_start = np.arange(n_cmp) * CMP_STRIDE
    cmp_end = cmp_start + CMP_BLOCK - 1
    blk_start = np.arange(n_blk) * SEL_BLOCK
    overlap = ((cmp_start[:, None] < blk_start[None, :] + SEL_BLOCK)
               & (cmp_start[:, None] + CMP_BLOCK > blk_start[None, :])).astype(np.float32)
    gather_blocks = jax.vmap(jax.vmap(lambda kb, ib: kb[ib]))
    blk_ids = jnp.arange(n_blk)

    def chunk_fn(args):
        c, qc, gc = args
        t = c * QUERY_CHUNK + jnp.arange(QUERY_CHUNK)
        logits = jnp.einsum("bghtd,bgnd->bghtn", qc, k_cmp).astype(jnp.float32) * scale
        valid = cmp_end[None, :] <= t[:, None]
        p_cmp = _softmax_f32(logits, valid) * valid
        o_cmp = jnp.einsum("bghtn,bgnd->bghtd", p_cmp.astype(v_cmp.dtype), v_cmp)
        imp = jnp.einsum("bghtn,nj->bgtj", p_cmp, overlap)
        cur = (t // SEL_BLOCK)[:, None]
        forced = (blk_ids[None] == 0) | (blk_ids[None] == cur) | (blk_ids[None] == cur - 1)
        imp = jnp.where(forced, FORCE_SCORE, imp)
        imp = jnp.where(blk_ids[None] > cur, MASK_SCORE, imp)
        _, idx = lax.top_k(imp, n_sel)
        ks = gather_blocks(k_sel, idx).reshape(b, N_KV_GROUPS, QUERY_CHUNK, n_sel * SEL_BLOCK, HEAD_DIM)
        vs = gather_blocks(v_sel, idx).reshape(b, N_KV_GROUPS, QUERY_CHUNK, n_sel * SEL_BLOCK, HEAD_DIM)
        kpos = (idx[..., None] * SEL_BLOCK + jnp.arange(SEL_BLOCK)).reshape(
            b, N_KV_GROUPS, QUERY_CHUNK, n_sel * SEL_BLOCK)
        smask = (kpos <= t[:, None])[:, :, None]
        logits = jnp.einsum("bghtd,bgtkd->bghtk", qc, ks).astype(jnp.float32) * scale
        p_sel = _softmax_f32(logits, smask)
        o_sel = jnp.einsum("bghtk,bgtkd->bghtd", p_sel.astype(vs.dtype), vs)
        start = c * QUERY_CHUNK
        kw = lax.dynamic_slice_in_dim(k_win, start, WINDOW + QUERY_CHUNK, axis=2)
        vw = lax.dynamic_slice_in_dim(v_win, start, WINDOW + QUERY_CHUNK, axis=2)
        wpos = start - WINDOW + jnp.arange(WINDOW + QUERY_CHUNK)
        wmask = ((wpos[None] <= t[:, None]) & (wpos[None] > t[:, None] - WINDOW)
                 & (wpos[None] >= 0))
        logits = jnp.einsum("bghtd,bgkd->bghtk", qc, kw).astype(jnp.float32) * scale
        p_win = _softmax_f32(logits, wmask)
        o_win = jnp.einsum("bghtk,bgkd->bghtd", p_win.astype(vw.dtype), vw)
        out = gc[..., 0:1] * o_cmp + gc[..., 1:2] * o_sel + gc[..., 2:3] * o_win
        return out.astype(qc.dtype)

    outs = lax.map(chunk_fn, (jnp.arange(n_chunk), q, gate))
    o = outs.transpose(1, 0, 4, 2, 3, 5).reshape(b, s, N_HEADS * HEAD_DIM)
    return o @ w_o

def second_inputs(seed: int = 0) -> dict:
    key = jax.random.key(seed)
    ks = jax.random.split(key, 20)
    nrm = lambda k, shape, scale: jax.random.normal(k, shape, jnp.float32) * scale
    gain = lambda k, shape: 1.0 + 0.02 * jax.random.normal(k, shape, jnp.float32)
    qg_width = N_HEADS * HEAD_DIM + N_BRANCH * N_HEADS
    return {
        "x": nrm(ks[0], (BATCH, SEQ, D_MODEL), 1.0),
        "ffn_norm": gain(ks[1], (DEPTH, 2, D_MODEL)),
        "ffn_w_gate_up": nrm(ks[2], (DEPTH, 2, D_MODEL, 2 * D_FF_2), D_MODEL ** -0.5),
        "ffn_w_down": nrm(ks[3], (DEPTH, 2, D_FF_2, D_MODEL), D_FF_2 ** -0.5),
        "mix_norm": gain(ks[4], (DEPTH, D_MODEL)),
        "conv_w_in": nrm(ks[5], (N_A_LAYERS_2, D_MODEL, 3 * D_MODEL), D_MODEL ** -0.5),
        "conv_w": nrm(ks[6], (N_A_LAYERS_2, CONV_WIDTH, D_MODEL), CONV_WIDTH ** -0.5),
        "conv_w_out": nrm(ks[7], (N_A_LAYERS_2, D_MODEL, D_MODEL), D_MODEL ** -0.5),
        "kv_norm": gain(ks[8], (D_MODEL,)),
        "kv_w": nrm(ks[9], (D_MODEL, N_KV_SLOTS * N_KV_GROUPS * HEAD_DIM), D_MODEL ** -0.5),
        "cmp_pos": nrm(ks[10], (2, CMP_BLOCK, HEAD_DIM), 0.1),
        "cmp_w1": nrm(ks[11], (2, CMP_BLOCK * HEAD_DIM, CMP_HIDDEN), (CMP_BLOCK * HEAD_DIM) ** -0.5),
        "cmp_b1": nrm(ks[12], (2, CMP_HIDDEN), 0.01),
        "cmp_w2": nrm(ks[13], (2, CMP_HIDDEN, HEAD_DIM), CMP_HIDDEN ** -0.5),
        "k_norm": gain(ks[14], (N_BRANCH, HEAD_DIM)),
        "nsa_w_qg": nrm(ks[15], (N_B_LAYERS_2, D_MODEL, qg_width), D_MODEL ** -0.5),
        "q_norm": gain(ks[16], (N_B_LAYERS_2, HEAD_DIM)),
        "nsa_w_o": nrm(ks[17], (N_B_LAYERS_2, N_HEADS * HEAD_DIM, D_MODEL), (N_HEADS * HEAD_DIM) ** -0.5),
    }

def second_block(x, ffn_norm, ffn_w_gate_up, ffn_w_down, mix_norm, conv_w_in, conv_w, conv_w_out,
              kv_norm, kv_w, cmp_pos, cmp_w1, cmp_b1, cmp_w2, k_norm, nsa_w_qg, q_norm, nsa_w_o):
    h = x
    shared = None
    for layer in range(DEPTH):
        h = h + 0.5 * _swiglu(_rmsnorm(h, ffn_norm[layer, 0]), ffn_w_gate_up[layer, 0], ffn_w_down[layer, 0])
        hn = _rmsnorm(h, mix_norm[layer])
        if layer < N_A_LAYERS_2:
            h = h + _short_conv(hn, conv_w_in[layer], conv_w[layer], conv_w_out[layer])
        else:
            i = layer - N_A_LAYERS_2
            h = h + _nsa(hn, nsa_w_qg[i], q_norm[i], nsa_w_o[i], *shared)
        h = h + 0.5 * _swiglu(_rmsnorm(h, ffn_norm[layer, 1]), ffn_w_gate_up[layer, 1], ffn_w_down[layer, 1])
        if layer == N_A_LAYERS_2 - 1:
            shared = _shared_kv(h, kv_norm, kv_w, cmp_pos, cmp_w1, cmp_b1, cmp_w2, k_norm)
    return h


def setup_inputs(seed=0):
    out = dict(first_inputs(seed))
    for name, value in second_inputs(seed + 1).items():
        if name != "x":
            out[name + "_2"] = value
    return out


def reference(
    x, norm_mix, norm_ffn, hgrn_w_in, hgrn_lb_logits, hgrn_out_norm, hgrn_w_out, moba_w_in,
    moba_w_out, rel_bias_table, ffn_w13, ffn_w2, final_norm, ffn_norm_2, ffn_w_gate_up_2,
    ffn_w_down_2, mix_norm_2, conv_w_in_2, conv_w_2, conv_w_out_2, kv_norm_2, kv_w_2, cmp_pos_2,
    cmp_w1_2, cmp_b1_2, cmp_w2_2, k_norm_2, nsa_w_qg_2, q_norm_2, nsa_w_o_2,
):
    x = first_block(
        x, norm_mix, norm_ffn, hgrn_w_in, hgrn_lb_logits, hgrn_out_norm, hgrn_w_out, moba_w_in,
        moba_w_out, rel_bias_table, ffn_w13, ffn_w2, final_norm,
    )
    return second_block(
        x, ffn_norm_2, ffn_w_gate_up_2, ffn_w_down_2, mix_norm_2, conv_w_in_2, conv_w_2,
        conv_w_out_2, kv_norm_2, kv_w_2, cmp_pos_2, cmp_w1_2, cmp_b1_2, cmp_w2_2, k_norm_2,
        nsa_w_qg_2, q_norm_2, nsa_w_o_2,
    )


_drawn_inputs = setup_inputs


def setup_inputs(seed=0):
    import zlib

    import numpy as np

    out = dict(_drawn_inputs(seed))
    spreads = {}
    factors = {'hgrn_lb_logits': 3.886,
     'hgrn_out_norm': 2.91,
     'ffn_norm_2': 3.543,
     'kv_norm_2': 8.0,
     'cmp_pos_2': 3.013,
     'cmp_b1_2': 43.528,
     'k_norm_2': 8.0,
     'q_norm_2': 8.0}
    for name, (base, spread) in spreads.items():
        noise = np.random.default_rng([zlib.crc32(name.encode()), seed]).standard_normal(out[name].shape)
        drawn = base * np.exp(spread * noise) if base else spread * noise
        out[name] = __import__('jax').numpy.asarray(drawn.astype(out[name].dtype))
    for name, factor in factors.items():
        out[name] = (out[name] * factor).astype(out[name].dtype)
    return out
```

```python
from contextlib import ExitStack

import numpy as np

import concourse.bass as bass
from concourse import mybir

F32 = mybir.dt.float32
F32R = mybir.dt.float32r
BF16 = mybir.dt.bfloat16
U32 = mybir.dt.uint32
ALU = mybir.AluOpType
ACT = mybir.ActivationFunctionType
AX = mybir.AxisListType

P = 128
S = 256
TT = S // P
D = 1024
KT = D // P
CW = 256
RING = 3
HEADS = 8
F_FF = 2816
PAIRS = F_FF // CW
EPS = 1e-6
NEG = -1e30
LEVELS = 8
NH = 16
HD = 64
NG = 4
CMP_STRIDE, CMP_BLOCK = 16, 32
N_CMP = (S - CMP_BLOCK) // CMP_STRIDE + 1
TAIL = 48
BUCKETS, MAX_DISTANCE = 32, 1024

C_MASK = 0
C_CAUSAL = C_MASK + LEVELS * P
C_CMP = C_CAUSAL + 3 * P
C_VALID = C_CMP + TT * N_CMP
C_ONE = C_VALID + TT * N_CMP
C_HALF = C_ONE + 2
C_COLS = C_HALF + NH * TT

R_ONORM, R_LB, R_CONV, R_B1, R_POS = 0, 8, 24, 48, 52
ROWS = R_POS + 32

PHASES = ["hgrn", "ffn0", "moba", "ffn1", "final", "ffn2", "conv", "ffn3", "kv", "ffn4", "nsa", "ffn5"]


def constants():
    c = np.zeros((P, C_COLS), np.float32)
    s, t = np.arange(P)[:, None], np.arange(P)[None, :]
    c[:, :P] = s == t
    for level in range(LEVELS - 1):
        m = 1 << level
        keep = (s // (2 * m) == t // (2 * m)) & (s // m % 2 == 0) & (t // m % 2 == 1)
        c[:, C_MASK + (level + 1) * P:C_MASK + (level + 2) * P] = keep
    diagonal = np.where(np.arange(P)[None, :] <= np.arange(P)[:, None], 0, NEG)
    c[:, C_CAUSAL:C_CAUSAL + P] = diagonal
    c[:, C_CAUSAL + 2 * P:C_CAUSAL + 3 * P] = diagonal
    end = np.arange(N_CMP) * CMP_STRIDE + CMP_BLOCK - 1
    for tt in range(TT):
        valid = end[None, :] <= (tt * P + np.arange(P))[:, None]
        c[:, C_CMP + tt * N_CMP:C_CMP + (tt + 1) * N_CMP] = np.where(valid, 0, NEG)
        c[:, C_VALID + tt * N_CMP:C_VALID + (tt + 1) * N_CMP] = valid
    c[:, C_ONE:C_ONE + 2] = 1
    c[:, C_HALF:C_HALF + NH * TT] = -0.5
    dist = S - 1 - np.arange(2 * S)
    n = np.maximum(dist, 0)
    exact = BUCKETS // 2
    far = np.log(np.maximum(n, exact).astype(np.float32) / np.float32(exact)) / np.float32(np.log(MAX_DISTANCE / exact))
    far = exact + (far * np.float32(BUCKETS - exact)).astype(np.int32)
    bucket = np.where(n < exact, n, np.minimum(far, BUCKETS - 1))
    places = np.zeros((BUCKETS + 1, 2 * S), np.float32)
    places[bucket, np.arange(2 * S)] = dist >= 0
    places[BUCKETS] = dist < 0
    return c, places


class Place:

    def __init__(self):
        self.chunk = 0
        self.split = 0
        self.h = 0
        self.sums = 0
        self.turned = 0
        self.xn = 0
        self.gains = 0
        self.hids = 0
        self.y = 0
        self.fills = [0] * 8
        self.att = 0
        self.pscaled = 0


def build(nc, w, out, phases=PHASES):
    with ExitStack() as ctx:
        def sb(name, shape, dt=F32):
            return ctx.enter_context(nc.sbuf_tensor(name, shape, dt))

        def sem(name):
            return ctx.enter_context(nc.semaphore(name))

        ps = ctx.enter_context(nc.psum_tensor("ps", [P, 8, 512], F32))

        raw = [sb(f"raw{n}", [P, 2048]) for n in range(RING)]
        whi = [sb(f"whi{n}", [P, 2048], F32R) for n in range(RING)]
        wlo = [sb(f"wlo{n}", [P, 2048], F32R) for n in range(RING)]
        h = sb("h", [P, TT, D])
        xn = sb("xn", [P, TT, D])
        xhi = sb("xhi", [P, KT, S], F32R)
        xlo = sb("xlo", [P, KT, S], F32R)
        gain = [sb(f"gain{n}", [P, D]) for n in range(2)]
        junk = sb("junk", [P, D])
        silu = sb("silu", [P, 2, S])
        hid = sb("hid", [P, 2, S])
        hhi = sb("hhi", [P, 2, S], F32R)
        hlo = sb("hlo", [P, 2, S], F32R)
        ss = sb("ss", [P, TT])
        ms = sb("ms", [P, TT])
        rstd = sb("rstd", [P, TT])
        const = sb("const", [P, C_COLS])
        zero = sb("zero", [P, 512], BF16)
        rows = sb("rows", [ROWS, P])
        cols = sb("cols", [P, ROWS])
        arena = sb("arena", [P, 13312])

        def area(start, *dims):
            n = int(np.prod(dims))
            assert start + n <= 13312
            v = arena[:, start:start + n]
            if len(dims) == 2:
                v = v.rearrange("p (a b) -> p a b", b=dims[1])
            if len(dims) == 3:
                v = v.rearrange("p (a b c) -> p a b c", b=dims[1], c=dims[2])
            return v

        ident = const[:, 0:P]
        one = const[:, C_ONE:C_ONE + 1]
        causal = const[:, C_CAUSAL:C_CAUSAL + 3 * P]

        gq = area(0, HEADS, S)
        gk = area(2048, HEADS, S)
        gf = [area(4096, HEADS, S), area(6144, HEADS, P)]
        gsig = area(7168, HEADS, S)
        gsc = area(9216, HEADS, 3, P)
        gin = xn
        lbw = sb("lbw", [P, 6, HEADS])
        orms = sb("orms", [P, 2, TT])

        att_l = area(9216, 2, 2, 3 * P)
        att_pt = area(10752, 2, 2, 3 * P)
        nmax = sb("nmax", [P, 2, 4])
        sums = sb("sums", [P, 2, 4])
        coef = sb("coef", [P, 2, 4])

        mq = area(0, HEADS, S)
        mk = area(2048, HEADS, S)
        mv = area(4096, TT, D)
        mbias = area(6144, HEADS, 3 * P)
        table = sb("table_sb", [BUCKETS + 1, HEADS])
        places = sb("places_sb", [BUCKETS + 1, 2 * S])
        bias_row = sb("bias_row", [HEADS, 2 * S])
        bias_dram = nc.dram_tensor("bias_rows", [P, HEADS, 2 * S], F32, kind="Internal").ap()

        cpad = area(0, 2, S + 2)
        cgate = area(516, 2, S)
        cacc = area(1028, 2, S)
        cy = area(2048, KT, S)

        raw_t = area(0, 2, 2, S)
        pairs_t = area(1024, 2, NG, S)
        cz = area(3072, 4, NG * N_CMP)
        cz2 = area(3328, 4, NG * N_CMP)
        csig = area(3584, 4, NG * N_CMP)
        kn = area(4096, 17, HD)
        kd = area(9216, 17, 2, HD)
        kt = area(6144, 2, NG, S)
        vn = area(8192, 2, TT, NG * HD)
        kct = area(12288, NG * N_CMP)
        vc = area(12352, NG, HD)
        kss = sb("kss", [P, 2, 17])
        krs = sb("krs", [P, 17])
        kgain = sb("kgain", [P, 3, HD])
        qgain = sb("qgain", [P, HD])
        w2sb = sb("w2sb", [P, 4, HD])
        b1col = sb("b1col", [P, 4])

        nq = area(0, NH // 2, S)
        cl = area(2048, TT, NH * N_CMP)
        cp = area(2560, TT, NH, 32)
        cpt = area(3584, NG, S)
        qsq = area(4608, NH, HD)
        gates = sb("gates", [P, TT, TAIL])
        qss = sb("qss", [P, 2, TT * NH])
        qrs = sb("qrs", [P, TT * NH])
        cmx = sb("cmx", [P, TT * NH])
        csum = sb("csum", [P, 2, TT * NH])

        landed = [sem(f"chunk_landed{n}") for n in range(RING)]
        split_hi = sem("split_hi")
        split_lo = sem("split_lo")
        chunk_used = sem("chunk_used")
        bank_free = [sem(f"bank_free{n}") for n in range(8)]
        x_landed = sem("x_landed")
        const_landed = sem("const_landed")
        gain_landed = [sem(f"gain_landed{n}") for n in range(2)]
        h_ready = sem("h_ready")
        squares_summed = sem("squares_summed")
        ms_ready = sem("ms_ready")
        rstd_ready = sem("rstd_ready")
        xn_ready = sem("xn_ready")
        turned = sem("turned")
        xhi_ready = sem("xhi_ready")
        silu_ready = sem("silu_ready")
        hid_ready = sem("hid_ready")
        hhi_ready = sem("hhi_ready")
        hlo_ready = sem("hlo_ready")
        zero_ready = sem("zero_ready")
        cols_turned = sem("cols_turned")
        cols_ready = sem("cols_ready")
        dve_wrote = sem("dve_wrote")
        lb_exp = sem("lb_exp")
        lb_shift = sem("lb_shift")
        q_sig = sem("q_sig")
        qk_ready = sem("qk_ready")
        level_scored = sem("level_scored")
        o_ready = sem("o_ready")
        o_squared = sem("o_squared")
        y_ready = sem("y_ready")
        yhi_ready = sem("yhi_ready")
        ylo_ready = sem("ylo_ready")
        dve_round = sem("conv_rounds_done")
        o_summed = sem("o_summed")
        orms_ready = sem("orms_ready")
        out_landed = sem("out_landed")
        bias_rowed = sem("bias_rowed")
        bias_copied = sem("bias_copied")
        bias_stored = sem("bias_stored")
        bias_landed = sem("bias_landed")
        scored = sem("scored")
        max_ready = sem("max_ready")
        exp_ready = sem("exp_ready")
        probs_ready = sem("probs_ready")
        probs_turned = sem("probs_turned")
        pt_ready = sem("pt_ready")
        pv_done = sem("pv_done")
        conv_done = sem("conv_done")
        gate_kept = sem("gate_kept")
        raw_kept = sem("raw_kept")
        pairs_landed = sem("pairs_landed")
        blocks_hi = sem("blocks_hi")
        blocks_lo = sem("blocks_lo")
        gelu_in = sem("gelu_in")
        gelu_sig = sem("gelu_sig")
        gelu_ready = sem("gelu_ready")
        cmp_done = sem("cmp_done")
        kn_kept = sem("kn_kept")
        kms_ready = sem("kms_ready")
        krs_ready = sem("krs_ready")
        kd_ready = sem("kd_ready")
        kt_turned = sem("kt_turned")
        kt_kept = sem("kt_kept")
        vc_kept = sem("vc_kept")
        q_kept = sem("q_kept")
        qms_ready = sem("qms_ready")
        qrs_ready = sem("qrs_ready")
        qn_ready = sem("qn_ready")
        q_turned = sem("q_turned")
        nq_ready = sem("nq_ready")
        gates_ready = sem("gates_ready")
        cmp_scored = sem("cmp_scored")
        cmp_shifted = sem("cmp_shifted")
        cmp_exp = sem("cmp_exp")
        cmp_probs = sem("cmp_probs")
        cmp_turned = sem("cmp_turned")
        cpt_ready = sem("cpt_ready")
        zeroed = sem("zeroed")
        small_landed = sem("small_landed")

        def columns(matrix, at):
            return matrix.rearrange("(k p) n -> p k n", p=P)[:, :, bass.ds(at, CW)]

        def down_rows(matrix, at):
            return matrix[bass.ds(at, CW), :].rearrange("(k p) n -> p k n", p=P)

        ffn_up = [w["ffn_w13"][0], w["ffn_w13"][1]] + [w["ffn_w_gate_up_2"][a, b] for a in range(2) for b in range(2)]
        ffn_down = [w["ffn_w2"][0], w["ffn_w2"][1]] + [w["ffn_w_down_2"][a, b] for a in range(2) for b in range(2)]
        gains = {
            "hgrn": w["norm_mix"][0], "ffn0": w["norm_ffn"][0], "moba": w["norm_mix"][1], "ffn1": w["norm_ffn"][1],
            "final": w["final_norm"], "ffn2": w["ffn_norm_2"][0, 0], "conv": w["mix_norm_2"][0],
            "ffn3": w["ffn_norm_2"][0, 1], "kv": w["kv_norm_2"], "ffn4": w["ffn_norm_2"][1, 0],
            "nsa": w["mix_norm_2"][1], "ffn5": w["ffn_norm_2"][1, 1],
        }
        gain_rows = [gains[name] for name in phases]
        out_w = {"hgrn": w["hgrn_w_out"][0], "moba": w["moba_w_out"][0], "conv": w["conv_w_out_2"][0], "nsa": w["nsa_w_o_2"][0]}

        def thirds(v):
            return v.rearrange("p (k n) -> p k n", k=KT)

        def moba_out(pair):
            return (lambda x: x[:, 2 * pair:2 * pair + 2, :].rearrange("p a (t s) -> p t a s", t=TT)), \
                ps[:, 6:8, 0:2 * P].rearrange("p t (a s) -> p t a s", a=2)

        def nsa_out(pair):
            return (lambda x: x[:, pair, :].rearrange("p (t s) -> p t s", t=TT)), ps[:, 6:8, 0:P]

        def blocks(x, a):
            n = 16 * (NG * N_CMP + 2)
            return x[:].rearrange("p k s -> p (k s)")[:, a * n:(a + 1) * n].rearrange("p (j n) -> p j n", j=16)

        def windows(a, half):
            return pairs_t[:, a].rearrange("p g (m r) -> p r g m", r=16)[:, 0:16:2, :, half:half + N_CMP]

        block = ctx.enter_context(nc.Block())

        @block.sync
        def _(sp):
            at = Place()

            def load(src, i=0):
                c = at.chunk
                at.chunk += 1
                if c >= RING:
                    sp.wait_ge(split_hi, i * RING + (c - RING + 1))
                    sp.wait_ge(split_lo, i * RING + (c - RING + 1))
                dst = raw[c % RING][:, 0:src.shape[1] * src.shape[2]].rearrange("p (k n) -> p k n", k=src.shape[1])
                sp.dma_start(dst, src).then_inc(landed[c % RING], 16)

            def trios(matrix, starts, n=4):
                for r in range(3):
                    load(columns(matrix, starts[r]))
                with sp.Fori(0, n - 1) as i:
                    for r in range(3):
                        load(columns(matrix, i * CW + (starts[r] + CW)), i)
                at.chunk += 3 * (n - 2)

            def out_product(name):
                for q in range(4):
                    load(columns(out_w[name], q * CW))

            def ffn(n):
                up, down = ffn_up[n], ffn_down[n]
                load(columns(up, 0))
                load(columns(up, F_FF))
                with sp.Fori(0, PAIRS - 1) as i:
                    load(columns(up, i * CW + CW), i)
                    load(down_rows(down, i * CW), i)
                    load(columns(up, i * CW + (F_FF + CW)), i)
                at.chunk += 3 * (PAIRS - 2)
                load(down_rows(down, (PAIRS - 1) * CW))

            for name in phases:
                if name == "hgrn":
                    trios(w["hgrn_w_in"][0], (0, D, 3 * D))
                    for q in range(4):
                        load(columns(w["hgrn_w_in"][0], 2 * D + q * CW))
                    out_product(name)
                elif name.startswith("ffn"):
                    ffn(int(name[3:]))
                elif name == "moba":
                    trios(w["moba_w_in"][0], (0, D, 2 * D))
                    out_product(name)
                elif name == "conv":
                    trios(w["conv_w_in_2"][0], (D, 2 * D, 0))
                    out_product(name)
                elif name == "kv":
                    for slot in range(6):
                        load(columns(w["kv_w_2"], slot * CW))
                    for a in range(2):
                        for half in range(2):
                            load(w["cmp_w1_2"][a, half * D:(half + 1) * D, :].rearrange("(k p) n -> p k n", p=P))
                elif name == "nsa":
                    for q in range(4):
                        load(columns(w["nsa_w_qg_2"][0], q * CW))
                    load(w["nsa_w_qg_2"][0].rearrange("(k p) n -> p k n", p=P)[:, :, D:D + TAIL])
                    out_product(name)
            sp.wait_ge(h_ready, 2 * len([p for p in phases if p != "kv"]))
            sp.dma_start(out.rearrange("a (t p) d -> (a p) t d", p=P), h[:]).then_inc(out_landed, 16)
            sp.wait_ge(out_landed, 16)

        @block.scalar
        def _(act):
            at = Place()

            def split(i=0, ahead=False, width=2048):
                c = at.chunk
                at.chunk += 1
                if c < at.split:
                    return
                if ahead:
                    at.split = c + 1
                act.wait_ge(landed[c % RING], i * 16 + 16 * (c // RING + 1))
                if c >= RING:
                    act.wait_ge(chunk_used, i * RING + (c - RING + 1))
                act.activation(whi[c % RING][:, 0:width], raw[c % RING][:, 0:width], ACT.Copy).then_inc(split_hi, 1)

            def split_ahead(n=1):
                c = at.chunk
                for _ in range(n):
                    split(ahead=True)
                at.chunk = c

            def load_gain():
                g = at.gains
                at.gains += 1
                if g < len(gain_rows):
                    act.dma_start(gain[g % 2][:], gain_rows[g].partition_broadcast(P)).then_inc(gain_landed[g % 2], 16)

            def norm(turns=True, same=False):
                for t in range(TT):
                    if at.h == 0:
                        act.wait_ge(x_landed, 16)
                    else:
                        act.wait_ge(h_ready, 2 * at.h - 1 + t)
                    act.activation(xn[:, t, :], h[:, t, :], ACT.Square, accum_out=ss[:, t:t + 1]).then_inc(squares_summed, 1)
                load_gain()
                if not turns:
                    at.h += 1
                    return
                split_ahead()
                for g in range(4):
                    t, half = g // 2, g % 2
                    act.wait_ge(turned, at.turned + g + 1)
                    act.activation(xhi[:, 4 * half:4 * half + 4, t * P:(t + 1) * P],
                                   ps[:, 6 + g % 2, :].rearrange("p (k t) -> p k t", k=4), ACT.Copy).then_inc(xhi_ready, 1)
                at.turned += 4

            def out_product():
                for q in range(4):
                    split()
                at.h += 1

            def ffn():
                first = at.chunk

                def activate():
                    act.activation(silu[:], ps[:, 4, :].rearrange("p (a s) -> p a s", a=2), ACT.Silu).then_inc(silu_ready, 1)

                def high_part():
                    act.activation(hhi[:], hid[:], ACT.Copy).then_inc(hhi_ready, 1)

                split()
                split()
                with act.Fori(0, PAIRS - 1) as i:
                    split(i)
                    act.wait_ge(chunk_used, i * 3 + (first + 1))
                    act.wait_ge(hid_ready, i + at.hids)
                    activate()
                    split(i)
                    act.wait_ge(hid_ready, i + (at.hids + 1))
                    high_part()
                    split(i)
                at.chunk += 3 * (PAIRS - 2)
                at.hids += PAIRS - 1
                act.wait_ge(chunk_used, first + 3 * (PAIRS - 1))
                act.wait_ge(hid_ready, at.hids)
                activate()
                split()
                at.hids += 1
                act.wait_ge(hid_ready, at.hids)
                high_part()
                at.h += 1

            def pair_of(bank):
                return ps[:, bank, :].rearrange("p (a s) -> p a s", a=2)

            def rounds(evacuate, n=4):
                first = at.chunk
                for r in range(3):
                    split()
                with act.Fori(0, n - 1) as i:
                    for r in range(3):
                        split(i)
                        act.wait_ge(chunk_used, i * 3 + (first + r + 1))
                        evacuate(i, r)
                at.chunk += 3 * (n - 2)
                for r in range(3):
                    split()
                    act.wait_ge(chunk_used, first + 3 * (n - 1) + r + 1)
                    evacuate(n - 1, r)
                at.split = at.chunk
                at.chunk -= 3

            def hgrn():
                def evacuate(i, r):
                    if r == 0:
                        act.wait_ge(bank_free[0], i)
                        act.activation(junk[:, 0:2 * S].rearrange("p (a s) -> p a s", a=2), pair_of(0), ACT.Sigmoid).then_inc(q_sig, 1)
                    else:
                        dst = gf[0] if r == 1 else gsig
                        act.activation(dst[:, bass.ds(i * 2, 2), :], pair_of(r), ACT.Sigmoid).then_inc(bank_free[r], 1)

                act.wait_ge(lb_shift, 1)
                act.activation(lbw[:, 0:2, :], lbw[:, 2:4, :], ACT.Exp).then_inc(lb_exp, 1)
                rounds(evacuate)
                first = at.chunk
                at.chunk += 3
                act.wait_ge(bias_copied, 1)
                act.dma_start(bias_dram.rearrange("p h y -> h p y"), bias_row[:].unsqueeze(1).broadcast_to([HEADS, P, 2 * S]))\
                   .then_inc(bias_stored, 16)
                for n in range(4):
                    act.wait_ge(chunk_used, first + n + 1)
                    split()
                    act.activation(gin[:, :, n * CW:(n + 1) * CW], pair_of(4 + n % 2), ACT.Copy).then_inc(bank_free[4 + n % 2], 1)
                for p in range(4):
                    act.wait_ge(o_ready, p + 1)
                    act.activation(gq[:, 2 * p:2 * p + 2, :], pair_of(4 + p % 2), ACT.Square).then_inc(o_squared, 1)
                    act.wait_ge(y_ready, at.y + p + 1)
                    act.activation(xhi[:, 2 * p:2 * p + 2, :], gk[:, 2 * p:2 * p + 2, :], ACT.Copy).then_inc(yhi_ready, 1)
                at.y += 4
                split()
                at.h += 1

            def attention(pairs, branches, pair_out):
                units = pairs * branches
                for i in range(units + 2):
                    if i < units:
                        act.wait_ge(max_ready, at.att + i + 1)
                        for t in range(TT):
                            for a in range(2):
                                logits = att_l[:, i % 2, a, t * P:t * P + (t + 1) * P]
                                n = t * 2 + a
                                ins = act.activation(logits, logits, ACT.Exp, bias=nmax[:, i % 2, n:n + 1],
                                                     accum_out=sums[:, i % 2, n:n + 1])
                        ins.then_inc(exp_ready, 1)
                    if 0 <= i - 1 < units:
                        act.wait_ge(probs_turned, at.att + i)
                        if i - 1 >= 2:
                            act.wait_ge(pv_done, at.att + i - 2)
                        act.activation(att_pt[:, (i - 1) % 2, :, :], ps[:, 4:6, 0:3 * P], ACT.Copy).then_inc(pt_ready, 1)
                    if i >= 2 and (i - 1) % branches == 0:
                        pair = (i - 2) // branches
                        act.wait_ge(pv_done, at.att + i - 1)
                        dst, src = pair_out(pair)
                        act.activation(dst(xhi), src, ACT.Copy).then_inc(yhi_ready, 1)
                at.att += units
                at.y += pairs

            def moba():
                first = at.chunk

                def evacuate(i, r):
                    if r < 2:
                        dst = (mq, mk)[r]
                        act.activation(dst[:, bass.ds(i * 2, 2), :], pair_of(r), ACT.Copy).then_inc(bank_free[r], 1)

                act.wait_ge(bias_stored, 16)
                for t in range(TT):
                    cols_t = slice(t * P, t * P + (t + 1) * P)
                    src = bass.AP(bias_dram.tensor, S - 1 - t * P, [[HEADS * 2 * S - 1, P], [2 * S, HEADS], [1, (t + 1) * P]])
                    act.dma_start(mbias[:, :, cols_t], src).then_inc(bias_landed, 16)
                rounds(evacuate)
                attention(HEADS // 2, 1, moba_out)
                out_product()

            def conv():
                def evacuate(i, r):
                    if r == 0:
                        act.wait_ge(conv_done, i)
                        act.activation(cgate[:], pair_of(0), ACT.Copy).then_inc(gate_kept, 1)

                rounds(evacuate)
                act.wait_ge(conv_done, 4)
                act.wait_ge(dve_round, 4)
                for p in range(4):
                    sl = slice(2 * p, 2 * p + 2)
                    act.activation(xhi[:, sl, :], cy[:, sl, :], ACT.Copy).then_inc(yhi_ready, 1)
                at.y += 4
                out_product()

            def shared_kv():
                first = at.chunk
                dst = [raw_t[:, 0], raw_t[:, 1], kn[:, 0:8, :], vn[:, 0], kn[:, 8:16, :], vn[:, 1]]
                for slot in range(6):
                    split()
                    if slot >= 2:
                        keep(first, slot - 2, dst)
                split_ahead(1)
                keep(first, 4, dst)
                split_ahead(2)
                keep(first, 5, dst)
                act.wait_ge(raw_kept, 2)
                for a in range(2):
                    for side in range(2):
                        for gp in range(2):
                            act.dma_start(pairs_t[side * HD:(side + 1) * HD, a, gp::2, 0:S - side],
                                          raw_t[gp * HD:(gp + 1) * HD, a, :, side:S]).then_inc(pairs_landed, 16)
                act.wait_ge(pairs_landed, 16 * 8)
                for a in range(2):
                    for half in range(2):
                        act.activation(blocks(xhi, a)[:, 8 * half:8 * half + 8, 0:NG * N_CMP].rearrange("p j (g n) -> p j g n", g=NG),
                                       windows(a, half), ACT.Copy)
                    pos = cols[:, R_POS + 16 * a:R_POS + 16 * a + 16].unsqueeze(2).broadcast_to([P, 16, 2])
                    act.activation(blocks(xhi, a)[:, :, NG * N_CMP:], pos, ACT.Copy).then_inc(blocks_hi, 1)
                for n in range(4):
                    split()
                act.wait_ge(gelu_in, 1)
                act.activation(csig[:], cz2[:], ACT.Sigmoid, scale=2 * float(np.sqrt(2 / np.pi))).then_inc(gelu_sig, 1)
                for n in range(4):
                    act.wait_ge(kt_turned, n + 1)
                    act.activation(kt[:, n // 2, :, (n % 2) * P:(n % 2 + 1) * P], ps[:, n, :].rearrange("p (g s) -> p g s", g=NG),
                                   ACT.Copy).then_inc(kt_kept, 1)
                act.wait_ge(kt_turned, 5)
                act.activation(kct[:], ps[:, 4, 0:NG * N_CMP], ACT.Copy).then_inc(kt_kept, 1)

            def keep(first, slot, dst):
                act.wait_ge(chunk_used, first + slot + 1)
                src = ps[:, slot % 4, :]
                d = dst[slot]
                shape = {2: "p (a b) -> p a b", }[2]
                act.activation(d, src.rearrange(shape, a=d.shape[1]), ACT.Copy).then_inc(raw_kept if slot < 2 else kn_kept, 1)

            def nsa():
                first = at.chunk
                for q in range(4):
                    split()
                split(width=KT * TAIL)
                for q in range(4):
                    act.wait_ge(chunk_used, first + q + 1)
                    act.activation(xn[:, :, q * CW:(q + 1) * CW], pair_of(q), ACT.Copy).then_inc(q_kept, 1)
                act.wait_ge(chunk_used, first + 5)
                act.activation(gates[:], ps[:, 4, 0:TT * TAIL].rearrange("p (t n) -> p t n", t=TT), ACT.Sigmoid).then_inc(gates_ready, 1)
                split_ahead(3)
                for n in range(4):
                    act.wait_ge(q_turned, n + 1)
                    t, half = n // 2, n % 2
                    act.activation(nq[:, 4 * half:4 * half + 4, t * P:(t + 1) * P], ps[:, n, :].rearrange("p (k s) -> p k s", k=4),
                                   ACT.Copy).then_inc(nq_ready, 1)
                act.wait_ge(cmp_shifted, 1)
                act.activation(cl[:], cl[:], ACT.Exp).then_inc(cmp_exp, 1)
                for t in range(TT):
                    act.wait_ge(cmp_turned, t + 1)
                    act.activation(cpt[:, :, t * P:(t + 1) * P], ps[:, 4 + t, :].rearrange("p (g s) -> p g s", g=NG),
                                   ACT.Copy).then_inc(cpt_ready, 1)
                attention(NH // 2, 2, nsa_out)
                out_product()

            act.dma_start(h[:], w["x"].rearrange("a (t p) d -> (a p) t d", p=P)).then_inc(x_landed, 16)
            act.dma_start(const[:], w["masks"]).then_inc(const_landed, 16)
            load_gain()
            for r0, src in ((R_ONORM, w["hgrn_out_norm"]), (R_LB, w["hgrn_lb_logits"])):
                v = src.rearrange("a (k p) -> (a k) p", p=P)
                act.dma_start(rows[r0:r0 + v.shape[0], :], v).then_inc(const_landed, 16)
            v = w["conv_w_2"].rearrange("a c (k p) -> (a c k) p", p=P)
            act.dma_start(rows[R_CONV:R_CONV + 24, :], v).then_inc(const_landed, 16)
            act.dma_start(rows[R_B1:R_B1 + 4, :], w["cmp_b1_2"].rearrange("a (k p) -> (a k) p", p=P)).then_inc(const_landed, 16)
            act.dma_start(rows[R_POS:R_POS + 32, :], w["cmp_pos_2"].rearrange("a (j k) d -> (a j) (k d)", k=2)).then_inc(const_landed, 16)
            act.dma_start(table[0:BUCKETS, :], w["rel_bias_table"]).then_inc(small_landed, 16)
            act.dma_start(places[:], w["places"]).then_inc(small_landed, 16)
            act.dma_start(w2sb[:], w["cmp_w2_2"].rearrange("a (k p) d -> p (a k) d", p=P)).then_inc(small_landed, 16)
            for n in range(3):
                act.dma_start(kgain[:, n, :], w["k_norm_2"][n].partition_broadcast(P)).then_inc(small_landed, 16)
            act.dma_start(qgain[:], w["q_norm_2"][0].partition_broadcast(P)).then_inc(small_landed, 16)
            for name in phases:
                norm(turns=name != "final", same=name == "ffn4")
                if name.startswith("ffn"):
                    ffn()
                elif name != "final":
                    {"hgrn": hgrn, "moba": moba, "conv": conv, "kv": shared_kv, "nsa": nsa}[name]()

        @block.gpsimd
        def _(pool):
            done = 0
            norms = 0
            pool.wait_ge(const_landed, 16 * 6)
            for name in phases:
                for t in range(TT):
                    pool.wait_ge(squares_summed, 2 * norms + t + 1)
                    pool.tensor_scalar(ms[:, t:t + 1], ss[:, t:t + 1], 1.0 / D, EPS, ALU.mult, ALU.add).then_inc(ms_ready, 1)
                    pool.wait_ge(ms_ready, 2 * norms + t + 1)
                    pool.tensor_tensor(rstd[:, t:t + 1], ms[:, t:t + 1], const[:, C_HALF:C_HALF + 1], ALU.pow).then_inc(rstd_ready, 1)
                    pool.wait_ge(rstd_ready, 2 * norms + t + 1)
                norms += 1
                if name == "kv":
                    pool.wait_ge(kms_ready, 1)
                    pool.tensor_tensor(krs[:], kss[:, 1, :], const[:, C_HALF:C_HALF + 17], ALU.pow).then_inc(krs_ready, 1)
                    pool.wait_ge(krs_ready, 1)
                if name == "nsa":
                    for t in range(TT):
                        part = slice(t * NH, (t + 1) * NH)
                        pool.wait_ge(qms_ready, t + 1)
                        pool.tensor_tensor(qrs[:, part], qss[:, 1, part], const[:, C_HALF:C_HALF + NH], ALU.pow).then_inc(qrs_ready, 1)
                        pool.wait_ge(qrs_ready, t + 1)
                if name == "hgrn":
                    pool.wait_ge(o_summed, 2)
                    pool.tensor_tensor(orms[:, 1, :], orms[:, 0, :], const[:, C_HALF:C_HALF + TT], ALU.pow).then_inc(orms_ready, 1)
                    pool.wait_ge(orms_ready, 1)

        @block.vector
        def _(dve):
            at = Place()
            links = [0]

            def link(ins):
                links[0] += 1
                ins.then_inc(dve_wrote, 1)
                dve.wait_ge(dve_wrote, links[0])

            def split(i=0, ahead=False, width=2048):
                c = at.chunk
                at.chunk += 1
                if c < at.split:
                    return
                if ahead:
                    at.split = c + 1
                dve.wait_ge(split_hi, i * RING + (c + 1))
                dve.tensor_tensor(wlo[c % RING][:, 0:width], raw[c % RING][:, 0:width], whi[c % RING][:, 0:width].bitcast(F32),
                                  ALU.subtract).then_inc(split_lo, 1)

            def split_ahead(n=1):
                c = at.chunk
                for _ in range(n):
                    split(ahead=True)
                at.chunk = c

            def norm(turns=True):
                g = at.gains
                at.gains += 1
                dve.wait_ge(gain_landed[g % 2], 16 * (g // 2 + 1))
                for t in range(TT):
                    dve.wait_ge(rstd_ready, 2 * g + t + 1)
                    dst = xn if turns else h
                    dve.scalar_tensor_tensor(out=dst[:, t, :], in0=h[:, t, :], scalar=rstd[:, t:t + 1], in1=gain[g % 2][:],
                                             op0=ALU.mult, op1=ALU.mult).then_inc(xn_ready if turns else h_ready, 1)
                if not turns:
                    at.h += 1
                    return
                split_ahead()
                for g in range(4):
                    t, half = g // 2, g % 2
                    dve.wait_ge(xhi_ready, at.turned + g + 1)
                    dst = slice(4 * half, 4 * half + 4), slice(t * P, (t + 1) * P)
                    dve.tensor_tensor(xlo[:, dst[0], dst[1]], ps[:, 6 + g % 2, :].rearrange("p (k t) -> p k t", k=4),
                                      xhi[:, dst[0], dst[1]].bitcast(F32), ALU.subtract).then_inc(bank_free[6 + g % 2], 1)
                at.turned += 4

            def out_product(scale=None):
                first = at.chunk
                for q in range(4):
                    split()
                for q in range(4):
                    dve.wait_ge(chunk_used, first + q + 1)
                    for t in range(TT):
                        piece = h[:, t, q * CW:(q + 1) * CW]
                        prod = ps[:, q, t * CW:(t + 1) * CW]
                        if scale is None:
                            ins = dve.tensor_tensor(piece, prod, piece, ALU.add)
                        else:
                            ins = dve.scalar_tensor_tensor(out=piece, in0=prod, scalar=scale[:, t:t + 1], in1=piece,
                                                           op0=ALU.mult, op1=ALU.add)
                        if q == 3:
                            ins.then_inc(h_ready, 1)
                at.h += 1

            def ffn(alpha):
                first = at.chunk

                def multiply():
                    dve.tensor_tensor(hid[:], silu[:], ps[:, 5, :].rearrange("p (a s) -> p a s", a=2), ALU.mult).then_inc(hid_ready, 1)

                def low_part():
                    dve.tensor_tensor(hlo[:], hid[:], hhi[:].bitcast(F32), ALU.subtract).then_inc(hlo_ready, 1)

                split()
                split()
                with dve.Fori(0, PAIRS - 1) as i:
                    split(i)
                    split(i)
                    dve.wait_ge(silu_ready, i + (at.hids + 1))
                    dve.wait_ge(chunk_used, i * 3 + (first + 2))
                    multiply()
                    dve.wait_ge(hhi_ready, i + (at.hids + 1))
                    low_part()
                    split(i)
                at.chunk += 3 * (PAIRS - 2)
                at.hids += PAIRS
                split()
                dve.wait_ge(silu_ready, at.hids)
                dve.wait_ge(chunk_used, at.chunk - 1)
                multiply()
                dve.wait_ge(hhi_ready, at.hids)
                low_part()
                dve.wait_ge(chunk_used, at.chunk)
                for t in range(TT):
                    acc = ps[:, 2 * t:2 * t + 2, :].rearrange("p a b -> p (a b)")
                    dve.scalar_tensor_tensor(out=h[:, t, :], in0=acc, scalar=alpha, in1=h[:, t, :],
                                             op0=ALU.mult, op1=ALU.add).then_inc(h_ready, 1)
                at.h += 1

            def pair_of(bank):
                return ps[:, bank, :].rearrange("p (a s) -> p a s", a=2)

            def rounds(take, n=4):
                first = at.chunk
                for r in range(3):
                    split()
                with dve.Fori(0, n - 1) as i:
                    for r in range(3):
                        split(i)
                        take(i, r, i * 3 + (first + r + 1))
                at.chunk += 3 * (n - 2)
                for r in range(3):
                    split()
                    take(n - 1, r, first + 3 * (n - 1) + r + 1)
                at.split = at.chunk
                at.chunk -= 3

            def lower_bound():
                l0, l1 = cols[:, R_LB:R_LB + 8], cols[:, R_LB + 8:R_LB + 16]
                link(dve.tensor_tensor(lbw[:, 4, :], l0, l1, ALU.max))
                link(dve.tensor_tensor(lbw[:, 2, :], l0, lbw[:, 4, :], ALU.subtract))
                dve.tensor_tensor(lbw[:, 3, :], l1, lbw[:, 4, :], ALU.subtract).then_inc(lb_shift, 1)
                dve.wait_ge(lb_exp, 1)
                link(dve.tensor_tensor(lbw[:, 2, :], lbw[:, 0, :], lbw[:, 1, :], ALU.add))
                link(dve.reciprocal(lbw[:, 3, :], lbw[:, 2, :]))
                link(dve.tensor_tensor(lbw[:, 5, :], lbw[:, 0, :], lbw[:, 3, :], ALU.mult))
                link(dve.tensor_scalar(lbw[:, 4, :], lbw[:, 5, :], -1.0, 1.0, ALU.mult, ALU.add))

            def hgrn():
                lower_bound()

                def take(i, r, used):
                    if r == 0:
                        dve.wait_ge(q_sig, i + 1)
                        dve.tensor_tensor(gq[:, bass.ds(i * 2, 2), :], junk[:, 0:2 * S].rearrange("p (a s) -> p a s", a=2),
                                          pair_of(0), ALU.mult).then_inc(bank_free[0], 1)

                rounds(take)
                at.chunk += 3
                dve.wait_ge(bank_free[1], 4)
                for hg in range(2):
                    hs = slice(4 * hg, 4 * hg + 4)
                    f = gf[0][:, hs, :]
                    for row, op in ((4, ALU.mult), (5, ALU.add)):
                        link(dve.tensor_tensor(f, f, lbw[:, row, hs].unsqueeze(2).broadcast_to([P, 4, S]), op))
                    dve.tensor_scalar(gk[:, hs, :], f, -1.0, 1.0, ALU.mult, ALU.add).then_inc(qk_ready, 1)
                for s in range(LEVELS + 1):
                    for hg in range(2):
                        hs = slice(4 * hg, 4 * hg + 4)
                        dve.wait_ge(level_scored, 2 * s + hg + 1)
                        if s == 0:
                            dve.tensor_tensor(gq[:, hs, :], gq[:, hs, :], gf[0][:, hs, :], ALU.mult).then_inc(qk_ready, 1)
                        elif s < LEVELS:
                            m = 1 << (s - 1)
                            n = S // m
                            total = gf[(s - 1) % 2][:, hs, 0:n].rearrange("p h (b two) -> p h b two", two=2)
                            dve.tensor_tensor(gf[s % 2][:, hs, 0:n // 2], total[:, :, :, 0], total[:, :, :, 1], ALU.mult)
                            for x, side, other in ((gq, 1, 0), (gk, 0, 1)):
                                v = x[:, hs, :].rearrange("p h (b two m) -> p (h b) two m", two=2, m=m)[:, :, side, :]
                                f = gf[(s - 1) % 2][:, hs, 0:n]
                                if n == S:
                                    f = f.rearrange("p h (b two) -> p (h b) two", two=2)[:, :, other:other + 1]
                                else:
                                    v = x[:, hs, :].rearrange("p h (b two m) -> p h b two m", two=2, m=m)[:, :, :, side, :]
                                    f = f.rearrange("p h (b two) -> p h b two", two=2)[:, :, :, other:other + 1]
                                ins = dve.tensor_tensor(v, v, f.broadcast_to(v.shape), ALU.mult)
                            ins.then_inc(qk_ready, 1)
                        if s == LEVELS:
                            dve.tensor_copy(gsc[:, hs, 2, :], ps[:, 2 * hg, :].rearrange("p (h t) -> p h t", h=4)).then_inc(bank_free[2 * hg], 1)
                            continue
                        for t in range(TT):
                            src = ps[:, 2 * hg + t, :].rearrange("p (h t) -> p h t", h=4)
                            mask = const[:, C_MASK + s * P:C_MASK + (s + 1) * P].unsqueeze(1).broadcast_to([P, 4, P])
                            if s == 0:
                                ins = dve.tensor_tensor(gsc[:, hs, t, :], src, mask, ALU.mult)
                            else:
                                ins = dve.copy_predicated(gsc[:, hs, t, :], mask.bitcast(U32), src)
                            ins.then_inc(bank_free[2 * hg + t], 1)
                    if s >= 2 and s % 2 == 0:
                        split()
                for p in range(4):
                    dve.wait_ge(o_squared, p + 1)
                    for a in range(2):
                        hd = 2 * p + a
                        ins = dve.scalar_tensor_tensor(out=gk[:, hd, :], in0=ps[:, 4 + p % 2, a * S:(a + 1) * S],
                                                       scalar=cols[:, R_ONORM + hd:R_ONORM + hd + 1], in1=gsig[:, hd, :],
                                                       op0=ALU.mult, op1=ALU.mult)
                    ins.then_inc(y_ready, 1)
                    dve.wait_ge(yhi_ready, at.y + p + 1)
                    sl = slice(2 * p, 2 * p + 2)
                    dve.tensor_tensor(xlo[:, sl, :], gk[:, sl, :], xhi[:, sl, :].bitcast(F32), ALU.subtract).then_inc(ylo_ready, 1)
                at.y += 4
                for t in range(TT):
                    dve.wait_ge(o_summed, 1)
                dve.tensor_scalar(orms[:, 0, :], ps[:, 6, 0:TT], 1.0 / D, EPS, ALU.mult, ALU.add).then_inc(o_summed, 1)
                return orms[:, 1, :]

            def attention(pairs, branches, pair_out, bias, scale, gate=None):
                units = pairs * branches
                for i in range(units + 2):
                    if i < units:
                        dve.wait_ge(scored, at.att + i + 1)
                        if i >= 2:
                            dve.wait_ge(probs_turned, at.att + i - 1)
                        b = i % 2
                        link(dve.scalar_tensor_tensor(out=att_l[:, b], in0=ps[:, 2 * b:2 * b + 2, 0:3 * P], scalar=scale,
                                                      in1=bias(i), op0=ALU.mult, op1=ALU.add))
                        for t in range(TT):
                            ins = dve.tensor_reduce(nmax[:, b, 2 * t:2 * t + 2], att_l[:, b, :, t * P:t * P + (t + 1) * P],
                                                    AX.X, ALU.max, negate=True)
                        ins.then_inc(max_ready, 1)
                    if 0 <= i - 1 < units:
                        b = (i - 1) % 2
                        dve.wait_ge(exp_ready, at.att + i)
                        link(dve.reciprocal(coef[:, b, :], sums[:, b, :]))
                        if gate is not None:
                            link(dve.tensor_tensor(coef[:, b, :].rearrange("p (t a) -> p t a", t=TT),
                                                   coef[:, b, :].rearrange("p (t a) -> p t a", t=TT), gate(i - 1), ALU.mult))
                        for t in range(TT):
                            for a in range(2):
                                x = att_l[:, b, a, t * P:t * P + (t + 1) * P]
                                n = 2 * t + a
                                ins = dve.tensor_scalar(x, x, coef[:, b, n:n + 1], None, ALU.mult)
                        ins.then_inc(probs_ready, 1)
                    if i >= 2 and (i - 1) % branches == 0:
                        pair = (i - 2) // branches
                        dve.wait_ge(yhi_ready, at.y + pair + 1)
                        dst, src = pair_out(pair)
                        dve.tensor_tensor(dst(xlo), src, dst(xhi).bitcast(F32), ALU.subtract).then_inc(ylo_ready, 1)
                at.att += units
                at.y += pairs

            def moba():
                def take(i, r, used):
                    if r == 2:
                        dve.wait_ge(chunk_used, used)
                        dve.tensor_scalar(mv[:, :, bass.ds(i * CW, CW)], pair_of(2), 1.0, None, ALU.mult).then_inc(bank_free[2], 1)

                rounds(take)
                dve.wait_ge(bias_landed, 32)
                attention(HEADS // 2, 1, moba_out, lambda u: mbias[:, 2 * u:2 * u + 2, :], P ** -0.5)
                out_product()

            def conv():
                per_round = 4
                base = links[0] + 1
                link(dve.memset(cpad[:, :, 0:2], 0.0))

                def tap_link(ins, i, n):
                    ins.then_inc(dve_wrote, 1)
                    dve.wait_ge(dve_wrote, i * per_round + (base + n))

                def take(i, r, used):
                    if r == 1:
                        dve.wait_ge(gate_kept, i + 1)
                        dve.wait_ge(chunk_used, used)
                        tap_link(dve.tensor_tensor(cpad[:, :, 2:S + 2], cgate[:], pair_of(1), ALU.mult), i, 1)
                        for tap in range(3):
                            for n in range(2):
                                scalar = cols[:, bass.ds(i * 2 + (R_CONV + 8 * tap + n), 1)]
                                src = cpad[:, n, tap:tap + S]
                                if tap == 0:
                                    ins = dve.tensor_scalar(cacc[:, n, :], src, scalar, None, ALU.mult)
                                else:
                                    ins = dve.scalar_tensor_tensor(out=cacc[:, n, :], in0=src, scalar=scalar, in1=cacc[:, n, :],
                                                                   op0=ALU.mult, op1=ALU.add)
                                if n == 0 and tap == 0:
                                    ins.then_inc(conv_done, 1)
                            tap_link(ins, i, 2 + tap)
                    if r == 2:
                        dve.wait_ge(chunk_used, used)
                        dve.tensor_tensor(cy[:, bass.ds(i * 2, 2), :], cacc[:], pair_of(2), ALU.mult).then_inc(dve_round, 1)

                rounds(take)
                links[0] += 4 * per_round
                for p in range(4):
                    sl = slice(2 * p, 2 * p + 2)
                    dve.wait_ge(yhi_ready, at.y + p + 1)
                    dve.tensor_tensor(xlo[:, sl, :], cy[:, sl, :], xhi[:, sl, :].bitcast(F32), ALU.subtract).then_inc(ylo_ready, 1)
                at.y += 4
                out_product()

            def inverse_rms(x, square, ssum, n, ready):
                link(dve.tensor_tensor(square, x, x, ALU.mult))
                link(dve.tensor_reduce(ssum[:, 0, n], square, AX.X, ALU.add))
                dve.tensor_scalar(ssum[:, 1, n], ssum[:, 0, n], 1.0 / HD, EPS, ALU.mult, ALU.add).then_inc(ready, 1)

            def shared_kv():
                for slot in range(6):
                    split()
                split_ahead(3)
                dve.wait_ge(small_landed, 16 * 7)
                link(dve.tensor_tensor(kgain[:], kgain[:], qgain[:].unsqueeze(1).broadcast_to([P, 3, HD]), ALU.mult))
                for a in range(2):
                    dve.wait_ge(blocks_hi, a + 1)
                    for half in range(2):
                        dst = [blocks(x, a)[:, 8 * half:8 * half + 8, 0:NG * N_CMP].rearrange("p j (g n) -> p j g n", g=NG) for x in (xhi, xlo)]
                        dve.tensor_tensor(dst[1], windows(a, half), dst[0].bitcast(F32), ALU.subtract)
                    pos = cols[:, R_POS + 16 * a:R_POS + 16 * a + 16].unsqueeze(2).broadcast_to([P, 16, 2])
                    dst = [blocks(x, a)[:, :, NG * N_CMP:] for x in (xhi, xlo)]
                    dve.tensor_tensor(dst[1], pos, dst[0].bitcast(F32), ALU.subtract).then_inc(blocks_lo, 1)
                for n in range(4):
                    split()
                for n in range(4):
                    dve.wait_ge(chunk_used, at.chunk - 2 + 2 * (n // 2))
                    src = ps[:, 4 + n, :]
                    link(dve.tensor_tensor(b1col[:, n:n + 1], src[:, NG * N_CMP:NG * N_CMP + 1], cols[:, R_B1 + n:R_B1 + n + 1], ALU.add))
                    link(dve.tensor_scalar(cz[:, n, :], src[:, 0:NG * N_CMP], b1col[:, n:n + 1], None, ALU.add))
                link(dve.tensor_tensor(cz2[:], cz[:], cz[:], ALU.mult))
                link(dve.tensor_scalar(cz2[:], cz2[:], 0.044715, 1.0, ALU.mult, ALU.add))
                dve.tensor_tensor(cz2[:], cz2[:], cz[:], ALU.mult).then_inc(gelu_in, 1)
                dve.wait_ge(gelu_sig, 1)
                dve.tensor_tensor(cz[:], cz[:], csig[:], ALU.mult).then_inc(gelu_ready, 1)
                link(dve.memset(kn[:, 16, :], 1.0))
                dve.wait_ge(cmp_done, 2)
                for hh in range(4):
                    at_hh = slice(32 * hh, 32 * hh + N_CMP)
                    ins = dve.tensor_copy(vc[at_hh], ps[at_hh, 5, 0:NG * HD].rearrange("p (g d) -> p g d", g=NG))
                ins.then_inc(vc_kept, 1)
                link(dve.tensor_copy(kn[0:NG * N_CMP, 16, :], ps[0:NG * N_CMP, 4, 0:HD]))
                dve.wait_ge(kn_kept, 4)
                inverse_rms(kn[:], kd[:, :, 0, :], kss, slice(0, 17), kms_ready)
                dve.wait_ge(krs_ready, 1)
                link(dve.tensor_tensor(kn[:], kn[:], krs[:].unsqueeze(2).broadcast_to([P, 17, HD]), ALU.mult))
                for n, (lo, hi) in enumerate(((16, 17), (0, 8), (8, 16))):
                    shape = [P, hi - lo, 2, HD]
                    g = kgain[:, n, :].unsqueeze(1).unsqueeze(1).broadcast_to(shape)
                    dve.tensor_tensor(kd[:, lo:hi], kn[:, lo:hi, :].unsqueeze(2).broadcast_to(shape), g, ALU.mult).then_inc(kd_ready, 1)

            def nsa():
                for q in range(4):
                    split()
                split(width=KT * TAIL)
                split_ahead(3)
                link(dve.memset(cp[:], 0.0))
                dve.wait_ge(q_kept, 4)
                for t in range(TT):
                    part = slice(t * NH, (t + 1) * NH)
                    q = xn[:, t, :].rearrange("p (h d) -> p h d", h=NH)
                    inverse_rms(q, qsq[:], qss, part, qms_ready)
                    dve.wait_ge(qrs_ready, t + 1)
                    dve.tensor_tensor(q, q, qrs[:, part].unsqueeze(2).broadcast_to([P, NH, HD]), ALU.mult).then_inc(qn_ready, 1)
                dve.wait_ge(cmp_scored, 1)
                for t in range(TT):
                    c = slice(C_CMP + t * N_CMP, C_CMP + (t + 1) * N_CMP)
                    for side in range(2):
                        dst = cl[:, t, :].rearrange("p (h two n) -> p h two n", two=2, n=N_CMP)[:, :, side, :]
                        src = ps[:, 2 * t + side, 0:NH // 2 * N_CMP].rearrange("p (h n) -> p h n", n=N_CMP)
                        ins = dve.scalar_tensor_tensor(out=dst, in0=src, scalar=HD ** -0.5, op0=ALU.mult, op1=ALU.add,
                                                       in1=const[:, c].unsqueeze(1).broadcast_to([P, NH // 2, N_CMP]))
                link(ins)
                every = cl[:].rearrange("p t (h n) -> p (t h) n", h=NH)
                wide = [P, TT * NH, N_CMP]
                link(dve.tensor_reduce(cmx[:], every, AX.X, ALU.max))
                dve.tensor_tensor(every, every, cmx[:].unsqueeze(2).broadcast_to(wide), ALU.subtract).then_inc(cmp_shifted, 1)
                dve.wait_ge(cmp_exp, 1)
                link(dve.tensor_reduce(csum[:, 0, :], every, AX.X, ALU.add))
                link(dve.reciprocal(csum[:, 1, :], csum[:, 0, :]))
                dve.wait_ge(gates_ready, 1)
                gate = gates[:].rearrange("p t (h b) -> p (t h) b", b=3)
                link(dve.tensor_tensor(csum[:, 0, :], csum[:, 1, :], gate[:, :, 0], ALU.mult))
                link(dve.tensor_tensor(every, every, csum[:, 0, :].unsqueeze(2).broadcast_to(wide), ALU.mult))
                for t in range(TT):
                    c = slice(C_VALID + t * N_CMP, C_VALID + (t + 1) * N_CMP)
                    dve.tensor_tensor(cp[:, t, :, 0:N_CMP], cl[:, t, :].rearrange("p (h n) -> p h n", h=NH),
                                      const[:, c].unsqueeze(1).broadcast_to([P, NH, N_CMP]), ALU.mult).then_inc(cmp_probs, 1)
                attention(NH // 2, 2, nsa_out, lambda u: causal.unsqueeze(1).broadcast_to([P, 2, 3 * P]), HD ** -0.5,
                          lambda u: gates[:].rearrange("p t (h b) -> p t h b", b=3)[:, :, 2 * (u // 2):2 * (u // 2) + 2, 1 + u % 2])
                out_product()

            dve.memset(zero[:], 0.0).then_inc(zero_ready, 1)
            dve.memset(table[BUCKETS:BUCKETS + 1, :], NEG).then_inc(zero_ready, 1)
            dve.wait_ge(cols_turned, 1)
            link(dve.tensor_copy(cols[:], ps[:, 7, 0:ROWS]))
            dve.wait_ge(bias_rowed, 1)
            dve.tensor_copy(bias_row[:], ps[0:HEADS, 5, :]).then_inc(bias_copied, 1)
            for name in phases:
                norm(turns=name != "final")
                if name == "hgrn":
                    scale = hgrn()
                    dve.wait_ge(orms_ready, 1)
                    at.chunk -= 3
                    at.split = at.chunk + 3
                    out_product(scale)
                elif name.startswith("ffn"):
                    ffn(1.0 if name in ("ffn0", "ffn1") else 0.5)
                elif name != "final":
                    {"moba": moba, "conv": conv, "kv": shared_kv, "nsa": nsa}[name]()

        @block.tensor
        def _(pe):
            at = Place()

            def free(bank, i=0):
                n = at.fills[bank]
                at.fills[bank] += 1
                if not isinstance(i, int) or n + i > 0:
                    pe.wait_ge(bank_free[bank], i + n)

            def passes(out, part, m, k, cols, start, stop):
                pass

            def across(bank, i=0):
                c = at.chunk
                at.chunk += 1
                pe.wait_ge(split_lo, i * RING + (c + 1))
                hi, lo = thirds(whi[c % RING][:]), thirds(wlo[c % RING][:])
                for n in range(2):
                    out = ps[:, bank, n * S:(n + 1) * S]
                    tile = slice(n * P, (n + 1) * P)
                    for k in range(KT):
                        pe.matmul(out, hi[:, k, tile], xhi[:, k, :], start=k == 0, stop=False)
                        pe.matmul(out, hi[:, k, tile], xlo[:, k, :], start=False, stop=False)
                        mm = pe.matmul(out, lo[:, k, tile], xhi[:, k, :], start=False, stop=k == KT - 1)
                mm.then_inc(chunk_used, 1)

            def along(bank, i=0, width=CW):
                c = at.chunk
                at.chunk += 1
                pe.wait_ge(split_lo, i * RING + (c + 1))
                hi, lo = thirds(whi[c % RING][:, 0:KT * width]), thirds(wlo[c % RING][:, 0:KT * width])
                for t in range(TT):
                    out = ps[:, bank, t * width:(t + 1) * width]
                    tile = slice(t * P, (t + 1) * P)
                    for k in range(KT):
                        pe.matmul(out, xhi[:, k, tile], hi[:, k, :], start=k == 0, stop=False)
                        pe.matmul(out, xhi[:, k, tile], lo[:, k, :], start=False, stop=False)
                        mm = pe.matmul(out, xlo[:, k, tile], hi[:, k, :], start=False, stop=k == KT - 1)
                mm.then_inc(chunk_used, 1)

            def norm():
                for g in range(4):
                    t, half = g // 2, g % 2
                    pe.wait_ge(xn_ready, at.xn + t + 1)
                    free(6 + g % 2)
                    for k in range(4):
                        kk = 4 * half + k
                        mm = pe.transpose(ps[:, 6 + g % 2, k * P:(k + 1) * P], xn[:, t, kk * P:(kk + 1) * P], ident)
                    mm.then_inc(turned, 1)
                at.xn += 2
                pe.wait_ge(bank_free[6], at.fills[6])
                pe.wait_ge(bank_free[7], at.fills[7])

            def out_product(skip_wait=False):
                for q in range(4):
                    if q == 0:
                        pe.wait_ge(ylo_ready, at.y)
                    if at.fills[q]:
                        pe.wait_ge(bank_free[q], at.fills[q])
                    along(q)

            def ffn():
                pe.wait_ge(zero_ready, 1)

                def down(i=0, last=False):
                    c = at.chunk
                    at.chunk += 1
                    pe.wait_ge(split_lo, i * RING + (c + 1))
                    hi = whi[c % RING][:].rearrange("p (k n) -> p k n", k=2)
                    lo = wlo[c % RING][:].rearrange("p (k n) -> p k n", k=2)
                    for k in range(2):
                        for t in range(TT):
                            tile = slice(t * P, (t + 1) * P)
                            for a, b in ((hhi, hi), (hhi, lo), (hlo, hi)):
                                for n in range(2):
                                    mm = pe.matmul(ps[:, 2 * t + n, :], a[:, k, tile], b[:, k, n * 512:(n + 1) * 512],
                                                   start=False, stop=last and k == 1 and b is hi and a is hlo,
                                                   skip_group_check=True)
                    mm.then_inc(chunk_used, 1)

                for b in range(4):
                    if at.fills[b]:
                        pe.wait_ge(bank_free[b], at.fills[b])
                    pe.matmul(ps[:, b, :], zero[:, 0:P], zero[:], start=True, stop=False, skip_group_check=True)
                if at.fills[4]:
                    pe.wait_ge(bank_free[4], at.fills[4])
                    pe.wait_ge(bank_free[5], at.fills[5])
                across(4)
                across(5)
                with pe.Fori(0, PAIRS - 1) as i:
                    pe.wait_ge(silu_ready, i + (at.hids + 1))
                    across(4, i)
                    pe.wait_ge(hlo_ready, i + (at.hids + 1))
                    down(i)
                    across(5, i)
                at.chunk += 3 * (PAIRS - 2)
                at.hids += PAIRS
                pe.wait_ge(hlo_ready, at.hids)
                down(last=True)

            def rounds(kinds, n=4):
                for r in range(3):
                    free(r)
                    kinds[r](r)
                with pe.Fori(0, n - 1) as i:
                    for r in range(3):
                        free(r, i)
                        kinds[r](r, i)
                at.chunk += 3 * (n - 2)
                for r in range(3):
                    at.fills[r] += n - 2

            def hgrn():
                rounds((across, across, across))
                steps = 0
                for s in range(LEVELS + 1):
                    for hg in range(2):
                        if s == 0:
                            pe.wait_ge(bank_free[0], 4)
                        pe.wait_ge(qk_ready, 2 * s + hg + 1)
                        if s == LEVELS:
                            free(2 * hg)
                            for a in range(4):
                                hd = 4 * hg + a
                                mm = pe.matmul(ps[:, 2 * hg, a * P:(a + 1) * P], gk[:, hd, 0:P], gq[:, hd, P:2 * P], start=True, stop=True)
                            mm.then_inc(level_scored, 1)
                            continue
                        for t in range(TT):
                            tile = slice(t * P, (t + 1) * P)
                            free(2 * hg + t)
                            for a in range(4):
                                hd = 4 * hg + a
                                mm = pe.matmul(ps[:, 2 * hg + t, a * P:(a + 1) * P], gk[:, hd, tile], gq[:, hd, tile], start=True, stop=True)
                        mm.then_inc(level_scored, 1)
                    if s % 2 == 1:
                        free(4 + s // 2 % 2)
                        along(4 + s // 2 % 2)
                for p in range(4):
                    bank = 4 + p % 2
                    hg = p // 2
                    pe.wait_ge(bank_free[2 * hg], at.fills[2 * hg])
                    if p < 2:
                        pe.wait_ge(bank_free[bank], at.fills[bank])
                    else:
                        pe.wait_ge(ylo_ready, at.y + p - 1)
                    for a in range(2):
                        hd = 2 * p + a
                        wide = slice(hd * P, (hd + 1) * P)
                        o = ps[:, bank, a * S:(a + 1) * S]
                        pe.matmul(o[:, 0:P], gin[:, 0, wide], gsc[:, hd, 0, :], start=True, stop=True)
                        pe.matmul(o[:, P:S], gin[:, 0, wide], gsc[:, hd, 2, :], start=True, stop=False)
                        mm = pe.matmul(o[:, P:S], gin[:, 1, wide], gsc[:, hd, 1, :], start=False, stop=True)
                    mm.then_inc(o_ready, 1)
                pe.wait_ge(o_squared, 4)
                for t in range(TT):
                    for hd in range(HEADS):
                        mm = pe.matmul(ps[:, 6, t:t + 1], gq[:, hd, t * P:(t + 1) * P], one, start=hd == 0, stop=hd == HEADS - 1)
                mm.then_inc(o_summed, 1)
                at.y += 4

            def attention(pairs, branches, q_of, k_of, pv):
                units = pairs * branches
                for b in range(8):
                    if at.fills[b]:
                        pe.wait_ge(bank_free[b], at.fills[b])
                for i in range(units + 2):
                    if i < units:
                        b = i % 2
                        if i >= 2:
                            pe.wait_ge(max_ready, at.att + i - 1)
                        for a in range(2):
                            q, k = q_of(i, a), k_of(i, a)
                            pe.matmul(ps[:, 2 * b + a, 0:P], q[:, 0:P], k[:, 0:P], start=True, stop=True)
                            mm = pe.matmul(ps[:, 2 * b + a, P:3 * P], q[:, P:S], k, start=True, stop=True)
                        mm.then_inc(scored, 1)
                    if 0 <= i - 1 < units:
                        pe.wait_ge(probs_ready, at.att + i)
                        if i >= 2:
                            pe.wait_ge(pt_ready, at.att + i - 1)
                        for a in range(2):
                            for n in range(3):
                                mm = pe.transpose(ps[:, 4 + a, n * P:(n + 1) * P], att_l[:, (i - 1) % 2, a, n * P:(n + 1) * P], ident)
                        mm.then_inc(probs_turned, 1)
                    if i >= 2:
                        pair = (i - 2) // branches
                        pe.wait_ge(pt_ready, at.att + i - 1)
                        if pair and (i - 2) % branches == 0:
                            pe.wait_ge(ylo_ready, at.y + pair)
                        pv(i - 2, att_pt[:, i % 2]).then_inc(pv_done, 1)
                at.att += units
                at.y += pairs

            def moba():
                rounds((across, across, along))

                def pv(u, pt):
                    for a in range(2):
                        v = mv[:, :, (2 * u + a) * P:(2 * u + a + 1) * P]
                        part = slice(a * P, (a + 1) * P)
                        pe.matmul(ps[:, 6, part], v[:, 0, :], pt[:, a, 0:P], start=True, stop=True)
                        pe.matmul(ps[:, 7, part], v[:, 0, :], pt[:, a, P:2 * P], start=True, stop=False)
                        mm = pe.matmul(ps[:, 7, part], v[:, 1, :], pt[:, a, 2 * P:3 * P], start=False, stop=True)
                    return mm

                attention(HEADS // 2, 1, lambda u, a: mq[:, 2 * u + a, :], lambda u, a: mk[:, 2 * u + a, :], pv)
                out_product()

            def conv():
                for r in range(3):
                    if at.fills[r]:
                        pe.wait_ge(bank_free[r], at.fills[r])
                for r, kind in enumerate((across, across, across)):
                    kind(r)
                with pe.Fori(0, 3) as i:
                    for r in range(3):
                        pe.wait_ge((conv_done, conv_done, dve_round)[r], i + 1)
                        across(r, i)
                at.chunk += 6
                pe.wait_ge(dve_round, 4)
                at.y += 4
                out_product()

            def shared_kv():
                for slot in range(6):
                    bank = slot % 4
                    if slot < 4:
                        if at.fills[bank]:
                            pe.wait_ge(bank_free[bank], at.fills[bank])
                    else:
                        pe.wait_ge(raw_kept, slot - 3)
                    (across if slot < 2 else along)(bank)
                width = NG * N_CMP + 2
                for a in range(2):
                    pe.wait_ge(blocks_lo, a + 1)
                    for n in range(2):
                        if at.fills[4 + 2 * a + n]:
                            pe.wait_ge(bank_free[4 + 2 * a + n], at.fills[4 + 2 * a + n])
                    for half in range(2):
                        c = at.chunk
                        at.chunk += 1
                        pe.wait_ge(split_lo, c + 1)
                        hi, lo = thirds(whi[c % RING][:]), thirds(wlo[c % RING][:])
                        for n in range(2):
                            out = ps[:, 4 + 2 * a + n, 0:width]
                            tile = slice(n * P, (n + 1) * P)
                            for k in range(KT):
                                j = 8 * half + k
                                pe.matmul(out, hi[:, k, tile], blocks(xhi, a)[:, j, :], start=j == 0, stop=False)
                                pe.matmul(out, hi[:, k, tile], blocks(xlo, a)[:, j, :], start=False, stop=False)
                                mm = pe.matmul(out, lo[:, k, tile], blocks(xhi, a)[:, j, :], start=False, stop=j == 15)
                        mm.then_inc(chunk_used, 1)
                pe.wait_ge(gelu_ready, 1)
                for k in range(2):
                    mm = pe.matmul(ps[0:NG * N_CMP, 4, 0:HD], cz[:, k, :], w2sb[:, k, :], start=k == 0, stop=k == 1)
                mm.then_inc(cmp_done, 1)
                for hh in range(4):
                    for g in range(NG):
                        for k in range(2):
                            mm = pe.matmul(ps[32 * hh:32 * hh + N_CMP, 5, g * HD:(g + 1) * HD],
                                           cz[:, 2 + k, g * N_CMP:(g + 1) * N_CMP], w2sb[:, 2 + k, :], start=k == 0, stop=k == 1)
                mm.then_inc(cmp_done, 1)
                pe.wait_ge(kd_ready, 3)
                for n in range(4):
                    for g in range(NG):
                        mm = pe.transpose(ps[:, n, g * P:(g + 1) * P], kd[:, 4 * n + g].rearrange("p a d -> p (a d)"), ident)
                    mm.then_inc(kt_turned, 1)
                c = NG * N_CMP
                pe.transpose(ps[:, 4, 0:c], kd[0:c, 16].rearrange("p a d -> p (a d)"), ident[0:c, 0:c]).then_inc(kt_turned, 1)
                pe.wait_ge(kt_kept, 5)

            def nsa():
                for q in range(4):
                    along(q)
                along(4, width=TAIL)
                for n in range(4):
                    t, half = n // 2, n % 2
                    pe.wait_ge(qn_ready, t + 1)
                    for k in range(4):
                        kk = 4 * half + k
                        mm = pe.transpose(ps[:, n, k * P:(k + 1) * P], xn[:, t, kk * P:(kk + 1) * P], ident)
                    mm.then_inc(q_turned, 1)
                pe.wait_ge(nq_ready, 4)
                pe.wait_ge(gates_ready, 1)
                for t in range(TT):
                    for hd in range(NH):
                        side = slice(hd % 2 * HD, hd % 2 * HD + HD)
                        g = hd // 4
                        mm = pe.matmul(ps[:, 2 * t + hd % 2, hd // 2 * N_CMP:(hd // 2 + 1) * N_CMP], nq[side, hd // 2, t * P:(t + 1) * P],
                                       kct[side, g * N_CMP:(g + 1) * N_CMP], start=True, stop=True)
                mm.then_inc(cmp_scored, 1)
                for t in range(TT):
                    pe.wait_ge(cmp_probs, t + 1)
                    for g in range(NG):
                        mm = pe.transpose(ps[:, 4 + t, g * P:(g + 1) * P], cp[:, t, 4 * g:4 * g + 4, :].rearrange("p h n -> p (h n)"), ident)
                    mm.then_inc(cmp_turned, 1)
                pe.wait_ge(cpt_ready, 2)

                def q_of(u, a):
                    return nq[a * HD:(a + 1) * HD, u // 2, :]

                def k_of(u, a):
                    return kt[a * HD:(a + 1) * HD, u % 2, u // 4, :]

                def pv(u, pt):
                    pair, branch = u // 2, u % 2
                    g = pair // 2
                    for a in range(2):
                        hd = 2 * pair + a
                        out = [ps[a * HD:(a + 1) * HD, 6 + t, 0:P] for t in range(TT)]
                        if branch == 0:
                            rows_c = slice(32 * (hd % 4), 32 * (hd % 4) + N_CMP)
                            for t in range(TT):
                                pe.matmul(out[t], vc[rows_c, g, :], cpt[rows_c, g, t * P:(t + 1) * P], start=True, stop=False)
                        v = vn[:, branch, :, g * HD:(g + 1) * HD]
                        last = branch == 1
                        pe.matmul(out[0], v[:, 0, :], pt[:, a, 0:P], start=False, stop=last)
                        pe.matmul(out[1], v[:, 0, :], pt[:, a, P:2 * P], start=False, stop=False)
                        mm = pe.matmul(out[1], v[:, 1, :], pt[:, a, 2 * P:3 * P], start=False, stop=last)
                    return mm

                attention(NH // 2, 2, q_of, k_of, pv)
                out_product()

            pe.wait_ge(const_landed, 16 * 6)
            pe.transpose(ps[:, 7, 0:ROWS], rows[:], ident[0:ROWS, 0:ROWS]).then_inc(cols_turned, 1)
            pe.wait_ge(small_landed, 16 * 7)
            pe.wait_ge(zero_ready, 2)
            pe.matmul(ps[0:HEADS, 5, :], table[:], places[:], start=True, stop=True).then_inc(bias_rowed, 1)
            for name in phases:
                if name == "final":
                    continue
                if name == "hgrn":
                    pe.wait_ge(dve_wrote, 1)
                norm()
                if name == "hgrn":
                    hgrn()
                    out_product()
                elif name.startswith("ffn"):
                    ffn()
                else:
                    {"moba": moba, "conv": conv, "kv": shared_kv, "nsa": nsa}[name]()


_INS = ['x', 'norm_mix', 'norm_ffn', 'hgrn_w_in', 'hgrn_lb_logits', 'hgrn_out_norm', 'hgrn_w_out', 'moba_w_in', 'moba_w_out', 'rel_bias_table', 'ffn_w13', 'ffn_w2', 'final_norm', 'ffn_norm_2', 'ffn_w_gate_up_2', 'ffn_w_down_2', 'mix_norm_2', 'conv_w_in_2', 'conv_w_2', 'conv_w_out_2', 'kv_norm_2', 'kv_w_2', 'cmp_pos_2', 'cmp_w1_2', 'cmp_b1_2', 'cmp_w2_2', 'k_norm_2', 'nsa_w_qg_2', 'q_norm_2', 'nsa_w_o_2']


def kernel(**inputs):
    import concourse.bacc as bacc
    from concourse.bass_utils import run_bass_kernel_spmd

    nc = bacc.Bacc("TRN2", target_bir_lowering=False, num_devices=1)
    masks, places = constants()
    arrays = {name: np.ascontiguousarray(inputs[name]) for name in _INS}
    arrays["masks"], arrays["places"] = masks, places
    w = {name: nc.dram_tensor(f"in_{name}", a.shape, mybir.dt.from_np(a.dtype), kind="ExternalInput").ap() for name, a in arrays.items()}
    out = nc.dram_tensor("out_0", (1, S, D), F32, kind="ExternalOutput").ap()
    build(nc, w, out)
    r = run_bass_kernel_spmd(nc, [{f"in_{name}": a for name, a in arrays.items()}], core_ids=[0])
    return r.results[0]["out_0"]
```

```python
from contextlib import ExitStack

import numpy as np

import concourse.bass as bass
from concourse import mybir

F32 = mybir.dt.float32
F32R = mybir.dt.float32r
BF16 = mybir.dt.bfloat16
U32 = mybir.dt.uint32
ALU = mybir.AluOpType
ACT = mybir.ActivationFunctionType
AX = mybir.AxisListType

P = 128
S = 256
TT = S // P
D = 1024
KT = D // P
CW = 256
RING = 3
HEADS = 8
F_FF = 2816
PAIRS = F_FF // CW
EPS = 1e-6
NEG = -1e30
LEVELS = 8
NH = 16
HD = 64
NG = 4
CMP_STRIDE, CMP_BLOCK = 16, 32
N_CMP = (S - CMP_BLOCK) // CMP_STRIDE + 1
TAIL = 48
BUCKETS, MAX_DISTANCE = 32, 1024

C_MASK = 0
C_CAUSAL = C_MASK + LEVELS * P
C_CMP = C_CAUSAL + 3 * P
C_VALID = C_CMP + TT * N_CMP
C_ONE = C_VALID + TT * N_CMP
C_HALF = C_ONE + 2
C_COLS = C_HALF + NH * TT

C_BANKS = (5, 6, 7, 0)
KT_BANKS = (5, 6, 7, 0)

R_ONORM, R_LB, R_CONV, R_B1, R_POS = 0, 8, 24, 48, 52
ROWS = R_POS + 32

PHASES = ["hgrn", "ffn0", "moba", "ffn1", "final", "ffn2", "conv", "ffn3", "kv", "ffn4", "nsa", "ffn5"]


def constants():
    c = np.zeros((P, C_COLS), np.float32)
    s, t = np.arange(P)[:, None], np.arange(P)[None, :]
    c[:, :P] = s == t
    for level in range(LEVELS - 1):
        m = 1 << level
        keep = (s // (2 * m) == t // (2 * m)) & (s // m % 2 == 0) & (t // m % 2 == 1)
        c[:, C_MASK + (level + 1) * P:C_MASK + (level + 2) * P] = keep
    diagonal = np.where(np.arange(P)[None, :] <= np.arange(P)[:, None], 0, NEG)
    c[:, C_CAUSAL:C_CAUSAL + P] = diagonal
    c[:, C_CAUSAL + 2 * P:C_CAUSAL + 3 * P] = diagonal
    end = np.arange(N_CMP) * CMP_STRIDE + CMP_BLOCK - 1
    for tt in range(TT):
        valid = end[None, :] <= (tt * P + np.arange(P))[:, None]
        c[:, C_CMP + tt * N_CMP:C_CMP + (tt + 1) * N_CMP] = np.where(valid, 0, NEG)
        c[:, C_VALID + tt * N_CMP:C_VALID + (tt + 1) * N_CMP] = valid
    c[:, C_ONE:C_ONE + 2] = 1
    c[:, C_HALF:C_HALF + NH * TT] = -0.5
    dist = S - 1 - np.arange(2 * S)
    n = np.maximum(dist, 0)
    exact = BUCKETS // 2
    far = np.log(np.maximum(n, exact).astype(np.float32) / np.float32(exact)) / np.float32(np.log(MAX_DISTANCE / exact))
    far = exact + (far * np.float32(BUCKETS - exact)).astype(np.int32)
    bucket = np.where(n < exact, n, np.minimum(far, BUCKETS - 1))
    places = np.zeros((BUCKETS + 1, 2 * S), np.float32)
    places[bucket, np.arange(2 * S)] = dist >= 0
    places[BUCKETS] = dist < 0
    return c, places


class Place:

    def __init__(self):
        self.chunk = 0
        self.split = 0
        self.h = 0
        self.sums = 0
        self.turned = 0
        self.xn = 0
        self.gains = 0
        self.hids = 0
        self.y = 0
        self.fills = [1] + [0] * 7
        self.att = 0
        self.h_ffn = 0
        self.fresh = False
        self.by_tile = True
        self.direct = []
        self.last = False


    def take_direct(self):
        self.direct.append(self.chunk)
        self.chunk += 1

    def splits(self, c):
        return c - sum(d < c for d in self.direct)


def build(nc, w, out, phases=PHASES):
    with ExitStack() as ctx:
        def sb(name, shape, dt=F32):
            return ctx.enter_context(nc.sbuf_tensor(name, shape, dt))

        def sem(name):
            return ctx.enter_context(nc.semaphore(name))

        ps = ctx.enter_context(nc.psum_tensor("ps", [P, 8, 512], F32))

        raw = [sb(f"raw{n}", [P, 2048]) for n in range(RING)]
        whi = [sb(f"whi{n}", [P, 2048], F32R) for n in range(RING)]
        wlo = [sb(f"wlo{n}", [P, 2048], F32R) for n in range(RING)]
        h = sb("h", [P, TT, D])
        xn = sb("xn", [P, TT, D])
        xhi = sb("xhi", [P, KT, S], F32R)
        xlo = sb("xlo", [P, KT, S], F32R)
        gain = [sb(f"gain{n}", [P, D]) for n in range(2)]
        junk = sb("junk", [P, D])
        silu = sb("silu", [P, 2, S])
        hid = sb("hid", [P, 2, S])
        hhi = sb("hhi", [P, 2, S], F32R)
        hlo = sb("hlo", [P, 2, S], F32R)
        ss = sb("ss", [P, TT, 2])
        ms = sb("ms", [P, TT])
        rstd = sb("rstd", [P, TT])
        const = sb("const", [P, C_COLS])
        token = sb("token", [P, 3])
        zero = sb("zero", [P, 512], BF16)
        rows = sb("rows", [ROWS, P])
        cols = sb("cols", [P, ROWS])
        arena = sb("arena", [P, 13312])

        def area(start, *dims):
            n = int(np.prod(dims))
            assert start + n <= 13312
            v = arena[:, start:start + n]
            if len(dims) == 2:
                v = v.rearrange("p (a b) -> p a b", b=dims[1])
            if len(dims) == 3:
                v = v.rearrange("p (a b c) -> p a b c", b=dims[1], c=dims[2])
            return v

        ident = const[:, 0:P]
        one = const[:, C_ONE:C_ONE + 1]
        causal = const[:, C_CAUSAL:C_CAUSAL + 3 * P]

        gq = area(0, HEADS, S)
        gk = area(2048, HEADS, S)
        gf = [area(4096, HEADS, S), area(6144, HEADS, P)]
        gsig = area(7168, HEADS, S)
        gsc = area(9216, HEADS, 3, P)
        gin = xn
        lbw = sb("lbw", [P, 6, HEADS])
        orms = sb("orms", [P, 2, TT])

        att_l = area(9216, 2, 2, 3 * P)
        att_pt = area(10752, 2, 2, 3 * P)
        nmax = sb("nmax", [P, 2, 4])
        sums = sb("sums", [P, 2, 4])
        coef = sb("coef", [P, 2, 4])

        mq = area(0, HEADS, S)
        mk = area(2048, HEADS, S)
        mv = area(4096, TT, D)
        mbias = area(6144, HEADS, 3 * P)
        table = sb("table_sb", [BUCKETS + 1, HEADS])
        places = sb("places_sb", [BUCKETS + 1, 2 * S])
        bias_row = sb("bias_row", [HEADS, 2 * S])
        bias_dram = nc.dram_tensor("bias_rows", [P, HEADS, 2 * S], F32, kind="Internal").ap()

        cpad = area(0, 2, S + 2)
        cgate = area(516, 2, S)
        cacc = area(1028, 2, S)
        cy = area(2048, KT, S)

        raw_t = area(0, 2, 2, S)
        pairs_t = area(1024, 2, NG, S)
        kn = area(4096, 17, HD)
        kd = area(9216, 17, 2, HD)
        kt = area(6144, 2, NG, S)
        vn = area(8192, 2, TT, NG * HD)
        blk = [area(11392 + 960 * a, 16, NG * N_CMP) for a in range(2)]
        cz, cz2, csig = silu[:].rearrange("p a s -> p (a s)"), hid[:].rearrange("p a s -> p (a s)"), area(3584, 240)
        czv = junk[:].rearrange("p (k g h n) -> p k g h n", k=2, g=NG, h=4)
        kct = area(5696, NG, 2, N_CMP)
        vc = area(5816, NG, HD)
        kss = sb("kss", [P, 2, 17])
        krs = sb("krs", [P, 17])
        kgain = sb("kgain", [P, 3, HD])
        qgain = sb("qgain", [P, HD])
        w2sb = sb("w2sb", [P, 4, HD])

        nq = area(0, NH // 2, S)
        cl = area(2048, TT, NH * N_CMP)
        cp = area(2560, TT, NH, 32)
        cpt = area(3584, NG, S)
        qsq = area(5184, TT, 4, HD)
        gates_t = sb("gates_t", [TAIL, S])
        gates = sb("gates", [P, TT, TAIL])
        qss = sb("qss", [P, 2, 4, TT * 4])
        qrs = sb("qrs", [P, 4, TT * 4])
        cmx = sb("cmx", [P, TT * NH])
        csum = sb("csum", [P, 2, TT * NH])

        landed = [sem(f"chunk_landed{n}") for n in range(RING)]
        split_hi = sem("split_hi")
        split_lo = sem("split_lo")
        chunk_used = sem("chunk_used")
        bank_free = [sem(f"bank_free{n}") for n in range(8)]
        x_landed = sem("x_landed")
        const_landed = sem("const_landed")
        gain_landed = [sem(f"gain_landed{n}") for n in range(2)]
        h_ready = sem("h_ready")
        squares_summed = sem("squares_summed")
        ms_ready = sem("ms_ready")
        rstd_ready = sem("rstd_ready")
        xn_ready = sem("xn_ready")
        turned = sem("turned")
        xhi_ready = sem("xhi_ready")
        silu_ready = sem("silu_ready")
        half_summed = sem("half_summed")
        hid_ready = sem("hid_ready")
        hhi_ready = sem("hhi_ready")
        hlo_ready = sem("hlo_ready")
        zero_ready = sem("zero_ready")
        cols_turned = sem("cols_turned")
        cols_ready = sem("cols_ready")
        dve_wrote = sem("dve_wrote")
        lb_exp = sem("lb_exp")
        lb_shift = sem("lb_shift")
        q_sig = sem("q_sig")
        qk_ready = sem("qk_ready")
        level_scored = sem("level_scored")
        o_ready = sem("o_ready")
        o_squared = sem("o_squared")
        y_ready = sem("y_ready")
        yhi_ready = sem("yhi_ready")
        ylo_ready = sem("ylo_ready")
        dve_round = sem("conv_rounds_done")
        o_summed = sem("o_summed")
        orms_ready = sem("orms_ready")
        out_landed = sem("out_landed")
        bias_rowed = sem("bias_rowed")
        bias_copied = sem("bias_copied")
        bias_stored = sem("bias_stored")
        bias_landed = sem("bias_landed")
        scored = sem("scored")
        max_ready = sem("max_ready")
        exp_ready = sem("exp_ready")
        probs_ready = sem("probs_ready")
        probs_turned = sem("probs_turned")
        pt_ready = sem("pt_ready")
        pv_done = sem("pv_done")
        conv_done = sem("conv_done")
        gate_kept = sem("gate_kept")
        raw_kept = sem("raw_kept")
        pairs_landed = sem("pairs_landed")
        gelu_in = sem("gelu_in")
        gelu_sig = sem("gelu_sig")
        gelu_ready = sem("gelu_ready")
        cmp_done = sem("cmp_done")
        kn_kept = sem("kn_kept")
        kms_ready = sem("kms_ready")
        krs_ready = sem("krs_ready")
        kd_ready = sem("kd_ready")
        kt_turned = sem("kt_turned")
        kt_kept = sem("kt_kept")
        vc_kept = sem("vc_kept")
        q_kept = sem("q_kept")
        qms_ready = sem("qms_ready")
        qrs_ready = sem("qrs_ready")
        qn_ready = sem("qn_ready")
        q_turned = sem("q_turned")
        nq_ready = sem("nq_ready")
        gates_ready = sem("gates_ready")
        gates_t_ready = sem("gates_t_ready")
        gates_turned = sem("gates_turned")
        blocks_ready = sem("blocks_ready")
        kc_kept = sem("kc_kept")
        kct_ready = sem("kct_ready")
        kct_zeroed = sem("kct_zeroed")
        cmp_scored = sem("cmp_scored")
        cmp_shifted = sem("cmp_shifted")
        cmp_exp = sem("cmp_exp")
        cmp_probs = sem("cmp_probs")
        cmp_turned = sem("cmp_turned")
        cpt_ready = sem("cpt_ready")
        zeroed = sem("zeroed")
        small_landed = sem("small_landed")

        def columns(matrix, at):
            return matrix.rearrange("(k p) n -> p k n", p=P)[:, :, bass.ds(at, CW)]

        def down_rows(matrix, at):
            return matrix[bass.ds(at, CW), :].rearrange("(k p) n -> p k n", p=P)

        ffn_up = [w["ffn_w13"][0], w["ffn_w13"][1]] + [w["ffn_w_gate_up_2"][a, b] for a in range(2) for b in range(2)]
        ffn_down = [w["ffn_w2"][0], w["ffn_w2"][1]] + [w["ffn_w_down_2"][a, b] for a in range(2) for b in range(2)]
        gains = {
            "hgrn": w["norm_mix"][0], "ffn0": w["norm_ffn"][0], "moba": w["norm_mix"][1], "ffn1": w["norm_ffn"][1],
            "final": w["final_norm"], "ffn2": w["ffn_norm_2"][0, 0], "conv": w["mix_norm_2"][0],
            "ffn3": w["ffn_norm_2"][0, 1], "kv": w["kv_norm_2"], "ffn4": w["ffn_norm_2"][1, 0],
            "nsa": w["mix_norm_2"][1], "ffn5": w["ffn_norm_2"][1, 1],
        }
        weighty = [name for name in phases if name != "final"]
        gain_rows = [gains[name] for name in phases]
        out_w = {"hgrn": w["hgrn_w_out"][0], "moba": w["moba_w_out"][0], "conv": w["conv_w_out_2"][0], "nsa": w["nsa_w_o_2"][0]}

        def thirds(v):
            return v.rearrange("p (k n) -> p k n", k=KT)

        def moba_out(pair):
            return (lambda x: x[:, 2 * pair:2 * pair + 2, :].rearrange("p a (t s) -> p t a s", t=TT)), \
                ps[:, 6:8, 0:2 * P].rearrange("p t (a s) -> p t a s", a=2)

        def nsa_out(pair):
            return (lambda x: x[:, pair, :].rearrange("p (t s) -> p t s", t=TT)), ps[:, 6:8, 0:P]

        def windows(a, half):
            return pairs_t[:, a].rearrange("p g (m r) -> p r g m", r=16)[:, 0:16:2, :, half:half + N_CMP]

        def halves(by_tile):
            return [(n // 2, n % 2) if by_tile else (n % 2, n // 2) for n in range(4)]

        block = ctx.enter_context(nc.Block())

        @block.sync
        def _(sp):
            at = Place()

            def load(src, i=0):
                c = at.chunk
                at.chunk += 1
                if c - RING in at.direct:
                    sp.wait_ge(chunk_used, c - RING + 1)
                elif c >= RING:
                    sp.wait_ge(split_hi, i * RING + (at.splits(c - RING) + 1))
                    sp.wait_ge(split_lo, i * RING + (at.splits(c - RING) + 1))
                dst = raw[c % RING][:, 0:src.shape[1] * src.shape[2]].rearrange("p (k n) -> p k n", k=src.shape[1])
                sp.dma_start(dst, src).then_inc(landed[c % RING], 16)

            def trios(matrix, starts, n=4):
                for r in range(3):
                    load(columns(matrix, starts[r]))
                with sp.Fori(0, n - 1) as i:
                    for r in range(3):
                        load(columns(matrix, i * CW + (starts[r] + CW)), i)
                at.chunk += 3 * (n - 2)

            def out_product(name):
                for q in range(4):
                    load(columns(out_w[name], q * CW))

            def ffn(n):
                up, down = ffn_up[n], ffn_down[n]
                load(columns(up, 0))
                load(columns(up, F_FF))
                with sp.Fori(0, PAIRS - 2) as i:
                    load(columns(up, i * CW + CW), i)
                    load(down_rows(down, i * CW), i)
                    load(columns(up, i * CW + (F_FF + CW)), i)
                at.chunk += 3 * (PAIRS - 3)
                load(columns(up, (PAIRS - 1) * CW))
                load(columns(up, (2 * PAIRS - 1) * CW))
                load(down_rows(down, (PAIRS - 2) * CW))
                load(down_rows(down, (PAIRS - 1) * CW))

            for name in phases:
                if name == "hgrn":
                    trios(w["hgrn_w_in"][0], (0, D, 3 * D))
                    for q in range(4):
                        load(columns(w["hgrn_w_in"][0], 2 * D + q * CW))
                    out_product(name)
                elif name.startswith("ffn"):
                    ffn(int(name[3:]))
                elif name == "moba":
                    trios(w["moba_w_in"][0], (0, D, 2 * D))
                    out_product(name)
                elif name == "conv":
                    trios(w["conv_w_in_2"][0], (D, 2 * D, 0))
                    out_product(name)
                elif name == "kv":
                    for slot in range(6):
                        load(columns(w["kv_w_2"], slot * CW))
                elif name == "nsa":
                    load(w["nsa_w_qg_2"][0].rearrange("(k p) n -> p k n", p=P)[:, :, D:D + TAIL])
                    for q in range(4):
                        load(columns(w["nsa_w_qg_2"][0], q * CW))
                    for a in range(2):
                        for half in range(2):
                            c = at.chunk
                            load(w["cmp_w1_2"][a, half * D:(half + 1) * D, :].rearrange("(k p) n -> p k n", p=P))
                            at.direct.append(c)
                    out_product(name)
            sp.wait_ge(h_ready, 4 * len([p for p in phases if p != "kv"]))
            sp.dma_start(out.rearrange("a (t p) d -> (a p) t d", p=P), h[:]).then_inc(out_landed, 16)
            sp.wait_ge(out_landed, 16)

        @block.scalar
        def _(act):
            at = Place()

            def split(i=0, ahead=False, width=2048):
                c = at.chunk
                at.chunk += 1
                if c < at.split:
                    return
                if ahead:
                    at.split = c + 1
                act.wait_ge(landed[c % RING], i * 16 + 16 * (c // RING + 1))
                if c >= RING:
                    act.wait_ge(chunk_used, i * RING + (c - RING + 1))
                act.activation(whi[c % RING][:, 0:width], raw[c % RING][:, 0:width], ACT.Copy).then_inc(split_hi, 1)

            def split_ahead(n=1):
                c = at.chunk
                for _ in range(0 if at.last else n):
                    split(ahead=True)
                at.chunk = c

            def load_gain():
                g = at.gains
                at.gains += 1
                if g < len(gain_rows):
                    act.dma_start(gain[g % 2][:], gain_rows[g].partition_broadcast(P)).then_inc(gain_landed[g % 2], 16)

            def squares():
                for n, (t, half) in enumerate(halves(at.by_tile)):
                    if at.h == 0:
                        act.wait_ge(x_landed, 16)
                    else:
                        act.wait_ge(h_ready, 4 * (at.h - 1) + n + 1)
                    cols_h = slice(half * 512, half * 512 + 512)
                    act.activation(xn[:, t, cols_h], h[:, t, cols_h], ACT.Square, accum_out=ss[:, t, half:half + 1])\
                       .then_inc(squares_summed, 1)
                load_gain()

            def x_high():
                for g in range(4):
                    t, half = g // 2, g % 2
                    act.wait_ge(turned, at.turned + g + 1)
                    act.activation(xhi[:, 4 * half:4 * half + 4, t * P:(t + 1) * P],
                                   ps[:, 4 + g, :].rearrange("p (k t) -> p k t", k=4), ACT.Copy).then_inc(xhi_ready, 1)
                at.turned += 4

            def out_product():
                for q in range(4):
                    split()
                split_ahead(2)
                at.h += 1

            def ffn():
                first = at.chunk

                def activate():
                    act.activation(silu[:], ps[:, 4, :].rearrange("p (a s) -> p a s", a=2), ACT.Silu).then_inc(silu_ready, 1)

                def high_part(dst=hhi[:]):
                    act.activation(dst, hid[:], ACT.Copy).then_inc(hhi_ready, 1)

                split()
                split()
                with act.Fori(0, PAIRS - 2) as i:
                    split(i)
                    act.wait_ge(chunk_used, i * 3 + (first + 1))
                    act.wait_ge(hid_ready, i + (at.hids + 1))
                    activate()
                    split(i)
                    act.wait_ge(hid_ready, i + (at.hids + 2))
                    high_part()
                    split(i)
                at.chunk += 3 * (PAIRS - 3)
                at.hids += PAIRS - 2
                split()
                act.wait_ge(chunk_used, first + 3 * (PAIRS - 2))
                act.wait_ge(hid_ready, at.hids + 1)
                activate()
                split()
                act.wait_ge(hid_ready, at.hids + 2)
                high_part()
                split()
                act.wait_ge(chunk_used, at.chunk - 2)
                activate()
                split()
                act.wait_ge(hid_ready, at.hids + 3)
                high_part(xhi[:, 0:2, :])
                at.hids += 2
                split_ahead(2)
                at.h += 1

            def pair_of(bank):
                return ps[:, bank, :].rearrange("p (a s) -> p a s", a=2)

            def rounds(evacuate, n=4):
                first = at.chunk
                for r in range(3):
                    split()
                with act.Fori(0, n - 1) as i:
                    for r in range(3):
                        split(i)
                        act.wait_ge(chunk_used, i * 3 + (first + r + 1))
                        evacuate(i, r)
                at.chunk += 3 * (n - 2)
                for r in range(3):
                    split()
                    act.wait_ge(chunk_used, first + 3 * (n - 1) + r + 1)
                    evacuate(n - 1, r)
                at.split = at.chunk
                at.chunk -= 3

            def hgrn():
                def evacuate(i, r):
                    if r == 0:
                        act.wait_ge(bank_free[0], i + 1)
                        act.activation(junk[:, 0:2 * S].rearrange("p (a s) -> p a s", a=2), pair_of(0), ACT.Sigmoid).then_inc(q_sig, 1)
                    else:
                        dst = gf[0] if r == 1 else gsig
                        act.activation(dst[:, bass.ds(i * 2, 2), :], pair_of(r), ACT.Sigmoid).then_inc(bank_free[r], 1)

                act.wait_ge(lb_shift, 1)
                act.activation(lbw[:, 0:2, :], lbw[:, 2:4, :], ACT.Exp).then_inc(lb_exp, 1)
                rounds(evacuate)
                first = at.chunk
                at.chunk += 3
                act.wait_ge(bias_copied, 1)
                act.dma_start(bias_dram.rearrange("p h y -> h p y"), bias_row[:].unsqueeze(1).broadcast_to([HEADS, P, 2 * S]))\
                   .then_inc(bias_stored, 16)
                for n in range(4):
                    act.wait_ge(chunk_used, first + n + 1)
                    split()
                    act.activation(gin[:, :, n * CW:(n + 1) * CW], pair_of(4 + n % 2), ACT.Copy).then_inc(bank_free[4 + n % 2], 1)
                for p in range(4):
                    act.wait_ge(o_ready, p + 1)
                    act.activation(gq[:, 2 * p:2 * p + 2, :], pair_of(4 + p % 2), ACT.Square).then_inc(o_squared, 1)
                    act.wait_ge(y_ready, at.y + p + 1)
                    act.activation(xhi[:, 2 * p:2 * p + 2, :], gk[:, 2 * p:2 * p + 2, :], ACT.Copy).then_inc(yhi_ready, 1)
                at.y += 4
                split()
                split_ahead(2)
                at.h += 1

            def attention(pairs, branches, pair_out):
                units = pairs * branches
                for i in range(units + 2):
                    if i < units:
                        act.wait_ge(max_ready, at.att + i + 1)
                        for t in range(TT):
                            for a in range(2):
                                logits = att_l[:, i % 2, a, t * P:t * P + (t + 1) * P]
                                n = t * 2 + a
                                ins = act.activation(logits, logits, ACT.Exp, bias=nmax[:, i % 2, n:n + 1],
                                                     accum_out=sums[:, i % 2, n:n + 1])
                        ins.then_inc(exp_ready, 1)
                    if 0 <= i - 1 < units:
                        act.wait_ge(probs_turned, at.att + i)
                        if i - 1 >= 2:
                            act.wait_ge(pv_done, at.att + i - 2)
                        act.activation(att_pt[:, (i - 1) % 2, :, :], ps[:, 4:6, 0:3 * P], ACT.Copy).then_inc(pt_ready, 1)
                    if i >= 2 and (i - 1) % branches == 0:
                        pair = (i - 2) // branches
                        act.wait_ge(pv_done, at.att + i - 1)
                        dst, src = pair_out(pair)
                        act.activation(dst(xhi), src, ACT.Copy).then_inc(yhi_ready, 1)
                at.att += units
                at.y += pairs

            def moba():
                first = at.chunk

                def evacuate(i, r):
                    if r < 2:
                        dst = (mq, mk)[r]
                        act.activation(dst[:, bass.ds(i * 2, 2), :], pair_of(r), ACT.Copy).then_inc(bank_free[r], 1)

                act.wait_ge(bias_stored, 16)
                for t in range(TT):
                    cols_t = slice(t * P, t * P + (t + 1) * P)
                    src = bass.AP(bias_dram.tensor, S - 1 - t * P, [[HEADS * 2 * S - 1, P], [2 * S, HEADS], [1, (t + 1) * P]])
                    act.dma_start(mbias[:, :, cols_t], src).then_inc(bias_landed, 16)
                rounds(evacuate)
                attention(HEADS // 2, 1, moba_out)
                out_product()

            def conv():
                def evacuate(i, r):
                    if r == 0:
                        act.wait_ge(conv_done, i + 1)
                        act.activation(cgate[:], pair_of(0), ACT.Copy).then_inc(gate_kept, 1)

                rounds(evacuate)
                act.wait_ge(conv_done, 5)
                act.wait_ge(dve_round, 4)
                for p in range(4):
                    sl = slice(2 * p, 2 * p + 2)
                    act.activation(xhi[:, sl, :], cy[:, sl, :], ACT.Copy).then_inc(yhi_ready, 1)
                at.y += 4
                out_product()

            def shared_kv():
                first = at.chunk
                dst = [raw_t[:, 0], raw_t[:, 1], kn[:, 0:8, :], vn[:, 0], kn[:, 8:16, :], vn[:, 1]]

                def keep(slot):
                    act.wait_ge(chunk_used, first + slot + 1)
                    d = dst[slot]
                    act.activation(d, ps[:, slot % 4, :].rearrange("p (a b) -> p a b", a=d.shape[1]), ACT.Copy)\
                       .then_inc(raw_kept if slot < 2 else kn_kept, 1)

                for slot in range(6):
                    split()
                    if slot >= 2:
                        keep(slot - 2)
                    if slot == 3:
                        act.wait_ge(raw_kept, 2)
                        for a in range(2):
                            for side in range(2):
                                for gp in range(2):
                                    act.dma_start(pairs_t[side * HD:(side + 1) * HD, a, gp::2, 0:S - side],
                                                  raw_t[gp * HD:(gp + 1) * HD, a, :, side:S]).then_inc(pairs_landed, 16)
                squares()
                keep(4)
                split_ahead(2)
                act.wait_ge(chunk_used, first + 6)
                x_high()
                keep(5)

            def nsa():
                first = at.chunk
                split(width=KT * TAIL)
                split()
                split()
                act.wait_ge(chunk_used, first + 1)
                act.activation(gates_t[:], ps[0:TAIL, 0, 0:S], ACT.Sigmoid).then_inc(gates_t_ready, 1)
                split()

                def keep(q):
                    act.wait_ge(chunk_used, first + q + 2)
                    act.activation(xn[:, :, q * CW:(q + 1) * CW], pair_of(1 + q), ACT.Copy).then_inc(q_kept, 1)

                keep(0)
                split()
                keep(1)
                act.wait_ge(gates_turned, 1)
                act.activation(gates[:], ps[:, 0, 0:TT * TAIL].rearrange("p (t n) -> p t n", t=TT), ACT.Copy).then_inc(gates_ready, 1)
                keep(2)
                for n in range(4):
                    act.wait_ge(kt_turned, n + 1)
                    act.activation(kt[:, n // 2, :, (n % 2) * P:(n % 2 + 1) * P], ps[:, KT_BANKS[n], :].rearrange("p (g s) -> p g s", g=NG),
                                   ACT.Copy).then_inc(kt_kept, 1)
                keep(3)
                for _ in range(4):
                    at.take_direct()
                for a in range(2):
                    part = slice(a * 2 * NG * N_CMP, (a + 1) * 2 * NG * N_CMP)
                    act.wait_ge(gelu_in, a + 1)
                    act.activation(csig[:, part], cz2[:, part], ACT.Sigmoid, scale=2 * float(np.sqrt(2 / np.pi))).then_inc(gelu_sig, 1)
                for n in range(4):
                    act.wait_ge(q_turned, n + 1)
                    t, half = n // 2, n % 2
                    act.activation(nq[:, 4 * half:4 * half + 4, t * P:(t + 1) * P], ps[:, 3 + n, :].rearrange("p (k s) -> p k s", k=4),
                                   ACT.Copy).then_inc(nq_ready, 1)
                act.wait_ge(kt_turned, 5)
                act.wait_ge(kct_zeroed, 1)
                for side in range(2):
                    half = slice(side * HD, (side + 1) * HD)
                    act.activation(kct[half, :, side, :], ps[half, 2, 0:NG * N_CMP].rearrange("p (g n) -> p g n", g=NG),
                                   ACT.Copy).then_inc(kct_ready, 1)
                split_ahead(3)
                act.wait_ge(cmp_shifted, 1)
                act.activation(cl[:], cl[:], ACT.Exp).then_inc(cmp_exp, 1)
                for t in range(TT):
                    act.wait_ge(cmp_turned, t + 1)
                    act.activation(cpt[:, :, t * P:(t + 1) * P], ps[:, 5 + t, :].rearrange("p (g s) -> p g s", g=NG),
                                   ACT.Copy).then_inc(cpt_ready, 1)
                attention(NH // 2, 2, nsa_out)
                out_product()

            act.dma_start(h[:], w["x"].rearrange("a (t p) d -> (a p) t d", p=P)).then_inc(x_landed, 16)
            act.dma_start(const[:], w["masks"]).then_inc(const_landed, 16)
            load_gain()
            for r0, src in ((R_ONORM, w["hgrn_out_norm"]), (R_LB, w["hgrn_lb_logits"])):
                v = src.rearrange("a (k p) -> (a k) p", p=P)
                act.dma_start(rows[r0:r0 + v.shape[0], :], v).then_inc(const_landed, 16)
            v = w["conv_w_2"].rearrange("a c (k p) -> (a c k) p", p=P)
            act.dma_start(rows[R_CONV:R_CONV + 24, :], v).then_inc(const_landed, 16)
            act.dma_start(rows[R_B1:R_B1 + 4, :], w["cmp_b1_2"].rearrange("a (k p) -> (a k) p", p=P)).then_inc(const_landed, 16)
            act.dma_start(rows[R_POS:R_POS + 32, :], w["cmp_pos_2"].rearrange("a (j k) d -> (a j) (k d)", k=2)).then_inc(const_landed, 16)
            act.dma_start(table[0:BUCKETS, :], w["rel_bias_table"]).then_inc(small_landed, 16)
            act.dma_start(places[:], w["places"]).then_inc(small_landed, 16)
            act.dma_start(w2sb[:], w["cmp_w2_2"].rearrange("a (k p) d -> p (a k) d", p=P)).then_inc(small_landed, 16)
            for n in range(3):
                act.dma_start(kgain[:, n, :], w["k_norm_2"][n].partition_broadcast(P)).then_inc(small_landed, 16)
            act.dma_start(qgain[:], w["q_norm_2"][0].partition_broadcast(P)).then_inc(small_landed, 16)
            split_ahead(2)
            for name in phases:
                at.last = name == weighty[-1]
                if name == "final":
                    squares()
                    at.h += 1
                elif name != "ffn4" or "kv" not in phases:
                    squares()
                    x_high()
                at.by_tile = name not in ("hgrn", "moba", "conv", "nsa")
                if name.startswith("ffn"):
                    ffn()
                elif name != "final":
                    {"hgrn": hgrn, "moba": moba, "conv": conv, "kv": shared_kv, "nsa": nsa}[name]()

        @block.gpsimd
        def _(pool):
            done = 0
            norms = 0
            by_tile = True
            pool.wait_ge(const_landed, 16 * 6)
            for name in phases:
                for t in range(TT):
                    pool.wait_ge(squares_summed, 4 * norms + [n + 1 for n, (tt, half) in enumerate(halves(by_tile)) if tt == t][1])
                    pool.tensor_tensor(ms[:, t:t + 1], ss[:, t, 0:1], ss[:, t, 1:2], ALU.add).then_inc(ms_ready, 1)
                    pool.wait_ge(ms_ready, 4 * norms + 2 * t + 1)
                    pool.tensor_scalar(ms[:, t:t + 1], ms[:, t:t + 1], 1.0 / D, EPS, ALU.mult, ALU.add).then_inc(ms_ready, 1)
                    pool.wait_ge(ms_ready, 4 * norms + 2 * t + 2)
                    pool.tensor_tensor(rstd[:, t:t + 1], ms[:, t:t + 1], const[:, C_HALF:C_HALF + 1], ALU.pow).then_inc(rstd_ready, 1)
                    pool.wait_ge(rstd_ready, 2 * norms + t + 1)
                norms += 1
                by_tile = name not in ("hgrn", "moba", "conv", "nsa")
                if name == "nsa":
                    pool.wait_ge(kms_ready, 1)
                    pool.tensor_tensor(krs[:, 0:16], kss[:, 1, 0:16], const[:, C_HALF:C_HALF + 16], ALU.pow).then_inc(krs_ready, 1)
                    pool.wait_ge(krs_ready, 1)
                    for q in range(4):
                        pool.wait_ge(qms_ready, q + 1)
                        pool.tensor_tensor(qrs[:, q, :], qss[:, 1, q, :], const[:, C_HALF:C_HALF + TT * 4], ALU.pow).then_inc(qrs_ready, 1)
                        pool.wait_ge(qrs_ready, q + 1)
                    pool.wait_ge(kms_ready, 2)
                    pool.tensor_tensor(krs[:, 16:17], kss[:, 1, 16:17], const[:, C_HALF:C_HALF + 1], ALU.pow).then_inc(krs_ready, 1)
                    pool.wait_ge(krs_ready, 2)
                if name == "hgrn":
                    pool.wait_ge(o_summed, 2)
                    pool.tensor_tensor(orms[:, 1, :], orms[:, 0, :], const[:, C_HALF:C_HALF + TT], ALU.pow).then_inc(orms_ready, 1)
                    pool.wait_ge(orms_ready, 1)

        @block.vector
        def _(dve):
            at = Place()
            links = [0]

            def link(ins):
                links[0] += 1
                ins.then_inc(dve_wrote, 1)
                dve.wait_ge(dve_wrote, links[0])

            def split(i=0, ahead=False, width=2048):
                c = at.chunk
                at.chunk += 1
                if c < at.split:
                    return
                if ahead:
                    at.split = c + 1
                dve.wait_ge(split_hi, i * RING + (at.splits(c) + 1))
                dve.tensor_tensor(wlo[c % RING][:, 0:width], raw[c % RING][:, 0:width], whi[c % RING][:, 0:width].bitcast(F32),
                                  ALU.subtract).then_inc(split_lo, 1)

            def split_ahead(n=1):
                c = at.chunk
                for _ in range(0 if at.last else n):
                    split(ahead=True)
                at.chunk = c

            def normalise(turns=True):
                g = at.gains
                at.gains += 1
                dve.wait_ge(gain_landed[g % 2], 16 * (g // 2 + 1))
                for t, half in halves(True):
                    if half == 0:
                        dve.wait_ge(rstd_ready, 2 * g + t + 1)
                    dst = xn if turns else h
                    cols_h = slice(half * 512, half * 512 + 512)
                    dve.scalar_tensor_tensor(out=dst[:, t, cols_h], in0=h[:, t, cols_h], scalar=rstd[:, t:t + 1],
                                             in1=gain[g % 2][:, cols_h], op0=ALU.mult, op1=ALU.mult)\
                       .then_inc(xn_ready if turns else h_ready, 1)

            def x_low():
                for g in range(4):
                    t, half = g // 2, g % 2
                    dve.wait_ge(xhi_ready, at.turned + g + 1)
                    dst = slice(4 * half, 4 * half + 4), slice(t * P, (t + 1) * P)
                    dve.tensor_tensor(xlo[:, dst[0], dst[1]], ps[:, 4 + g, :].rearrange("p (k t) -> p k t", k=4),
                                      xhi[:, dst[0], dst[1]].bitcast(F32), ALU.subtract).then_inc(bank_free[4 + g], 1)
                at.turned += 4

            def out_product(scale=None):
                first = at.chunk
                for q in range(4):
                    split()
                for q in range(4):
                    if q == 3:
                        split_ahead(1)
                    dve.wait_ge(chunk_used, first + q + 1)
                    for t in range(TT):
                        piece = h[:, t, q * CW:(q + 1) * CW]
                        prod = ps[:, q, t * CW:(t + 1) * CW]
                        if scale is None:
                            ins = dve.tensor_tensor(piece, prod, piece, ALU.add)
                        else:
                            ins = dve.scalar_tensor_tensor(out=piece, in0=prod, scalar=scale[:, t:t + 1], in1=piece,
                                                           op0=ALU.mult, op1=ALU.add)
                        if q % 2 == 1:
                            ins.then_inc(h_ready, 1)
                at.h += 1

            def ffn(alpha):
                first = at.chunk

                def multiply():
                    dve.tensor_tensor(hid[:], silu[:], ps[:, 5, :].rearrange("p (a s) -> p a s", a=2), ALU.mult).then_inc(hid_ready, 1)

                def low_part(dst=hlo[:], high=hhi[:]):
                    dve.tensor_tensor(dst, hid[:], high.bitcast(F32), ALU.subtract).then_inc(hlo_ready, 1)

                split()
                split()
                with dve.Fori(0, PAIRS - 2) as i:
                    split(i)
                    split(i)
                    dve.wait_ge(silu_ready, i + (at.hids + 1))
                    dve.wait_ge(chunk_used, i * 3 + (first + 2))
                    multiply()
                    dve.wait_ge(hhi_ready, i + (at.hids + 1))
                    low_part()
                    split(i)
                at.chunk += 3 * (PAIRS - 3)
                at.hids += PAIRS
                split()
                dve.wait_ge(silu_ready, at.hids - 1)
                dve.wait_ge(chunk_used, at.chunk - 1)
                multiply()
                split()
                dve.wait_ge(hhi_ready, at.hids - 1)
                low_part()
                split()
                split()
                dve.wait_ge(silu_ready, at.hids)
                dve.wait_ge(chunk_used, at.chunk - 2)
                dve.wait_ge(hlo_ready, at.hids - 1)
                multiply()
                dve.wait_ge(hhi_ready, at.hids)
                low_part(xlo[:, 0:2, :], xhi[:, 0:2, :])
                split_ahead(1)
                for n, (t, half) in enumerate(halves(True)):
                    if n < 3:
                        dve.wait_ge(half_summed, 3 * at.h_ffn + n + 1)
                    else:
                        dve.wait_ge(chunk_used, at.chunk)
                    piece = h[:, t, half * 512:half * 512 + 512]
                    dve.scalar_tensor_tensor(out=piece, in0=ps[:, 2 * t + half, :], scalar=alpha, in1=piece,
                                             op0=ALU.mult, op1=ALU.add).then_inc(h_ready, 1)
                at.h_ffn += 1
                at.h += 1

            def pair_of(bank):
                return ps[:, bank, :].rearrange("p (a s) -> p a s", a=2)

            def rounds(take, n=4):
                first = at.chunk
                for r in range(3):
                    split()
                with dve.Fori(0, n - 1) as i:
                    for r in range(3):
                        split(i)
                        take(i, r, i * 3 + (first + r + 1))
                at.chunk += 3 * (n - 2)
                for r in range(3):
                    split()
                    take(n - 1, r, first + 3 * (n - 1) + r + 1)
                at.split = at.chunk
                at.chunk -= 3

            def lower_bound():
                l0, l1 = cols[:, R_LB:R_LB + 8], cols[:, R_LB + 8:R_LB + 16]
                link(dve.tensor_tensor(lbw[:, 4, :], l0, l1, ALU.max))
                link(dve.tensor_tensor(lbw[:, 2, :], l0, lbw[:, 4, :], ALU.subtract))
                dve.tensor_tensor(lbw[:, 3, :], l1, lbw[:, 4, :], ALU.subtract).then_inc(lb_shift, 1)
                dve.wait_ge(lb_exp, 1)
                link(dve.tensor_tensor(lbw[:, 2, :], lbw[:, 0, :], lbw[:, 1, :], ALU.add))
                link(dve.reciprocal(lbw[:, 3, :], lbw[:, 2, :]))
                link(dve.tensor_tensor(lbw[:, 5, :], lbw[:, 0, :], lbw[:, 3, :], ALU.mult))
                link(dve.tensor_scalar(lbw[:, 4, :], lbw[:, 5, :], -1.0, 1.0, ALU.mult, ALU.add))

            def hgrn():
                lower_bound()

                def take(i, r, used):
                    if r == 0:
                        dve.wait_ge(q_sig, i + 1)
                        dve.tensor_tensor(gq[:, bass.ds(i * 2, 2), :], junk[:, 0:2 * S].rearrange("p (a s) -> p a s", a=2),
                                          pair_of(0), ALU.mult).then_inc(bank_free[0], 1)

                rounds(take)
                at.chunk += 3
                dve.wait_ge(bank_free[1], 4)
                for hg in range(2):
                    hs = slice(4 * hg, 4 * hg + 4)
                    f = gf[0][:, hs, :]
                    for row, op in ((4, ALU.mult), (5, ALU.add)):
                        link(dve.tensor_tensor(f, f, lbw[:, row, hs].unsqueeze(2).broadcast_to([P, 4, S]), op))
                    dve.tensor_scalar(gk[:, hs, :], f, -1.0, 1.0, ALU.mult, ALU.add).then_inc(qk_ready, 1)
                for s in range(LEVELS + 1):
                    for hg in range(2):
                        hs = slice(4 * hg, 4 * hg + 4)
                        dve.wait_ge(level_scored, 2 * s + hg + 1)
                        if s == 0:
                            dve.tensor_tensor(gq[:, hs, :], gq[:, hs, :], gf[0][:, hs, :], ALU.mult).then_inc(qk_ready, 1)
                        elif s < LEVELS:
                            m = 1 << (s - 1)
                            n = S // m
                            total = gf[(s - 1) % 2][:, hs, 0:n].rearrange("p h (b two) -> p h b two", two=2)
                            dve.tensor_tensor(gf[s % 2][:, hs, 0:n // 2], total[:, :, :, 0], total[:, :, :, 1], ALU.mult)
                            for x, side, other in ((gq, 1, 0), (gk, 0, 1)):
                                v = x[:, hs, :].rearrange("p h (b two m) -> p (h b) two m", two=2, m=m)[:, :, side, :]
                                f = gf[(s - 1) % 2][:, hs, 0:n]
                                if n == S:
                                    f = f.rearrange("p h (b two) -> p (h b) two", two=2)[:, :, other:other + 1]
                                else:
                                    v = x[:, hs, :].rearrange("p h (b two m) -> p h b two m", two=2, m=m)[:, :, :, side, :]
                                    f = f.rearrange("p h (b two) -> p h b two", two=2)[:, :, :, other:other + 1]
                                ins = dve.tensor_tensor(v, v, f.broadcast_to(v.shape), ALU.mult)
                            ins.then_inc(qk_ready, 1)
                        if s == LEVELS:
                            dve.tensor_copy(gsc[:, hs, 2, :], ps[:, 2 * hg, :].rearrange("p (h t) -> p h t", h=4)).then_inc(bank_free[2 * hg], 1)
                            continue
                        for t in range(TT):
                            src = ps[:, 2 * hg + t, :].rearrange("p (h t) -> p h t", h=4)
                            mask = const[:, C_MASK + s * P:C_MASK + (s + 1) * P].unsqueeze(1).broadcast_to([P, 4, P])
                            if s == 0:
                                ins = dve.tensor_tensor(gsc[:, hs, t, :], src, mask, ALU.mult)
                            else:
                                ins = dve.copy_predicated(gsc[:, hs, t, :], mask.bitcast(U32), src)
                            ins.then_inc(bank_free[2 * hg + t], 1)
                    if s >= 2 and s % 2 == 0:
                        split()
                for p in range(4):
                    dve.wait_ge(o_squared, p + 1)
                    for a in range(2):
                        hd = 2 * p + a
                        ins = dve.scalar_tensor_tensor(out=gk[:, hd, :], in0=ps[:, 4 + p % 2, a * S:(a + 1) * S],
                                                       scalar=cols[:, R_ONORM + hd:R_ONORM + hd + 1], in1=gsig[:, hd, :],
                                                       op0=ALU.mult, op1=ALU.mult)
                    ins.then_inc(y_ready, 1)
                    dve.wait_ge(yhi_ready, at.y + p + 1)
                    sl = slice(2 * p, 2 * p + 2)
                    dve.tensor_tensor(xlo[:, sl, :], gk[:, sl, :], xhi[:, sl, :].bitcast(F32), ALU.subtract).then_inc(ylo_ready, 1)
                at.y += 4
                for t in range(TT):
                    dve.wait_ge(o_summed, 1)
                dve.tensor_scalar(orms[:, 0, :], ps[:, 6, 0:TT], 1.0 / D, EPS, ALU.mult, ALU.add).then_inc(o_summed, 1)
                return orms[:, 1, :]

            def attention(pairs, branches, pair_out, bias, scale, gate=None):
                units = pairs * branches
                for i in range(units + 2):
                    if i < units:
                        dve.wait_ge(scored, at.att + i + 1)
                        if i >= 2:
                            dve.wait_ge(probs_turned, at.att + i - 1)
                        b = i % 2
                        link(dve.scalar_tensor_tensor(out=att_l[:, b], in0=ps[:, 2 * b:2 * b + 2, 0:3 * P], scalar=scale,
                                                      in1=bias(i), op0=ALU.mult, op1=ALU.add))
                        for t in range(TT):
                            ins = dve.tensor_reduce(nmax[:, b, 2 * t:2 * t + 2], att_l[:, b, :, t * P:t * P + (t + 1) * P],
                                                    AX.X, ALU.max, negate=True)
                        ins.then_inc(max_ready, 1)
                    if 0 <= i - 1 < units:
                        b = (i - 1) % 2
                        dve.wait_ge(exp_ready, at.att + i)
                        link(dve.reciprocal(coef[:, b, :], sums[:, b, :]))
                        if gate is not None:
                            link(dve.tensor_tensor(coef[:, b, :].rearrange("p (t a) -> p t a", t=TT),
                                                   coef[:, b, :].rearrange("p (t a) -> p t a", t=TT), gate(i - 1), ALU.mult))
                        for t in range(TT):
                            for a in range(2):
                                x = att_l[:, b, a, t * P:t * P + (t + 1) * P]
                                n = 2 * t + a
                                ins = dve.tensor_scalar(x, x, coef[:, b, n:n + 1], None, ALU.mult)
                        ins.then_inc(probs_ready, 1)
                    if i >= 2 and (i - 1) % branches == 0:
                        pair = (i - 2) // branches
                        dve.wait_ge(yhi_ready, at.y + pair + 1)
                        dst, src = pair_out(pair)
                        dve.tensor_tensor(dst(xlo), src, dst(xhi).bitcast(F32), ALU.subtract).then_inc(ylo_ready, 1)
                at.att += units
                at.y += pairs

            def moba():
                def take(i, r, used):
                    if r == 2:
                        dve.wait_ge(chunk_used, used)
                        dve.tensor_scalar(mv[:, :, bass.ds(i * CW, CW)], pair_of(2), 1.0, None, ALU.mult).then_inc(bank_free[2], 1)

                rounds(take)
                dve.wait_ge(bias_landed, 32)
                attention(HEADS // 2, 1, moba_out, lambda u: mbias[:, 2 * u:2 * u + 2, :], P ** -0.5)
                out_product()

            def conv():
                per_round = 4
                base = links[0] + 1
                link(dve.memset(cpad[:, :, 0:2], 0.0))

                def tap_link(ins, i, n):
                    ins.then_inc(dve_wrote, 1)
                    dve.wait_ge(dve_wrote, i * per_round + (base + n))

                def take(i, r, used):
                    if r == 1:
                        dve.wait_ge(gate_kept, i + 1)
                        dve.wait_ge(chunk_used, used)
                        tap_link(dve.tensor_tensor(cpad[:, :, 2:S + 2], cgate[:], pair_of(1), ALU.mult), i, 1)
                        for tap in range(3):
                            for n in range(2):
                                scalar = cols[:, bass.ds(i * 2 + (R_CONV + 8 * tap + n), 1)]
                                src = cpad[:, n, tap:tap + S]
                                if tap == 0:
                                    ins = dve.tensor_scalar(cacc[:, n, :], src, scalar, None, ALU.mult)
                                else:
                                    ins = dve.scalar_tensor_tensor(out=cacc[:, n, :], in0=src, scalar=scalar, in1=cacc[:, n, :],
                                                                   op0=ALU.mult, op1=ALU.add)
                                if n == 0 and tap == 0:
                                    ins.then_inc(conv_done, 1)
                            tap_link(ins, i, 2 + tap)
                    if r == 2:
                        dve.wait_ge(chunk_used, used)
                        dve.tensor_tensor(cy[:, bass.ds(i * 2, 2), :], cacc[:], pair_of(2), ALU.mult).then_inc(dve_round, 1)

                rounds(take)
                links[0] += 4 * per_round
                for p in range(4):
                    sl = slice(2 * p, 2 * p + 2)
                    dve.wait_ge(yhi_ready, at.y + p + 1)
                    dve.tensor_tensor(xlo[:, sl, :], cy[:, sl, :], xhi[:, sl, :].bitcast(F32), ALU.subtract).then_inc(ylo_ready, 1)
                at.y += 4
                out_product()

            def mean_square(x, square, ssum, out, ready):
                link(dve.tensor_tensor(square, x, x, ALU.mult))
                link(dve.tensor_reduce(ssum, square, AX.X, ALU.add))
                dve.tensor_scalar(out, ssum, 1.0 / HD, EPS, ALU.mult, ALU.add).then_inc(ready, 1)

            def shared_kv():
                for slot in range(6):
                    split()
                normalise()
                split_ahead(1)
                x_low()

            def nsa():
                first = at.chunk
                split(width=KT * TAIL)
                split()
                dve.wait_ge(small_landed, 16 * 7)
                link(dve.tensor_tensor(kgain[:], kgain[:], qgain[:].unsqueeze(1).broadcast_to([P, 3, HD]), ALU.mult))
                split()
                dve.memset(kct[:], 0.0).then_inc(kct_zeroed, 1)
                link(dve.memset(czv, 0.0))
                dve.wait_ge(kn_kept, 4)
                mean_square(kn[:, 0:16, :], kd[:, 0:16, 0, :], kss[:, 0, 0:16], kss[:, 1, 0:16], kms_ready)
                split()

                def duplicate(n, lo, hi):
                    shape = [P, hi - lo, 2, HD]
                    g = kgain[:, n, :].unsqueeze(1).unsqueeze(1).broadcast_to(shape)
                    dve.tensor_tensor(kd[:, lo:hi], kn[:, lo:hi, :].unsqueeze(2).broadcast_to(shape), g, ALU.mult).then_inc(kd_ready, 1)

                dve.wait_ge(krs_ready, 1)
                link(dve.tensor_tensor(kn[:, 0:16, :], kn[:, 0:16, :], krs[:, 0:16].unsqueeze(2).broadcast_to([P, 16, HD]), ALU.mult))
                duplicate(1, 0, 8)
                duplicate(2, 8, 16)

                def q_chunk(q):
                    return xn[:, :, q * CW:(q + 1) * CW].rearrange("p t (h d) -> p t h d", h=4)

                def q_squares(q):
                    dve.wait_ge(q_kept, q + 1)
                    mean_square(q_chunk(q), qsq[:], qss[:, 0, q, :].rearrange("p (t h) -> p t h", t=TT), qss[:, 1, q, :], qms_ready)

                def q_scale(q):
                    dve.wait_ge(qrs_ready, q + 1)
                    dve.tensor_tensor(q_chunk(q), q_chunk(q), qrs[:, q, :].rearrange("p (t h) -> p t h", t=TT).unsqueeze(3)
                                      .broadcast_to([P, TT, 4, HD]), ALU.mult).then_inc(qn_ready, 1)

                q_squares(0)
                split()
                dve.wait_ge(pairs_landed, 16 * 8)
                for a in range(2):
                    for half in range(2):
                        pos = cols[:, R_POS + 16 * a + 8 * half:R_POS + 16 * a + 8 * half + 8].unsqueeze(2).unsqueeze(3)
                        dve.tensor_tensor(blk[a][:, 8 * half:8 * half + 8, :].rearrange("p j (g n) -> p j g n", g=NG), windows(a, half),
                                          pos.broadcast_to([P, 8, NG, N_CMP]), ALU.add).then_inc(blocks_ready, 1)
                dve.wait_ge(blocks_ready, 4)
                link(dve.memset(cp[:], 0.0))
                q_squares(1)
                q_scale(0)
                q_squares(2)
                q_scale(1)
                q_squares(3)
                q_scale(2)
                q_scale(3)
                for _ in range(4):
                    at.take_direct()

                def gelu(a):
                    dve.wait_ge(chunk_used, first + 5 + 2 * (a + 1))
                    for n in range(2):
                        part = slice((2 * a + n) * NG * N_CMP, (2 * a + n + 1) * NG * N_CMP)
                        ins = dve.tensor_scalar(cz[:, part], ps[:, C_BANKS[2 * a + n], 0:NG * N_CMP],
                                                cols[:, R_B1 + 2 * a + n:R_B1 + 2 * a + n + 1], None, ALU.add)
                    link(ins)
                    part = slice(2 * a * NG * N_CMP, 2 * (a + 1) * NG * N_CMP)
                    link(dve.tensor_tensor(cz2[:, part], cz[:, part], cz[:, part], ALU.mult))
                    link(dve.tensor_scalar(cz2[:, part], cz2[:, part], 0.044715, 1.0, ALU.mult, ALU.add))
                    dve.tensor_tensor(cz2[:, part], cz2[:, part], cz[:, part], ALU.mult).then_inc(gelu_in, 1)
                    dve.wait_ge(gelu_sig, a + 1)
                    return part

                part = gelu(0)
                dve.tensor_tensor(cz[:, part], cz[:, part], csig[:, part], ALU.mult).then_inc(gelu_ready, 1)
                link(dve.memset(kn[:, 16, :], 1.0))
                dve.wait_ge(cmp_done, 1)
                dve.tensor_copy(kn[0:NG * N_CMP, 16, :], ps[0:NG * N_CMP, 1, 0:HD]).then_inc(kc_kept, 1)
                dve.wait_ge(kc_kept, 1)
                mean_square(kn[:, 16, :], kd[:, 16, 0, :], kss[:, 0, 16:17], kss[:, 1, 16:17], kms_ready)
                dve.wait_ge(krs_ready, 2)
                link(dve.tensor_tensor(kn[:, 16, :], kn[:, 16, :], krs[:, 16:17].broadcast_to([P, HD]), ALU.mult))
                duplicate(0, 16, 17)
                part = gelu(1)
                for k in range(2):
                    z, sg = (x[:, (2 + k) * NG * N_CMP:(3 + k) * NG * N_CMP].rearrange("p (g n) -> p g n", g=NG).unsqueeze(2)
                             .broadcast_to([P, NG, 4, N_CMP]) for x in (cz, csig))
                    ins = dve.tensor_tensor(czv[:, k, :, :, 0:N_CMP], z, sg, ALU.mult)
                ins.then_inc(gelu_ready, 1)
                split_ahead(3)
                dve.wait_ge(cmp_scored, 1)
                for t in range(TT):
                    c = slice(C_CMP + t * N_CMP, C_CMP + (t + 1) * N_CMP)
                    ins = dve.scalar_tensor_tensor(out=cl[:, t, :].rearrange("p (h n) -> p h n", n=N_CMP), op0=ALU.mult, op1=ALU.add,
                                                   in0=ps[:, 3 + t, 0:NH * N_CMP].rearrange("p (h n) -> p h n", n=N_CMP), scalar=HD ** -0.5,
                                                   in1=const[:, c].unsqueeze(1).broadcast_to([P, NH, N_CMP]))
                link(ins)
                every = cl[:].rearrange("p t (h n) -> p (t h) n", h=NH)
                wide = [P, TT * NH, N_CMP]
                link(dve.tensor_reduce(cmx[:], every, AX.X, ALU.max))
                dve.tensor_tensor(every, every, cmx[:].unsqueeze(2).broadcast_to(wide), ALU.subtract).then_inc(cmp_shifted, 1)
                dve.wait_ge(cmp_exp, 1)
                link(dve.tensor_reduce(csum[:, 0, :], every, AX.X, ALU.add))
                link(dve.reciprocal(csum[:, 1, :], csum[:, 0, :]))
                dve.wait_ge(gates_ready, 1)
                gate = gates[:].rearrange("p t (h b) -> p (t h) b", b=3)
                link(dve.tensor_tensor(csum[:, 0, :], csum[:, 1, :], gate[:, :, 0], ALU.mult))
                link(dve.tensor_tensor(every, every, csum[:, 0, :].unsqueeze(2).broadcast_to(wide), ALU.mult))
                for t in range(TT):
                    c = slice(C_VALID + t * N_CMP, C_VALID + (t + 1) * N_CMP)
                    dve.tensor_tensor(cp[:, t, :, 0:N_CMP], cl[:, t, :].rearrange("p (h n) -> p h n", h=NH),
                                      const[:, c].unsqueeze(1).broadcast_to([P, NH, N_CMP]), ALU.mult).then_inc(cmp_probs, 1)
                dve.wait_ge(cmp_done, 2)
                dve.tensor_copy(vc[:], ps[:, 1, 0:NG * HD].rearrange("p (g d) -> p g d", g=NG)).then_inc(vc_kept, 1)
                attention(NH // 2, 2, nsa_out, lambda u: causal.unsqueeze(1).broadcast_to([P, 2, 3 * P]), HD ** -0.5,
                          lambda u: gates[:].rearrange("p t (h b) -> p t h b", b=3)[:, :, 2 * (u // 2):2 * (u // 2) + 2, 1 + u % 2])
                out_product()

            for n, free_at_start in enumerate((bank_free[0], hid_ready, conv_done)):
                dve.memset(token[:, n:n + 1], 0.0).then_inc(free_at_start, 1)
            dve.memset(zero[:], 0.0).then_inc(zero_ready, 1)
            dve.memset(table[BUCKETS:BUCKETS + 1, :], NEG).then_inc(zero_ready, 1)
            dve.wait_ge(cols_turned, 1)
            link(dve.tensor_copy(cols[:], ps[:, 7, 0:ROWS]))
            dve.wait_ge(bias_rowed, 1)
            dve.tensor_copy(bias_row[:], ps[0:HEADS, 5, :]).then_inc(bias_copied, 1)
            split_ahead(2)
            for name in phases:
                at.last = name == weighty[-1]
                if name == "final":
                    normalise(turns=False)
                    at.h += 1
                elif name != "ffn4" or "kv" not in phases:
                    normalise()
                    x_low()
                if name == "hgrn":
                    scale = hgrn()
                    dve.wait_ge(orms_ready, 1)
                    at.chunk -= 3
                    at.split = at.chunk + 3
                    out_product(scale)
                elif name.startswith("ffn"):
                    ffn(1.0 if name in ("ffn0", "ffn1") else 0.5)
                elif name != "final":
                    {"moba": moba, "conv": conv, "kv": shared_kv, "nsa": nsa}[name]()

        @block.tensor
        def _(pe):
            at = Place()

            def free(bank, i=0):
                n = at.fills[bank]
                at.fills[bank] += 1
                if not isinstance(i, int) or n + i > 0:
                    pe.wait_ge(bank_free[bank], i + n)

            def x_high():
                if at.fresh:
                    pe.wait_ge(xhi_ready, at.turned)

            def x_low():
                if at.fresh:
                    for b in range(4, 8):
                        pe.wait_ge(bank_free[b], at.fills[b])
                    at.fresh = False

            def across(bank, i=0):
                c = at.chunk
                at.chunk += 1
                pe.wait_ge(split_lo, i * RING + (at.splits(c) + 1))
                hi, lo = thirds(whi[c % RING][:]), thirds(wlo[c % RING][:])
                x_high()
                for n in range(2):
                    out = ps[:, bank, n * S:(n + 1) * S]
                    tile = slice(n * P, (n + 1) * P)
                    for k in range(KT):
                        pe.matmul(out, hi[:, k, tile], xhi[:, k, :], start=k == 0, stop=False)
                        pe.matmul(out, lo[:, k, tile], xhi[:, k, :], start=False, stop=False)
                    x_low()
                    for k in range(KT):
                        mm = pe.matmul(out, hi[:, k, tile], xlo[:, k, :], start=False, stop=k == KT - 1)
                mm.then_inc(chunk_used, 1)

            def along(bank, i=0, width=CW):
                c = at.chunk
                at.chunk += 1
                pe.wait_ge(split_lo, i * RING + (at.splits(c) + 1))
                hi, lo = thirds(whi[c % RING][:, 0:KT * width]), thirds(wlo[c % RING][:, 0:KT * width])
                x_high()
                for t in range(TT):
                    out = ps[:, bank, t * width:(t + 1) * width]
                    tile = slice(t * P, (t + 1) * P)
                    for k in range(KT):
                        pe.matmul(out, xhi[:, k, tile], hi[:, k, :], start=k == 0, stop=False)
                        pe.matmul(out, xhi[:, k, tile], lo[:, k, :], start=False, stop=False)
                    x_low()
                    for k in range(KT):
                        mm = pe.matmul(out, xlo[:, k, tile], hi[:, k, :], start=False, stop=k == KT - 1)
                mm.then_inc(chunk_used, 1)

            def norm():
                for g in range(4):
                    t, half = g // 2, g % 2
                    pe.wait_ge(xn_ready, at.xn + g + 1)
                    free(4 + g)
                    for k in range(4):
                        kk = 4 * half + k
                        mm = pe.transpose(ps[:, 4 + g, k * P:(k + 1) * P], xn[:, t, kk * P:(kk + 1) * P], ident)
                    mm.then_inc(turned, 1)
                at.xn += 4
                at.turned += 4
                at.fresh = True

            def out_product(skip_wait=False):
                for q in range(4):
                    if q == 0:
                        pe.wait_ge(ylo_ready, at.y)
                    if at.fills[q]:
                        pe.wait_ge(bank_free[q], at.fills[q])
                    along(q)

            def ffn(after_kv):
                pe.wait_ge(zero_ready, 1)

                def down(i=0, high=hhi, low=hlo, last=False):
                    c = at.chunk
                    at.chunk += 1
                    pe.wait_ge(split_lo, i * RING + (at.splits(c) + 1))
                    hi = whi[c % RING][:].rearrange("p (k n) -> p k n", k=2)
                    lo = wlo[c % RING][:].rearrange("p (k n) -> p k n", k=2)
                    for n, (t, half) in enumerate(halves(True)):
                        tile = slice(t * P, (t + 1) * P)
                        for k in range(2):
                            for a, b in ((high, hi), (high, lo), (low, hi)):
                                mm = pe.matmul(ps[:, 2 * t + half, :], a[:, k, tile], b[:, k, half * 512:(half + 1) * 512],
                                               start=False, stop=last and k == 1 and b is hi and a is low,
                                               skip_group_check=True)
                        if last and n < 3:
                            mm.then_inc(half_summed, 1)
                    mm.then_inc(chunk_used, 1)

                pe.wait_ge(bank_free[4], at.fills[4])
                across(4)
                across(5)
                for b in range(4):
                    if at.fills[b]:
                        pe.wait_ge(bank_free[b], at.fills[b])
                    if after_kv:
                        pe.wait_ge(kn_kept, 4)
                    pe.matmul(ps[:, b, :], zero[:, 0:P], zero[:], start=True, stop=False, skip_group_check=True)
                with pe.Fori(0, PAIRS - 2) as i:
                    pe.wait_ge(silu_ready, i + (at.hids + 1))
                    across(4, i)
                    pe.wait_ge(hlo_ready, i + (at.hids + 1))
                    down(i)
                    across(5, i)
                at.chunk += 3 * (PAIRS - 3)
                at.hids += PAIRS
                pe.wait_ge(silu_ready, at.hids - 1)
                across(4)
                pe.wait_ge(hid_ready, at.hids)
                across(5)
                pe.wait_ge(hlo_ready, at.hids - 1)
                down()
                pe.wait_ge(hlo_ready, at.hids)
                down(high=xhi, low=xlo, last=True)

            def rounds(kinds, n=4):
                for r in range(3):
                    free(r)
                    kinds[r](r)
                with pe.Fori(0, n - 1) as i:
                    for r in range(3):
                        free(r, i)
                        kinds[r](r, i)
                at.chunk += 3 * (n - 2)
                for r in range(3):
                    at.fills[r] += n - 2

            def hgrn():
                rounds((across, across, across))
                steps = 0
                for s in range(LEVELS + 1):
                    for hg in range(2):
                        if s == 0:
                            pe.wait_ge(bank_free[0], 5)
                        pe.wait_ge(qk_ready, 2 * s + hg + 1)
                        if s == LEVELS:
                            free(2 * hg)
                            for a in range(4):
                                hd = 4 * hg + a
                                mm = pe.matmul(ps[:, 2 * hg, a * P:(a + 1) * P], gk[:, hd, 0:P], gq[:, hd, P:2 * P], start=True, stop=True)
                            mm.then_inc(level_scored, 1)
                            continue
                        for t in range(TT):
                            tile = slice(t * P, (t + 1) * P)
                            free(2 * hg + t)
                            for a in range(4):
                                hd = 4 * hg + a
                                mm = pe.matmul(ps[:, 2 * hg + t, a * P:(a + 1) * P], gk[:, hd, tile], gq[:, hd, tile], start=True, stop=True)
                        mm.then_inc(level_scored, 1)
                    if s % 2 == 1:
                        free(4 + s // 2 % 2)
                        along(4 + s // 2 % 2)
                for p in range(4):
                    bank = 4 + p % 2
                    hg = p // 2
                    pe.wait_ge(bank_free[2 * hg], at.fills[2 * hg])
                    if p < 2:
                        pe.wait_ge(bank_free[bank], at.fills[bank])
                    else:
                        pe.wait_ge(ylo_ready, at.y + p - 1)
                    for a in range(2):
                        hd = 2 * p + a
                        wide = slice(hd * P, (hd + 1) * P)
                        o = ps[:, bank, a * S:(a + 1) * S]
                        pe.matmul(o[:, 0:P], gin[:, 0, wide], gsc[:, hd, 0, :], start=True, stop=True)
                        pe.matmul(o[:, P:S], gin[:, 0, wide], gsc[:, hd, 2, :], start=True, stop=False)
                        mm = pe.matmul(o[:, P:S], gin[:, 1, wide], gsc[:, hd, 1, :], start=False, stop=True)
                    mm.then_inc(o_ready, 1)
                pe.wait_ge(o_squared, 4)
                for t in range(TT):
                    for hd in range(HEADS):
                        mm = pe.matmul(ps[:, 6, t:t + 1], gq[:, hd, t * P:(t + 1) * P], one, start=hd == 0, stop=hd == HEADS - 1)
                mm.then_inc(o_summed, 1)
                at.y += 4

            def attention(pairs, branches, q_of, k_of, pv):
                units = pairs * branches
                for b in range(8):
                    if at.fills[b]:
                        pe.wait_ge(bank_free[b], at.fills[b])

                def logits(u):
                    if u >= 2:
                        pe.wait_ge(max_ready, at.att + u - 1)
                    for a in range(2):
                        q, k = q_of(u, a), k_of(u, a)
                        bank = 2 * (u % 2) + a
                        pe.matmul(ps[:, bank, 0:P], q[:, 0:P], k[:, 0:P], start=True, stop=True)
                        mm = pe.matmul(ps[:, bank, P:3 * P], q[:, P:S], k, start=True, stop=True)
                    mm.then_inc(scored, 1)

                def turn(u):
                    pe.wait_ge(probs_ready, at.att + u + 1)
                    if u >= 1:
                        pe.wait_ge(pt_ready, at.att + u)
                    for a in range(2):
                        for n in range(3):
                            mm = pe.transpose(ps[:, 4 + a, n * P:(n + 1) * P], att_l[:, u % 2, a, n * P:(n + 1) * P], ident)
                    mm.then_inc(probs_turned, 1)

                def values(u):
                    pe.wait_ge(pt_ready, at.att + u + 1)
                    pair = u // branches
                    if pair and u % branches == 0:
                        pe.wait_ge(ylo_ready, at.y + pair)
                    pv(u, att_pt[:, u % 2]).then_inc(pv_done, 1)

                logits(0)
                for i in range(units + 2):
                    if i + 1 < units:
                        logits(i + 1)
                    if i >= 2:
                        values(i - 2)
                    if 0 <= i - 1 < units:
                        turn(i - 1)
                at.att += units
                at.y += pairs

            def moba():
                rounds((across, across, along))

                def pv(u, pt):
                    for a in range(2):
                        v = mv[:, :, (2 * u + a) * P:(2 * u + a + 1) * P]
                        part = slice(a * P, (a + 1) * P)
                        pe.matmul(ps[:, 6, part], v[:, 0, :], pt[:, a, 0:P], start=True, stop=True)
                        pe.matmul(ps[:, 7, part], v[:, 0, :], pt[:, a, P:2 * P], start=True, stop=False)
                        mm = pe.matmul(ps[:, 7, part], v[:, 1, :], pt[:, a, 2 * P:3 * P], start=False, stop=True)
                    return mm

                attention(HEADS // 2, 1, lambda u, a: mq[:, 2 * u + a, :], lambda u, a: mk[:, 2 * u + a, :], pv)
                out_product()

            def conv():
                for r in range(3):
                    if at.fills[r]:
                        pe.wait_ge(bank_free[r], at.fills[r])
                for r, kind in enumerate((across, across, across)):
                    kind(r)
                with pe.Fori(0, 3) as i:
                    for r in range(3):
                        pe.wait_ge((conv_done, conv_done, dve_round)[r], i + (2, 2, 1)[r])
                        across(r, i)
                at.chunk += 6
                pe.wait_ge(dve_round, 4)
                at.y += 4
                out_product()

            def shared_kv():
                for slot in range(6):
                    bank = slot % 4
                    if slot < 4:
                        if at.fills[bank]:
                            pe.wait_ge(bank_free[bank], at.fills[bank])
                    else:
                        pe.wait_ge(raw_kept, slot - 3)
                    if slot == 5:
                        norm()
                        at.fresh = False
                    (across if slot < 2 else along)(bank)
                at.fresh = True

            def nsa():
                c = at.chunk
                at.chunk += 1
                pe.wait_ge(split_lo, at.splits(c) + 1)
                hi, lo = thirds(whi[c % RING][:, 0:KT * TAIL]), thirds(wlo[c % RING][:, 0:KT * TAIL])
                x_high()
                out = ps[0:TAIL, 0, 0:S]
                for k in range(KT):
                    pe.matmul(out, hi[:, k, :], xhi[:, k, :], start=k == 0, stop=False)
                    pe.matmul(out, lo[:, k, :], xhi[:, k, :], start=False, stop=False)
                x_low()
                for k in range(KT):
                    mm = pe.matmul(out, hi[:, k, :], xlo[:, k, :], start=False, stop=k == KT - 1)
                mm.then_inc(chunk_used, 1)
                along(1)
                along(2)
                pe.wait_ge(gates_t_ready, 1)
                for t in range(TT):
                    mm = pe.transpose(ps[:, 0, t * TAIL:(t + 1) * TAIL], gates_t[:, t * P:(t + 1) * P], ident[0:TAIL, 0:TAIL])
                mm.then_inc(gates_turned, 1)
                along(3)
                pe.wait_ge(kd_ready, 2)
                for n in range(4):
                    if n == 3:
                        pe.wait_ge(gates_ready, 1)
                    for g in range(NG):
                        mm = pe.transpose(ps[:, KT_BANKS[n], g * P:(g + 1) * P], kd[:, 4 * n + g].rearrange("p a d -> p (a d)"), ident)
                    mm.then_inc(kt_turned, 1)
                along(4)

                def compress(a, half):
                    c = at.chunk
                    at.take_direct()
                    pe.wait_ge(landed[c % RING], 16 * (c // RING + 1))
                    pe.wait_ge(blocks_ready, 2 * a + half + 1)
                    if half == 0:
                        pe.wait_ge(kt_kept, 2 * a + 2)
                    for n in range(2):
                        for k in range(KT):
                            mm = pe.matmul(ps[:, C_BANKS[2 * a + n], 0:NG * N_CMP], thirds(raw[c % RING][:])[:, k, n * P:(n + 1) * P],
                                           blk[a][:, 8 * half + k, :], start=half == 0 and k == 0, stop=half == 1 and k == KT - 1)
                    mm.then_inc(chunk_used, 1)

                compress(0, 0)
                compress(0, 1)
                compress(1, 0)
                pe.wait_ge(gelu_ready, 1)
                pe.wait_ge(q_kept, 1)
                for k in range(2):
                    mm = pe.matmul(ps[0:NG * N_CMP, 1, 0:HD], cz[:, k * NG * N_CMP:(k + 1) * NG * N_CMP], w2sb[:, k, :], start=k == 0, stop=k == 1)
                mm.then_inc(cmp_done, 1)
                compress(1, 1)
                pe.wait_ge(q_kept, 4)
                for n in range(4):
                    t, half = n // 2, n % 2
                    pe.wait_ge(qn_ready, 4 if half else 2)
                    for k in range(4):
                        kk = 4 * half + k
                        mm = pe.transpose(ps[:, 3 + n, k * P:(k + 1) * P], xn[:, t, kk * P:(kk + 1) * P], ident)
                    mm.then_inc(q_turned, 1)
                pe.wait_ge(kd_ready, 3)
                c = NG * N_CMP
                pe.transpose(ps[:, 2, 0:c], kd[0:c, 16].rearrange("p a d -> p (a d)"), ident[0:c, 0:c]).then_inc(kt_turned, 1)
                pe.wait_ge(nq_ready, 4)
                pe.wait_ge(kct_ready, 2)
                for t in range(TT):
                    for pair in range(NH // 2):
                        mm = pe.matmul(ps[:, 3 + t, pair * 2 * N_CMP:(pair + 1) * 2 * N_CMP], nq[:, pair, t * P:(t + 1) * P],
                                       kct[:, pair // 2].rearrange("p a n -> p (a n)"), start=True, stop=True)
                mm.then_inc(cmp_scored, 1)
                pe.wait_ge(gelu_ready, 2)
                pe.wait_ge(kc_kept, 1)
                for g in range(NG):
                    for k in range(2):
                        mm = pe.matmul(ps[:, 1, g * HD:(g + 1) * HD], czv[:, k, g].rearrange("p h n -> p (h n)"), w2sb[:, 2 + k, :],
                                       start=k == 0, stop=k == 1)
                mm.then_inc(cmp_done, 1)
                for t in range(TT):
                    pe.wait_ge(cmp_probs, t + 1)
                    for g in range(NG):
                        mm = pe.transpose(ps[:, 5 + t, g * P:(g + 1) * P], cp[:, t, 4 * g:4 * g + 4, :].rearrange("p h n -> p (h n)"), ident)
                    mm.then_inc(cmp_turned, 1)
                pe.wait_ge(cpt_ready, 2)
                pe.wait_ge(vc_kept, 1)

                def q_of(u, a):
                    return nq[a * HD:(a + 1) * HD, u // 2, :]

                def k_of(u, a):
                    return kt[a * HD:(a + 1) * HD, u % 2, u // 4, :]

                def pv(u, pt):
                    pair, branch = u // 2, u % 2
                    g = pair // 2
                    for a in range(2):
                        hd = 2 * pair + a
                        out = [ps[a * HD:(a + 1) * HD, 6 + t, 0:P] for t in range(TT)]
                        if branch == 0:
                            rows_c = slice(32 * (hd % 4), 32 * (hd % 4) + N_CMP)
                            for t in range(TT):
                                pe.matmul(out[t], vc[rows_c, g, :], cpt[rows_c, g, t * P:(t + 1) * P], start=True, stop=False)
                        v = vn[:, branch, :, g * HD:(g + 1) * HD]
                        last = branch == 1
                        pe.matmul(out[0], v[:, 0, :], pt[:, a, 0:P], start=False, stop=last)
                        pe.matmul(out[1], v[:, 0, :], pt[:, a, P:2 * P], start=False, stop=False)
                        mm = pe.matmul(out[1], v[:, 1, :], pt[:, a, 2 * P:3 * P], start=False, stop=last)
                    return mm

                attention(NH // 2, 2, q_of, k_of, pv)
                out_product()

            pe.wait_ge(const_landed, 16 * 6)
            pe.transpose(ps[:, 7, 0:ROWS], rows[:], ident[0:ROWS, 0:ROWS]).then_inc(cols_turned, 1)
            pe.wait_ge(small_landed, 16 * 7)
            pe.wait_ge(zero_ready, 2)
            pe.matmul(ps[0:HEADS, 5, :], table[:], places[:], start=True, stop=True).then_inc(bias_rowed, 1)
            for name in phases:
                if name == "final":
                    continue
                if name == "hgrn":
                    pe.wait_ge(dve_wrote, 1)
                if name != "ffn4" or "kv" not in phases:
                    norm()
                if name == "hgrn":
                    hgrn()
                    out_product()
                elif name.startswith("ffn"):
                    ffn(name == "ffn4" and "kv" in phases)
                else:
                    {"moba": moba, "conv": conv, "kv": shared_kv, "nsa": nsa}[name]()


_INS = ['x', 'norm_mix', 'norm_ffn', 'hgrn_w_in', 'hgrn_lb_logits', 'hgrn_out_norm', 'hgrn_w_out', 'moba_w_in', 'moba_w_out', 'rel_bias_table', 'ffn_w13', 'ffn_w2', 'final_norm', 'ffn_norm_2', 'ffn_w_gate_up_2', 'ffn_w_down_2', 'mix_norm_2', 'conv_w_in_2', 'conv_w_2', 'conv_w_out_2', 'kv_norm_2', 'kv_w_2', 'cmp_pos_2', 'cmp_w1_2', 'cmp_b1_2', 'cmp_w2_2', 'k_norm_2', 'nsa_w_qg_2', 'q_norm_2', 'nsa_w_o_2']


def kernel(**inputs):
    import concourse.bacc as bacc
    from concourse.bass_utils import run_bass_kernel_spmd

    nc = bacc.Bacc("TRN2", target_bir_lowering=False, num_devices=1)
    masks, places = constants()
    arrays = {name: np.ascontiguousarray(inputs[name]) for name in _INS}
    arrays["masks"], arrays["places"] = masks, places
    w = {name: nc.dram_tensor(f"in_{name}", a.shape, mybir.dt.from_np(a.dtype), kind="ExternalInput").ap() for name, a in arrays.items()}
    out = nc.dram_tensor("out_0", (1, S, D), F32, kind="ExternalOutput").ap()
    build(nc, w, out)
    r = run_bass_kernel_spmd(nc, [{f"in_{name}": a for name, a in arrays.items()}], core_ids=[0])
    return r.results[0]["out_0"]
```

```python
from contextlib import ExitStack

import numpy as np

import concourse.bass as bass
from concourse import mybir

F32 = mybir.dt.float32
F32R = mybir.dt.float32r
BF16 = mybir.dt.bfloat16
U32 = mybir.dt.uint32
ALU = mybir.AluOpType
ACT = mybir.ActivationFunctionType
AX = mybir.AxisListType

P = 128
S = 256
TT = S // P
D = 1024
KT = D // P
CW = 256
RING = 3
HEADS = 8
F_FF = 2816
PAIRS = F_FF // CW
EPS = 1e-6
NEG = -1e30
LEVELS = 8
NH = 16
HD = 64
NG = 4
CMP_STRIDE, CMP_BLOCK = 16, 32
N_CMP = (S - CMP_BLOCK) // CMP_STRIDE + 1
TAIL = 48
BUCKETS, MAX_DISTANCE = 32, 1024

C_MASK = 0
C_CAUSAL = C_MASK + LEVELS * P
C_CMP = C_CAUSAL + 3 * P
C_VALID = C_CMP + TT * N_CMP
C_ONE = C_VALID + TT * N_CMP
C_HALF = C_ONE + 2
C_COLS = C_HALF + NH * TT

C_BANKS = (5, 6, 7, 0)
WARM_START = 22
WARM_FIRST = 5
WARM = {
    "start": (0, 0, 4, 0), "swiglu": (5, 0, 3, 0), "mixer": (12, 0, 3, 0), "final": (22, 0, 3, 0), "kv": (0, 0, 0, 0)}
WARM_MOBA, WARM_NSA = (6, 2), (12, 0)
WARM_CMP = 16

C_BANKS = (5, 6, 7, 0)
KT_BANKS = (5, 6, 7, 0)
BY_BLOCK = 6

R_ONORM, R_LB, R_CONV, R_B1, R_POS = 0, 8, 24, 48, 52
ROWS = R_POS + 32

PHASES = ["hgrn", "ffn0", "moba", "ffn1", "final", "ffn2", "conv", "ffn3", "kv", "ffn4", "nsa", "ffn5"]


def constants():
    c = np.zeros((P, C_COLS), np.float32)
    s, t = np.arange(P)[:, None], np.arange(P)[None, :]
    c[:, :P] = s == t
    for level in range(LEVELS - 1):
        m = 1 << level
        keep = (s // (2 * m) == t // (2 * m)) & (s // m % 2 == 0) & (t // m % 2 == 1)
        c[:, C_MASK + (level + 1) * P:C_MASK + (level + 2) * P] = keep
    diagonal = np.where(np.arange(P)[None, :] <= np.arange(P)[:, None], 0, NEG)
    c[:, C_CAUSAL:C_CAUSAL + P] = diagonal
    c[:, C_CAUSAL + 2 * P:C_CAUSAL + 3 * P] = diagonal
    end = np.arange(N_CMP) * CMP_STRIDE + CMP_BLOCK - 1
    for tt in range(TT):
        valid = end[None, :] <= (tt * P + np.arange(P))[:, None]
        c[:, C_CMP + tt * N_CMP:C_CMP + (tt + 1) * N_CMP] = np.where(valid, 0, NEG)
        c[:, C_VALID + tt * N_CMP:C_VALID + (tt + 1) * N_CMP] = valid
    c[:, C_ONE:C_ONE + 2] = 1
    c[:, C_HALF:C_HALF + NH * TT] = -0.5
    dist = S - 1 - np.arange(2 * S)
    n = np.maximum(dist, 0)
    exact = BUCKETS // 2
    far = np.log(np.maximum(n, exact).astype(np.float32) / np.float32(exact)) / np.float32(np.log(MAX_DISTANCE / exact))
    far = exact + (far * np.float32(BUCKETS - exact)).astype(np.int32)
    bucket = np.where(n < exact, n, np.minimum(far, BUCKETS - 1))
    places = np.zeros((BUCKETS + 1, 2 * S), np.float32)
    places[bucket, np.arange(2 * S)] = dist >= 0
    places[BUCKETS] = dist < 0
    return c, places


class Place:

    def __init__(self):
        self.chunk = 0
        self.split = 0
        self.h = 0
        self.turned = 0
        self.xn = 0
        self.gains = 0
        self.hids = 0
        self.y = 0
        self.fills = [1] + [0] * 7
        self.att = 0
        self.h_ffn = 0
        self.fresh = False
        self.by_tile = True
        self.direct = []
        self.last = False

    def take_direct(self):
        self.direct.append(self.chunk)
        self.chunk += 1

    def splits(self, c):
        return c - sum(d < c for d in self.direct)


def build(nc, w, out, phases=PHASES):
    with ExitStack() as ctx:
        def sb(name, shape, dt=F32):
            return ctx.enter_context(nc.sbuf_tensor(name, shape, dt))

        def sem(name):
            return ctx.enter_context(nc.semaphore(name))

        ps = ctx.enter_context(nc.psum_tensor("ps", [P, 8, 512], F32))

        raw = [sb(f"raw{n}", [P, 2048]) for n in range(RING)]
        whi = [sb(f"whi{n}", [P, 2048], F32R) for n in range(RING)]
        wlo = [sb(f"wlo{n}", [P, 2048], F32R) for n in range(RING)]
        h = sb("h", [P, TT, D])
        xn = sb("xn", [P, TT, D])
        xhi = sb("xhi", [P, KT, S], F32R)
        xlo = sb("xlo", [P, KT, S], F32R)
        gain = [sb(f"gain{n}", [P, D]) for n in range(2)]
        junk = sb("junk", [P, D])
        silu = sb("silu", [P, 2, S])
        hid = sb("hid", [P, 2, S])
        hhi = sb("hhi", [P, 2, S], F32R)
        hlo = sb("hlo", [P, 2, S], F32R)
        ss = sb("ss", [P, TT, 2])
        ms = sb("ms", [P, TT])
        rstd = sb("rstd", [P, TT])
        const = sb("const", [P, C_COLS])
        token = sb("token", [P, 3])
        ident_b = sb("ident_b", [P, P], BF16)
        mask_b = sb("mask_b", [P, 2 * P], BF16)
        zero = sb("zero", [P, 512], BF16)
        rows = sb("rows", [ROWS, P])
        cols = sb("cols", [P, ROWS])
        arena = sb("arena", [P, 13312])

        def area(start, *dims):
            n = int(np.prod(dims))
            assert start + n <= 13312
            v = arena[:, start:start + n]
            if len(dims) == 2:
                v = v.rearrange("p (a b) -> p a b", b=dims[1])
            if len(dims) == 3:
                v = v.rearrange("p (a b c) -> p a b c", b=dims[1], c=dims[2])
            return v

        ident = const[:, 0:P]
        one = const[:, C_ONE:C_ONE + 1]
        causal = const[:, C_CAUSAL:C_CAUSAL + 3 * P]

        gq = area(0, HEADS, S)
        gk = area(2048, HEADS, S)
        gf = [area(4096, HEADS, S), area(6144, HEADS, P)]
        gsig = area(7168, HEADS, S)
        gsc = area(9216, HEADS, 3, P)
        gin = xn
        lbw = sb("lbw", [P, 6, HEADS])
        orms = sb("orms", [P, 2, TT])

        att_l = area(9216, 2, 2, 3 * P)
        att_pt = area(10752, 2, 2, 3 * P)
        nmax = sb("nmax", [P, 2, 4])
        sums = sb("sums", [P, 2, 4])
        coef = sb("coef", [P, 2, 4])

        mq = area(0, HEADS, S)
        mk = area(2048, HEADS, S)
        mv = area(4096, TT, D)
        mbias = area(6144, HEADS, 3 * P)
        table = sb("table_sb", [BUCKETS + 1, HEADS])
        places = sb("places_sb", [BUCKETS + 1, 2 * S])
        bias_row = sb("bias_row", [HEADS, 2 * S])
        bias_dram = nc.dram_tensor("bias_rows", [P, HEADS, 2 * S], F32, kind="Internal").ap()

        cpad = area(0, 2, S + 2)
        cgate = area(516, 2, S)
        cacc = area(1028, 2, S)
        cy = area(2048, KT, S)

        raw_t = area(0, 2, 2, S)
        pairs_t = area(1024, 2, NG, S)
        kn = area(4096, 17, HD)
        kd = area(9216, 17, 2, HD)
        kt = area(6144, 2, NG, S)
        vn = area(8192, 2, TT, NG * HD)
        blk = [area(11392 + 960 * a, 16, NG * N_CMP) for a in range(2)]
        cz, cz2, csig = silu[:].rearrange("p a s -> p (a s)"), hid[:].rearrange("p a s -> p (a s)"), area(3584, 240)
        czv = junk[:].rearrange("p (k g h n) -> p k g h n", k=2, g=NG, h=4)
        kct = area(5696, NG, 2, N_CMP)
        vc = area(5816, NG, HD)
        kss = sb("kss", [P, 2, 17])
        krs = sb("krs", [P, 17])
        kgain = sb("kgain", [P, 3, HD])
        qgain = sb("qgain", [P, HD])
        w2sb = sb("w2sb", [P, 4, HD])

        nq = area(0, NH // 2, S)
        cl = area(2048, TT, NH * N_CMP)
        cp = area(2560, TT, NH, 32)
        cpt = area(3584, NG, S)
        qsq = area(5184, TT, 4, HD)
        gates_t = sb("gates_t", [TAIL, S])
        gates = sb("gates", [P, TT, TAIL])
        qss = sb("qss", [P, 2, 4, TT * 4])
        qrs = sb("qrs", [P, 4, TT * 4])
        cmx = sb("cmx", [P, TT * NH])
        csum = sb("csum", [P, 2, TT * NH])

        landed = [sem(f"chunk_landed{n}") for n in range(RING)]
        split_hi = sem("split_hi")
        split_lo = sem("split_lo")
        chunk_used = sem("chunk_used")
        bank_free = [sem(f"bank_free{n}") for n in range(8)]
        x_landed = [sem(f"x_landed{t}") for t in range(TT)]
        const_landed = sem("const_landed")
        ident_landed = sem("ident_landed")
        rows_landed = sem("rows_landed")
        gain_landed = [sem(f"gain_landed{n}") for n in range(2)]
        h_ready = sem("h_ready")
        squares_summed = sem("squares_summed")
        ms_ready = sem("ms_ready")
        rstd_ready = sem("rstd_ready")
        xn_ready = sem("xn_ready")
        turned = sem("turned")
        xhi_ready = sem("xhi_ready")
        silu_ready = sem("silu_ready")
        half_summed = sem("half_summed")
        hid_ready = sem("hid_ready")
        hhi_ready = sem("hhi_ready")
        hlo_ready = sem("hlo_ready")
        zero_ready = sem("zero_ready")
        cols_turned = sem("cols_turned")
        cols_ready = sem("cols_ready")
        dve_wrote = sem("dve_wrote")
        lb_exp = sem("lb_exp")
        lb_shift = sem("lb_shift")
        q_sig = sem("q_sig")
        fk_ready = sem("fk_ready")
        q_ready = sem("q_ready")
        k_ready = sem("k_ready")
        level_scored = sem("level_scored")
        o_ready = sem("o_ready")
        o_squared = sem("o_squared")
        heads_summed = sem("heads_summed")
        y_ready = sem("y_ready")
        yhi_ready = sem("yhi_ready")
        ylo_ready = sem("ylo_ready")
        conv_round_done = sem("conv_round_done")
        o_summed = sem("o_summed")
        orms_ready = sem("orms_ready")
        out_landed = sem("out_landed")
        bias_rowed = sem("bias_rowed")
        bias_copied = sem("bias_copied")
        bias_stored = sem("bias_stored")
        bias_landed = sem("bias_landed")
        scored = sem("scored")
        max_ready = sem("max_ready")
        exp_ready = sem("exp_ready")
        probs_ready = sem("probs_ready")
        probs_turned = sem("probs_turned")
        pt_ready = sem("pt_ready")
        pv_done = sem("pv_done")
        conv_done = sem("conv_done")
        gate_kept = sem("gate_kept")
        raw_kept = sem("raw_kept")
        pairs_landed = sem("pairs_landed")
        gelu_in = sem("gelu_in")
        gelu_sig = sem("gelu_sig")
        gelu_ready = sem("gelu_ready")
        cmp_done = sem("cmp_done")
        kn_kept = sem("kn_kept")
        kms_ready = sem("kms_ready")
        krs_ready = sem("krs_ready")
        kd_ready = sem("kd_ready")
        kt_turned = sem("kt_turned")
        kt_kept = sem("kt_kept")
        vc_kept = sem("vc_kept")
        q_kept = sem("q_kept")
        qms_ready = sem("qms_ready")
        qrs_ready = sem("qrs_ready")
        qn_ready = sem("qn_ready")
        q_turned = sem("q_turned")
        nq_ready = sem("nq_ready")
        gates_ready = sem("gates_ready")
        gates_t_ready = sem("gates_t_ready")
        gates_turned = sem("gates_turned")
        blocks_ready = sem("blocks_ready")
        kc_kept = sem("kc_kept")
        kct_ready = sem("kct_ready")
        kct_zeroed = sem("kct_zeroed")
        cmp_scored = sem("cmp_scored")
        cmp_shifted = sem("cmp_shifted")
        cmp_exp = sem("cmp_exp")
        cmp_probs = sem("cmp_probs")
        cmp_turned = sem("cmp_turned")
        cpt_ready = sem("cpt_ready")
        small_landed = sem("small_landed")

        def halves_of(x, s, hs, side):
            m = 1 << (s - 1)
            n = S // m
            f = gf[(s - 1) % 2][:, hs, 0:n]
            if n == S:
                v = x[:, hs, :].rearrange("p h (b two m) -> p (h b) two m", two=2, m=m)[:, :, side, :]
                f = f.rearrange("p h (b two) -> p (h b) two", two=2)[:, :, 1 - side:2 - side]
            else:
                v = x[:, hs, :].rearrange("p h (b two m) -> p h b two m", two=2, m=m)[:, :, :, side, :]
                f = f.rearrange("p h (b two) -> p h b two", two=2)[:, :, :, 1 - side:2 - side]
            return v, f.broadcast_to(v.shape)

        def columns(matrix, at):
            return matrix.rearrange("(k p) n -> p k n", p=P)[:, :, bass.ds(at, CW)]

        def down_rows(matrix, at):
            return matrix[bass.ds(at, CW), :].rearrange("(k p) n -> p k n", p=P)

        ffn_up = [w["ffn_w13"][0], w["ffn_w13"][1]] + [w["ffn_w_gate_up_2"][a, b] for a in range(2) for b in range(2)]
        ffn_down = [w["ffn_w2"][0], w["ffn_w2"][1]] + [w["ffn_w_down_2"][a, b] for a in range(2) for b in range(2)]
        gains = {
            "hgrn": w["norm_mix"][0], "ffn0": w["norm_ffn"][0], "moba": w["norm_mix"][1], "ffn1": w["norm_ffn"][1],
            "final": w["final_norm"], "ffn2": w["ffn_norm_2"][0, 0], "conv": w["mix_norm_2"][0],
            "ffn3": w["ffn_norm_2"][0, 1], "kv": w["kv_norm_2"], "ffn4": w["ffn_norm_2"][1, 0],
            "nsa": w["mix_norm_2"][1], "ffn5": w["ffn_norm_2"][1, 1],
        }
        weighty = [name for name in phases if name != "final"]
        gain_rows = [gains[name] for name in phases]
        out_w = {"hgrn": w["hgrn_w_out"][0], "moba": w["moba_w_out"][0], "conv": w["conv_w_out_2"][0], "nsa": w["nsa_w_o_2"][0]}

        def thirds(v):
            return v.rearrange("p (k n) -> p k n", k=KT)

        def moba_out(pair):
            return (lambda x: x[:, 2 * pair:2 * pair + 2, :].rearrange("p a (t s) -> p t a s", t=TT)), \
                ps[:, 6:8, 0:2 * P].rearrange("p t (a s) -> p t a s", a=2)

        def nsa_out(pair):
            return (lambda x: x[:, pair, :].rearrange("p (t s) -> p t s", t=TT)), ps[:, 6:8, 0:P]

        def windows(a, half):
            return pairs_t[:, a].rearrange("p g (m r) -> p r g m", r=16)[:, 0:16:2, :, half:half + N_CMP]

        def halves(by_tile):
            return [(n // 2, n % 2) if by_tile else (n % 2, n // 2) for n in range(4)]

        block = ctx.enter_context(nc.Block())

        @block.sync
        def _(sp):
            at = Place()

            def load(src, i=0):
                c = at.chunk
                at.chunk += 1
                if c - RING in at.direct:
                    sp.wait_ge(chunk_used, c - RING + 1)
                elif c >= RING:
                    sp.wait_ge(split_hi, i * RING + (at.splits(c - RING) + 1))
                    sp.wait_ge(split_lo, i * RING + (at.splits(c - RING) + 1))
                dst = raw[c % RING][:, 0:src.shape[1] * src.shape[2]].rearrange("p (k n) -> p k n", k=src.shape[1])
                sp.dma_start(dst, src).then_inc(landed[c % RING], 16)

            def parameters():
                for r0, src in ((R_ONORM, w["hgrn_out_norm"]), (R_LB, w["hgrn_lb_logits"])):
                    v = src.rearrange("a (k p) -> (a k) p", p=P)
                    sp.dma_start(rows[r0:r0 + v.shape[0], :], v).then_inc(rows_landed, 16)
                v = w["conv_w_2"].rearrange("a c (k p) -> (a c k) p", p=P)
                sp.dma_start(rows[R_CONV:R_CONV + 24, :], v).then_inc(rows_landed, 16)
                sp.dma_start(rows[R_B1:R_B1 + 4, :], w["cmp_b1_2"].rearrange("a (k p) -> (a k) p", p=P)).then_inc(rows_landed, 16)
                sp.dma_start(rows[R_POS:R_POS + 32, :], w["cmp_pos_2"].rearrange("a (j k) d -> (a j) (k d)", k=2)).then_inc(rows_landed, 16)
                sp.dma_start(const[:, P:C_ONE], w["masks"][:, P:C_ONE]).then_inc(const_landed, 16)
                sp.dma_start(table[0:BUCKETS, :], w["rel_bias_table"]).then_inc(small_landed, 16)
                sp.dma_start(places[:], w["places"]).then_inc(small_landed, 16)
                sp.dma_start(w2sb[:], w["cmp_w2_2"].rearrange("a (k p) d -> p (a k) d", p=P)).then_inc(small_landed, 16)
                for n in range(3):
                    sp.dma_start(kgain[:, n, :], w["k_norm_2"][n].partition_broadcast(P)).then_inc(small_landed, 16)
                sp.dma_start(qgain[:], w["q_norm_2"][0].partition_broadcast(P)).then_inc(small_landed, 16)

            def trios(matrix, starts, n=4):
                first = at.chunk == 0
                for r in range(3):
                    load(columns(matrix, starts[r]))
                if first:
                    parameters()
                with sp.Fori(0, n - 1) as i:
                    for r in range(3):
                        load(columns(matrix, i * CW + (starts[r] + CW)), i)
                at.chunk += 3 * (n - 2)

            def out_product(name):
                for q in range(4):
                    load(columns(out_w[name], q * CW))

            def ffn(n):
                up, down = ffn_up[n], ffn_down[n]
                load(columns(up, 0))
                load(columns(up, F_FF))
                with sp.Fori(0, PAIRS - 2) as i:
                    load(columns(up, i * CW + CW), i)
                    load(down_rows(down, i * CW), i)
                    load(columns(up, i * CW + (F_FF + CW)), i)
                at.chunk += 3 * (PAIRS - 3)
                load(columns(up, (PAIRS - 1) * CW))
                load(columns(up, (2 * PAIRS - 1) * CW))
                load(down_rows(down, (PAIRS - 2) * CW))
                load(down_rows(down, (PAIRS - 1) * CW))

            for t in range(TT):
                sp.dma_start(h[:, t, :], w["x"][0, t * P:(t + 1) * P, :]).then_inc(x_landed[t], 16)
            for name in phases:
                if name == "hgrn":
                    trios(w["hgrn_w_in"][0], (0, D, 3 * D))
                    for q in range(4):
                        load(columns(w["hgrn_w_in"][0], 2 * D + q * CW))
                    out_product(name)
                elif name.startswith("ffn"):
                    ffn(int(name[3:]))
                elif name == "moba":
                    trios(w["moba_w_in"][0], (0, D, 2 * D))
                    out_product(name)
                elif name == "conv":
                    trios(w["conv_w_in_2"][0], (D, 2 * D, 0))
                    out_product(name)
                elif name == "kv":
                    for slot in range(6):
                        load(columns(w["kv_w_2"], slot * CW))
                elif name == "nsa":
                    load(w["nsa_w_qg_2"][0].rearrange("(k p) n -> p k n", p=P)[:, :, D:D + TAIL])
                    for q in range(4):
                        load(columns(w["nsa_w_qg_2"][0], q * CW))
                    for a in range(2):
                        for half in range(2):
                            c = at.chunk
                            load(w["cmp_w1_2"][a, half * D:(half + 1) * D, :].rearrange("(k p) n -> p k n", p=P))
                            at.direct.append(c)
                    out_product(name)
            halves_done = 4 * len([p for p in phases if p != "kv"])
            for t in range(TT):
                sp.wait_ge(h_ready, halves_done - 2 + 2 * t)
                sp.dma_start(out[0, t * P:(t + 1) * P, :], h[:, t, :]).then_inc(out_landed, 16)
            sp.wait_ge(out_landed, 16 * TT)

        @block.scalar
        def _(act):
            at = Place()

            def split(i=0, ahead=False, width=2048):
                c = at.chunk
                at.chunk += 1
                if c < at.split:
                    return
                if ahead:
                    at.split = c + 1
                act.wait_ge(landed[c % RING], i * 16 + 16 * (c // RING + 1))
                if c >= RING:
                    act.wait_ge(chunk_used, i * RING + (c - RING + 1))
                act.activation(whi[c % RING][:, 0:width], raw[c % RING][:, 0:width], ACT.Copy).then_inc(split_hi, 1)

            def split_ahead(n=1):
                c = at.chunk
                for _ in range(0 if at.last else n):
                    split(ahead=True)
                at.chunk = c

            def load_gain():
                g = at.gains
                at.gains += 1
                if g < len(gain_rows):
                    act.dma_start(gain[g % 2][:], gain_rows[g].partition_broadcast(P)).then_inc(gain_landed[g % 2], 16)

            def squares():
                for n, (t, half) in enumerate(halves(at.by_tile)):
                    if at.h == 0:
                        act.wait_ge(x_landed[t], 16)
                    else:
                        act.wait_ge(h_ready, 4 * (at.h - 1) + n + 1)
                    cols_h = slice(half * 512, half * 512 + 512)
                    act.activation(xn[:, t, cols_h], h[:, t, cols_h], ACT.Square, scale=D ** -0.5, accum_out=ss[:, t, half:half + 1])\
                       .then_inc(squares_summed, 1)
                load_gain()

            def x_high():
                for g in range(4):
                    t, half = g // 2, g % 2
                    act.wait_ge(turned, at.turned + g + 1)
                    act.activation(xhi[:, 4 * half:4 * half + 4, t * P:(t + 1) * P],
                                   ps[:, 4 + g, :].rearrange("p (k t) -> p k t", k=4), ACT.Copy).then_inc(xhi_ready, 1)
                at.turned += 4

            def out_product():
                for q in range(4):
                    split()
                split_ahead(2)
                at.h += 1

            def ffn():
                first = at.chunk

                def activate():
                    act.activation(silu[:], ps[:, 4, :].rearrange("p (a s) -> p a s", a=2), ACT.Silu).then_inc(silu_ready, 1)

                def high_part(dst=hhi[:]):
                    act.activation(dst, hid[:], ACT.Copy).then_inc(hhi_ready, 1)

                split()
                split()
                with act.Fori(0, PAIRS - 2) as i:
                    split(i)
                    act.wait_ge(chunk_used, i * 3 + (first + 1))
                    act.wait_ge(hid_ready, i + (at.hids + 1))
                    activate()
                    split(i)
                    act.wait_ge(hid_ready, i + (at.hids + 2))
                    high_part()
                    split(i)
                at.chunk += 3 * (PAIRS - 3)
                at.hids += PAIRS - 2
                split()
                act.wait_ge(chunk_used, first + 3 * (PAIRS - 2))
                act.wait_ge(hid_ready, at.hids + 1)
                activate()
                split()
                act.wait_ge(hid_ready, at.hids + 2)
                high_part()
                split()
                act.wait_ge(chunk_used, at.chunk - 2)
                activate()
                split()
                act.wait_ge(hid_ready, at.hids + 3)
                high_part(xhi[:, 0:2, :])
                at.hids += 2
                split_ahead(2)
                at.h += 1

            def pair_of(bank):
                return ps[:, bank, :].rearrange("p (a s) -> p a s", a=2)

            def rounds(evacuate, n=4, tail=3):
                first = at.chunk
                for r in range(3):
                    split()
                with act.Fori(0, n - 1) as i:
                    for r in range(3):
                        split(i)
                        act.wait_ge(chunk_used, i * 3 + (first + r + 1))
                        evacuate(i, r)
                at.chunk += 3 * (n - 2)
                for r in range(3):
                    act.wait_ge(chunk_used, first + 3 * (n - 1) + r + 1)
                    evacuate(n - 1, r)
                    if r < tail:
                        split()
                at.split = at.chunk
                at.chunk -= tail

            def hgrn():
                def evacuate(i, r):
                    if r == 0:
                        act.wait_ge(bank_free[0], i + 1)
                        act.activation(junk[:, 0:2 * S].rearrange("p (a s) -> p a s", a=2), pair_of(0), ACT.Sigmoid).then_inc(q_sig, 1)
                    else:
                        dst = gf[0] if r == 1 else gsig
                        act.activation(dst[:, bass.ds(i * 2, 2), :], pair_of(r), ACT.Sigmoid).then_inc(bank_free[r], 1)

                def keep_blocks(s):
                    for hg in range(2):
                        act.wait_ge(level_scored, 2 * s + hg + 1)
                        hs = slice(4 * hg, 4 * hg + 4)
                        if s == LEVELS:
                            act.activation(gsc[:, hs, 2, :], ps[:, 2 * hg, :].rearrange("p (h t) -> p h t", h=4), ACT.Copy)\
                               .then_inc(bank_free[2 * hg], 1)
                            continue
                        m = 1 << (s - 1)
                        for t in range(TT):
                            for b in range(P // (2 * m)):
                                keys, queries = slice(2 * b * m, (2 * b + 1) * m), slice((2 * b + 1) * m, (2 * b + 2) * m)
                                ins = act.activation(gsc[keys, hs, t, queries], ps[keys, 2 * hg + t, :].rearrange("p (h t) -> p h t", h=4)
                                                     [:, :, queries], ACT.Copy)
                            ins.then_inc(bank_free[2 * hg + t], 1)

                split_ahead(3)
                act.wait_ge(lb_shift, 1)
                act.activation(lbw[:, 0:2, :], lbw[:, 2:4, :], ACT.Exp).then_inc(lb_exp, 1)
                rounds(evacuate)
                first = at.chunk
                at.chunk += 3
                act.wait_ge(bias_copied, 1)
                act.dma_start(bias_dram.rearrange("p h y -> h p y"), bias_row[:].unsqueeze(1).broadcast_to([HEADS, P, 2 * S]))\
                   .then_inc(bias_stored, 16)
                for n in range(4):
                    act.wait_ge(chunk_used, first + n + 1)
                    if n < 2:
                        split()
                    act.activation(gin[:, :, n * CW:(n + 1) * CW], pair_of(4 + n % 2), ACT.Copy).then_inc(bank_free[4 + n % 2], 1)
                    if n == 2:
                        for s in range(BY_BLOCK, LEVELS):
                            keep_blocks(s)
                    if n >= 2:
                        split()
                keep_blocks(LEVELS)
                for p in range(4):
                    act.wait_ge(o_ready, p + 1)
                    act.activation(gq[:, 2 * p:2 * p + 2, :], pair_of(4 + p), ACT.Square).then_inc(o_squared, 1)
                for p in range(4):
                    act.wait_ge(y_ready, at.y + p + 1)
                    act.activation(xhi[:, 2 * p:2 * p + 2, :], gk[:, 2 * p:2 * p + 2, :], ACT.Copy).then_inc(yhi_ready, 1)
                at.y += 4
                split()
                split_ahead(2)
                at.h += 1

            def attention(pairs, branches, pair_out, scale=None):
                units = pairs * branches
                for i in range(units + 2):
                    if i < units:
                        act.wait_ge(max_ready, at.att + i + 1)
                        if scale is not None and i >= 2:
                            act.wait_ge(probs_turned, at.att + i - 1)
                        for t in range(TT):
                            for a in range(2):
                                part = slice(t * P, t * P + (t + 1) * P)
                                probs = att_l[:, i % 2, a, part]
                                n = t * 2 + a
                                src = probs if scale is None else ps[:, 2 * (i % 2) + a, part]
                                ins = act.activation(probs, src, ACT.Exp, bias=nmax[:, i % 2, n:n + 1],
                                                     scale=1.0 if scale is None else scale, accum_out=sums[:, i % 2, n:n + 1])
                        ins.then_inc(exp_ready, 1)
                    if i >= 2 and (i - 1) % branches == 0:
                        act.wait_ge(pv_done, at.att + i - 1)
                        dst, src = pair_out((i - 2) // branches)
                        act.activation(dst(xhi), src, ACT.Copy).then_inc(yhi_ready, 1)
                    if 0 <= i - 1 < units:
                        act.wait_ge(probs_turned, at.att + i)
                        if i - 1 >= 2:
                            act.wait_ge(pv_done, at.att + i - 2)
                        act.activation(att_pt[:, (i - 1) % 2, :, :], ps[:, 4:6, 0:3 * P], ACT.Copy).then_inc(pt_ready, 1)
                at.att += units
                at.y += pairs

            def moba():

                def evacuate(i, r):
                    if r < 2:
                        dst = (mq, mk)[r]
                        act.activation(dst[:, bass.ds(i * 2, 2), :], pair_of(r), ACT.Copy).then_inc(bank_free[r], 1)

                act.wait_ge(bias_stored, 16)
                for t in range(TT):
                    cols_t = slice(t * P, t * P + (t + 1) * P)
                    src = bass.AP(bias_dram.tensor, S - 1 - t * P, [[HEADS * 2 * S - 1, P], [2 * S, HEADS], [1, (t + 1) * P]])
                    act.dma_start(mbias[:, :, cols_t], src).then_inc(bias_landed, 16)
                rounds(evacuate, tail=2)
                attention(HEADS // 2, 1, moba_out)
                out_product()

            def conv():
                def evacuate(i, r):
                    if r == 0:
                        act.wait_ge(conv_done, i + 1)
                        act.activation(cgate[:], pair_of(0), ACT.Copy).then_inc(gate_kept, 1)

                rounds(evacuate, tail=2)
                act.wait_ge(chunk_used, at.chunk)
                for p in range(4):
                    sl = slice(2 * p, 2 * p + 2)
                    act.wait_ge(conv_round_done, p + 1)
                    act.activation(xhi[:, sl, :], cy[:, sl, :], ACT.Copy).then_inc(yhi_ready, 1)
                at.y += 4
                out_product()

            def shared_kv():
                first = at.chunk
                dst = [raw_t[:, 0], raw_t[:, 1], kn[:, 0:8, :], vn[:, 0], kn[:, 8:16, :], vn[:, 1]]

                def keep(slot):
                    act.wait_ge(chunk_used, first + slot + 1)
                    d = dst[slot]
                    act.activation(d, ps[:, slot % 4, :].rearrange("p (a b) -> p a b", a=d.shape[1]), ACT.Copy)\
                       .then_inc(raw_kept if slot < 2 else kn_kept, 1)

                for slot in range(6):
                    split()
                    if slot >= 2:
                        keep(slot - 2)
                    if slot == 3:
                        act.wait_ge(raw_kept, 2)
                        for a in range(2):
                            for side in range(2):
                                for gp in range(2):
                                    act.dma_start(pairs_t[side * HD:(side + 1) * HD, a, gp::2, 0:S - side],
                                                  raw_t[gp * HD:(gp + 1) * HD, a, :, side:S]).then_inc(pairs_landed, 16)
                squares()
                keep(4)
                split_ahead(2)
                act.wait_ge(chunk_used, first + 6)
                x_high()
                keep(5)

            def nsa():
                first = at.chunk
                split(width=KT * TAIL)
                split()
                split()
                act.wait_ge(chunk_used, first + 1)
                act.activation(gates_t[:], ps[0:TAIL, 0, 0:S], ACT.Sigmoid).then_inc(gates_t_ready, 1)
                split()

                def keep(q):
                    act.wait_ge(chunk_used, first + q + 2)
                    act.activation(xn[:, :, q * CW:(q + 1) * CW], pair_of(1 + q), ACT.Copy).then_inc(q_kept, 1)

                keep(0)
                split()
                keep(1)
                act.wait_ge(gates_turned, 1)
                act.activation(gates[:], ps[:, 0, 0:TT * TAIL].rearrange("p (t n) -> p t n", t=TT), ACT.Copy).then_inc(gates_ready, 1)
                keep(2)
                for n in range(4):
                    act.wait_ge(kt_turned, n + 1)
                    act.activation(kt[:, n // 2, :, (n % 2) * P:(n % 2 + 1) * P], ps[:, KT_BANKS[n], :].rearrange("p (g s) -> p g s", g=NG),
                                   ACT.Copy).then_inc(kt_kept, 1)
                keep(3)
                for _ in range(4):
                    at.take_direct()
                for a in range(2):
                    part = slice(a * 2 * NG * N_CMP, (a + 1) * 2 * NG * N_CMP)
                    act.wait_ge(gelu_in, a + 1)
                    act.activation(csig[:, part], cz2[:, part], ACT.Sigmoid, scale=2 * float(np.sqrt(2 / np.pi))).then_inc(gelu_sig, 1)
                for n in range(4):
                    act.wait_ge(q_turned, n + 1)
                    t, half = n // 2, n % 2
                    act.activation(nq[:, 4 * half:4 * half + 4, t * P:(t + 1) * P], ps[:, 3 + n, :].rearrange("p (k s) -> p k s", k=4),
                                   ACT.Copy).then_inc(nq_ready, 1)
                act.wait_ge(kt_turned, 5)
                act.wait_ge(kct_zeroed, 1)
                for side in range(2):
                    half = slice(side * HD, (side + 1) * HD)
                    act.activation(kct[half, :, side, :], ps[half, 2, 0:NG * N_CMP].rearrange("p (g n) -> p g n", g=NG),
                                   ACT.Copy).then_inc(kct_ready, 1)
                split_ahead(3)
                act.wait_ge(cmp_shifted, 1)
                act.activation(cl[:], cl[:], ACT.Exp).then_inc(cmp_exp, 1)
                for t in range(TT):
                    act.wait_ge(cmp_turned, t + 1)
                    act.activation(cpt[:, :, t * P:(t + 1) * P], ps[:, 5 + t, :].rearrange("p (g s) -> p g s", g=NG),
                                   ACT.Copy).then_inc(cpt_ready, 1)
                attention(NH // 2, 2, nsa_out, HD ** -0.5)
                out_product()

            for part in (slice(0, P), slice(C_ONE, C_COLS)):
                act.dma_start(const[:, part], w["masks"][:, part]).then_inc(ident_landed, 16)
            load_gain()
            for name in phases:
                at.last = name == weighty[-1]
                if name == "final":
                    squares()
                    at.h += 1
                elif name != "ffn4" or "kv" not in phases:
                    squares()
                    if at.chunk == 0:
                        split_ahead(1)
                    x_high()
                at.by_tile = name not in ("hgrn", "moba", "conv", "nsa")
                if name.startswith("ffn"):
                    ffn()
                elif name != "final":
                    {"hgrn": hgrn, "moba": moba, "conv": conv, "kv": shared_kv, "nsa": nsa}[name]()

        @block.gpsimd
        def _(pool):
            done = 0
            norms = 0
            by_tile = True
            pool.wait_ge(ident_landed, 32)
            for name in phases:
                for t in range(TT):
                    pool.wait_ge(squares_summed, 4 * norms + [n + 1 for n, (tt, half) in enumerate(halves(by_tile)) if tt == t][1])
                    pool.tensor_scalar(ms[:, t:t + 1], ss[:, t, 0:1], ss[:, t, 1:2], EPS, ALU.add, ALU.add).then_inc(ms_ready, 1)
                    pool.wait_ge(ms_ready, 2 * norms + t + 1)
                    pool.tensor_tensor(rstd[:, t:t + 1], ms[:, t:t + 1], const[:, C_HALF:C_HALF + 1], ALU.pow).then_inc(rstd_ready, 1)
                    pool.wait_ge(rstd_ready, 2 * norms + t + 1)
                norms += 1
                by_tile = name not in ("hgrn", "moba", "conv", "nsa")
                if name == "nsa":
                    pool.wait_ge(kms_ready, 1)
                    pool.tensor_tensor(krs[:, 0:16], kss[:, 1, 0:16], const[:, C_HALF:C_HALF + 16], ALU.pow).then_inc(krs_ready, 1)
                    pool.wait_ge(krs_ready, 1)
                    for q in range(4):
                        pool.wait_ge(qms_ready, q + 1)
                        pool.tensor_tensor(qrs[:, q, :], qss[:, 1, q, :], const[:, C_HALF:C_HALF + TT * 4], ALU.pow).then_inc(qrs_ready, 1)
                        pool.wait_ge(qrs_ready, q + 1)
                    pool.wait_ge(kms_ready, 2)
                    pool.tensor_tensor(krs[:, 16:17], kss[:, 1, 16:17], const[:, C_HALF:C_HALF + 1], ALU.pow).then_inc(krs_ready, 1)
                    pool.wait_ge(krs_ready, 2)
                if name == "hgrn":
                    for s in range(1, LEVELS):
                        for hg in range(2):
                            pool.wait_ge(level_scored, 2 * s + hg + 1)
                            v, f = halves_of(gk, s, slice(4 * hg, 4 * hg + 4), 0)
                            pool.tensor_tensor(v, v, f, ALU.mult).then_inc(k_ready, 1)
                            pool.wait_ge(k_ready, 2 * (s - 1) + hg + 1)
                    pool.wait_ge(o_squared, 4)
                    for n, left in enumerate((4, 2, 1)):
                        pool.tensor_tensor(gq[:, 0:left, :], gq[:, 0:left, :], gq[:, left:2 * left, :], ALU.add).then_inc(heads_summed, 1)
                        pool.wait_ge(heads_summed, n + 1)
                    pool.wait_ge(o_summed, 2)
                    pool.tensor_tensor(orms[:, 1, :], orms[:, 0, :], const[:, C_HALF:C_HALF + TT], ALU.pow).then_inc(orms_ready, 1)
                    pool.wait_ge(orms_ready, 1)

        @block.vector
        def _(dve):
            at = Place()
            links = [0]

            def link(ins):
                links[0] += 1
                ins.then_inc(dve_wrote, 1)
                dve.wait_ge(dve_wrote, links[0])

            def split(i=0, ahead=False, width=2048):
                c = at.chunk
                at.chunk += 1
                if c < at.split:
                    return
                if ahead:
                    at.split = c + 1
                dve.wait_ge(split_hi, i * RING + (at.splits(c) + 1))
                dve.tensor_tensor(wlo[c % RING][:, 0:width], raw[c % RING][:, 0:width], whi[c % RING][:, 0:width].bitcast(F32),
                                  ALU.subtract).then_inc(split_lo, 1)

            def split_ahead(n=1):
                c = at.chunk
                for _ in range(0 if at.last else n):
                    split(ahead=True)
                at.chunk = c

            def normalise(turns=True):
                g = at.gains
                at.gains += 1
                dve.wait_ge(gain_landed[g % 2], 16 * (g // 2 + 1))
                for t, half in halves(True):
                    if half == 0:
                        dve.wait_ge(rstd_ready, 2 * g + t + 1)
                    dst = xn if turns else h
                    cols_h = slice(half * 512, half * 512 + 512)
                    dve.scalar_tensor_tensor(out=dst[:, t, cols_h], in0=h[:, t, cols_h], scalar=rstd[:, t:t + 1],
                                             in1=gain[g % 2][:, cols_h], op0=ALU.mult, op1=ALU.mult)\
                       .then_inc(xn_ready if turns else h_ready, 1)

            def x_low():
                for g in range(4):
                    t, half = g // 2, g % 2
                    dve.wait_ge(xhi_ready, at.turned + g + 1)
                    dst = slice(4 * half, 4 * half + 4), slice(t * P, (t + 1) * P)
                    dve.tensor_tensor(xlo[:, dst[0], dst[1]], ps[:, 4 + g, :].rearrange("p (k t) -> p k t", k=4),
                                      xhi[:, dst[0], dst[1]].bitcast(F32), ALU.subtract).then_inc(bank_free[4 + g], 1)
                at.turned += 4

            def out_product(scale=None):
                first = at.chunk
                for q in range(4):
                    split()
                for q in range(4):
                    if q == 3:
                        split_ahead(1)
                    dve.wait_ge(chunk_used, first + q + 1)
                    for t in range(TT):
                        piece = h[:, t, q * CW:(q + 1) * CW]
                        prod = ps[:, q, t * CW:(t + 1) * CW]
                        if scale is None:
                            ins = dve.tensor_tensor(piece, prod, piece, ALU.add)
                        else:
                            ins = dve.scalar_tensor_tensor(out=piece, in0=prod, scalar=scale[:, t:t + 1], in1=piece,
                                                           op0=ALU.mult, op1=ALU.add)
                        if q % 2 == 1:
                            ins.then_inc(h_ready, 1)
                at.h += 1

            def ffn(alpha):
                first = at.chunk

                def multiply():
                    dve.tensor_tensor(hid[:], silu[:], ps[:, 5, :].rearrange("p (a s) -> p a s", a=2), ALU.mult).then_inc(hid_ready, 1)

                def low_part(dst=hlo[:], high=hhi[:]):
                    dve.tensor_tensor(dst, hid[:], high.bitcast(F32), ALU.subtract).then_inc(hlo_ready, 1)

                split()
                split()
                with dve.Fori(0, PAIRS - 2) as i:
                    split(i)
                    split(i)
                    dve.wait_ge(silu_ready, i + (at.hids + 1))
                    dve.wait_ge(chunk_used, i * 3 + (first + 2))
                    multiply()
                    dve.wait_ge(hhi_ready, i + (at.hids + 1))
                    low_part()
                    split(i)
                at.chunk += 3 * (PAIRS - 3)
                at.hids += PAIRS
                split()
                dve.wait_ge(silu_ready, at.hids - 1)
                dve.wait_ge(chunk_used, at.chunk - 1)
                multiply()
                split()
                dve.wait_ge(hhi_ready, at.hids - 1)
                low_part()
                split()
                split()
                dve.wait_ge(silu_ready, at.hids)
                dve.wait_ge(chunk_used, at.chunk - 2)
                dve.wait_ge(hlo_ready, at.hids - 1)
                multiply()
                dve.wait_ge(hhi_ready, at.hids)
                low_part(xlo[:, 0:2, :], xhi[:, 0:2, :])
                split_ahead(1)
                for n, (t, half) in enumerate(halves(True)):
                    if n < 3:
                        dve.wait_ge(half_summed, 3 * at.h_ffn + n + 1)
                    else:
                        dve.wait_ge(chunk_used, at.chunk)
                    piece = h[:, t, half * 512:half * 512 + 512]
                    dve.scalar_tensor_tensor(out=piece, in0=ps[:, 2 * t + half, :], scalar=alpha, in1=piece,
                                             op0=ALU.mult, op1=ALU.add).then_inc(h_ready, 1)
                at.h_ffn += 1
                at.h += 1

            def pair_of(bank):
                return ps[:, bank, :].rearrange("p (a s) -> p a s", a=2)

            def rounds(take, n=4, tail=3):
                first = at.chunk
                for r in range(3):
                    split()
                with dve.Fori(0, n - 1) as i:
                    for r in range(3):
                        split(i)
                        take(i, r, i * 3 + (first + r + 1))
                at.chunk += 3 * (n - 2)
                for r in range(3):
                    take(n - 1, r, first + 3 * (n - 1) + r + 1)
                    if r < tail:
                        split()
                at.split = at.chunk
                at.chunk -= tail

            def lower_bound():
                l0, l1 = cols[:, R_LB:R_LB + 8], cols[:, R_LB + 8:R_LB + 16]
                link(dve.tensor_tensor(lbw[:, 4, :], l0, l1, ALU.max))
                link(dve.tensor_tensor(lbw[:, 2, :], l0, lbw[:, 4, :], ALU.subtract))
                dve.tensor_tensor(lbw[:, 3, :], l1, lbw[:, 4, :], ALU.subtract).then_inc(lb_shift, 1)
                dve.wait_ge(lb_exp, 1)
                link(dve.tensor_tensor(lbw[:, 2, :], lbw[:, 0, :], lbw[:, 1, :], ALU.add))
                link(dve.reciprocal(lbw[:, 3, :], lbw[:, 2, :]))
                link(dve.tensor_tensor(lbw[:, 5, :], lbw[:, 0, :], lbw[:, 3, :], ALU.mult))
                link(dve.tensor_scalar(lbw[:, 4, :], lbw[:, 5, :], -1.0, 1.0, ALU.mult, ALU.add))

            def hgrn():
                lower_bound()
                base = links[0] + 1

                def take(i, r, used):
                    if r == 0:
                        dve.wait_ge(q_sig, i + 1)
                        dve.tensor_tensor(gq[:, bass.ds(i * 2, 2), :], junk[:, 0:2 * S].rearrange("p (a s) -> p a s", a=2),
                                          pair_of(0), ALU.mult).then_inc(bank_free[0], 1)
                    if r == 1:
                        dve.wait_ge(bank_free[1], i + 1)
                        for a in range(2):
                            f = gf[0][:, bass.ds(i * 2 + a, 1), :]
                            ins = dve.tensor_scalar(f, f, lbw[:, 4, bass.ds(i * 2 + a, 1)], lbw[:, 5, bass.ds(i * 2 + a, 1)],
                                                    ALU.mult, ALU.add)
                        ins.then_inc(dve_wrote, 1)
                        dve.wait_ge(dve_wrote, i + base)
                        dve.tensor_scalar(gk[:, bass.ds(i * 2, 2), :], gf[0][:, bass.ds(i * 2, 2), :], -1.0, 1.0,
                                          ALU.mult, ALU.add).then_inc(fk_ready, 1)

                rounds(take, tail=1)
                links[0] += 4
                at.chunk += 1
                dve.wait_ge(bias_rowed, 1)
                dve.tensor_copy(bias_row[:], ps[0:HEADS, 7, :]).then_inc(bias_copied, 1)
                for s in range(LEVELS + 1):
                    for hg in range(2):
                        hs = slice(4 * hg, 4 * hg + 4)
                        dve.wait_ge(level_scored, 2 * s + hg + 1)
                        if s == 0:
                            dve.tensor_tensor(gq[:, hs, :], gq[:, hs, :], gf[0][:, hs, :], ALU.mult).then_inc(q_ready, 1)
                        elif s < LEVELS:
                            m = 1 << (s - 1)
                            n = S // m
                            total = gf[(s - 1) % 2][:, hs, 0:n].rearrange("p h (b two) -> p h b two", two=2)
                            dve.tensor_tensor(gf[s % 2][:, hs, 0:n // 2], total[:, :, :, 0], total[:, :, :, 1], ALU.mult)
                            v, f = halves_of(gq, s, hs, 1)
                            dve.tensor_tensor(v, v, f, ALU.mult).then_inc(q_ready, 1)
                        if s >= BY_BLOCK:
                            continue
                        for t in range(TT):
                            src = ps[:, 2 * hg + t, :].rearrange("p (h t) -> p h t", h=4)
                            mask = const[:, C_MASK + s * P:C_MASK + (s + 1) * P].unsqueeze(1).broadcast_to([P, 4, P])
                            if s == 0:
                                ins = dve.tensor_tensor(gsc[:, hs, t, :], src, mask, ALU.mult)
                            else:
                                ins = dve.copy_predicated(gsc[:, hs, t, :], mask.bitcast(U32), src)
                            ins.then_inc(bank_free[2 * hg + t], 1)
                    if s in (1, 3, 4, 5, 7):
                        split()
                for p in range(5):
                    if p < 4:
                        dve.wait_ge(o_squared, p + 1)
                        for a in range(2):
                            hd = 2 * p + a
                            ins = dve.scalar_tensor_tensor(out=gk[:, hd, :], in0=ps[:, 4 + p, a * S:(a + 1) * S],
                                                           scalar=cols[:, R_ONORM + hd:R_ONORM + hd + 1], in1=gsig[:, hd, :],
                                                           op0=ALU.mult, op1=ALU.mult)
                        ins.then_inc(y_ready, 1)
                    if p >= 1:
                        dve.wait_ge(yhi_ready, at.y + p)
                        sl = slice(2 * p - 2, 2 * p)
                        dve.tensor_tensor(xlo[:, sl, :], gk[:, sl, :], xhi[:, sl, :].bitcast(F32), ALU.subtract).then_inc(ylo_ready, 1)
                at.y += 4
                split()
                dve.wait_ge(o_summed, 1)
                dve.tensor_scalar(orms[:, 0, :], ps[:, 4, 0:TT], 1.0 / D, EPS, ALU.mult, ALU.add).then_inc(o_summed, 1)
                return orms[:, 1, :]

            def attention(pairs, branches, pair_out, bias, scale, gate=None):
                units = pairs * branches
                for i in range(units + 2):
                    if i < units:
                        dve.wait_ge(scored, at.att + i + 1)
                        b = i % 2
                        if bias is not None:
                            if i >= 2:
                                dve.wait_ge(probs_turned, at.att + i - 1)
                            link(dve.scalar_tensor_tensor(out=att_l[:, b], in0=ps[:, 2 * b:2 * b + 2, 0:3 * P], scalar=scale,
                                                          in1=bias(i), op0=ALU.mult, op1=ALU.add))
                        logits = ps[:, 2 * b:2 * b + 2, :] if bias is None else att_l[:, b]
                        for t in range(TT):
                            ins = dve.tensor_reduce(nmax[:, b, 2 * t:2 * t + 2], logits[:, :, t * P:t * P + (t + 1) * P],
                                                    AX.X, ALU.max, negate=True)
                        if bias is None:
                            link(ins)
                            ins = dve.tensor_scalar(nmax[:, b, :], nmax[:, b, :], scale, None, ALU.mult)
                        ins.then_inc(max_ready, 1)
                    if 0 <= i - 1 < units:
                        b = (i - 1) % 2
                        dve.wait_ge(exp_ready, at.att + i)
                        link(dve.reciprocal(coef[:, b, :], sums[:, b, :]))
                        if gate is not None:
                            link(dve.tensor_tensor(coef[:, b, :].rearrange("p (t a) -> p t a", t=TT),
                                                   coef[:, b, :].rearrange("p (t a) -> p t a", t=TT), gate(i - 1), ALU.mult))
                        for t in range(TT):
                            for a in range(2):
                                x = att_l[:, b, a, t * P:t * P + (t + 1) * P]
                                n = 2 * t + a
                                ins = dve.tensor_scalar(x, x, coef[:, b, n:n + 1], None, ALU.mult)
                        ins.then_inc(probs_ready, 1)
                    if i >= 2 and (i - 1) % branches == 0:
                        pair = (i - 2) // branches
                        dve.wait_ge(yhi_ready, at.y + pair + 1)
                        dst, src = pair_out(pair)
                        dve.tensor_tensor(dst(xlo), src, dst(xhi).bitcast(F32), ALU.subtract).then_inc(ylo_ready, 1)
                at.att += units
                at.y += pairs

            def moba():
                def take(i, r, used):
                    if r == 2:
                        dve.wait_ge(chunk_used, used)
                        dve.tensor_scalar(mv[:, :, bass.ds(i * CW, CW)], pair_of(2), 1.0, None, ALU.mult).then_inc(bank_free[2], 1)

                rounds(take, tail=2)
                dve.wait_ge(bias_landed, 32)
                attention(HEADS // 2, 1, moba_out, lambda u: mbias[:, 2 * u:2 * u + 2, :], P ** -0.5)
                out_product()

            def conv():
                per_round = 4
                base = links[0] + 1
                link(dve.memset(cpad[:, :, 0:2], 0.0))

                def tap_link(ins, i, n):
                    ins.then_inc(dve_wrote, 1)
                    dve.wait_ge(dve_wrote, i * per_round + (base + n))

                def take(i, r, used):
                    if r == 1:
                        dve.wait_ge(gate_kept, i + 1)
                        dve.wait_ge(chunk_used, used)
                        tap_link(dve.tensor_tensor(cpad[:, :, 2:S + 2], cgate[:], pair_of(1), ALU.mult), i, 1)
                        for tap in range(3):
                            for n in range(2):
                                scalar = cols[:, bass.ds(i * 2 + (R_CONV + 8 * tap + n), 1)]
                                src = cpad[:, n, tap:tap + S]
                                if tap == 0:
                                    ins = dve.tensor_scalar(cacc[:, n, :], src, scalar, None, ALU.mult)
                                else:
                                    ins = dve.scalar_tensor_tensor(out=cacc[:, n, :], in0=src, scalar=scalar, in1=cacc[:, n, :],
                                                                   op0=ALU.mult, op1=ALU.add)
                                if n == 0 and tap == 0:
                                    ins.then_inc(conv_done, 1)
                            tap_link(ins, i, 2 + tap)
                    if r == 2:
                        dve.wait_ge(chunk_used, used)
                        dve.tensor_tensor(cy[:, bass.ds(i * 2, 2), :], cacc[:], pair_of(2), ALU.mult).then_inc(conv_round_done, 1)

                rounds(take, tail=2)
                links[0] += 4 * per_round
                for p in range(4):
                    sl = slice(2 * p, 2 * p + 2)
                    dve.wait_ge(yhi_ready, at.y + p + 1)
                    dve.tensor_tensor(xlo[:, sl, :], cy[:, sl, :], xhi[:, sl, :].bitcast(F32), ALU.subtract).then_inc(ylo_ready, 1)
                at.y += 4
                out_product()

            def mean_square(x, square, ssum, out, ready):
                link(dve.tensor_tensor(square, x, x, ALU.mult))
                link(dve.tensor_reduce(ssum, square, AX.X, ALU.add))
                dve.tensor_scalar(out, ssum, 1.0 / HD, EPS, ALU.mult, ALU.add).then_inc(ready, 1)

            def shared_kv():
                for slot in range(6):
                    split()
                normalise()
                split_ahead(1)
                x_low()

            def nsa():
                first = at.chunk
                split(width=KT * TAIL)
                split()
                dve.wait_ge(small_landed, 16 * 7)
                link(dve.tensor_tensor(kgain[:], kgain[:], qgain[:].unsqueeze(1).broadcast_to([P, 3, HD]), ALU.mult))
                split()
                dve.memset(kct[:], 0.0).then_inc(kct_zeroed, 1)
                link(dve.memset(czv, 0.0))
                dve.wait_ge(kn_kept, 4)
                mean_square(kn[:, 0:16, :], kd[:, 0:16, 0, :], kss[:, 0, 0:16], kss[:, 1, 0:16], kms_ready)
                split()

                def duplicate(n, lo, hi):
                    shape = [P, hi - lo, 2, HD]
                    g = kgain[:, n, :].unsqueeze(1).unsqueeze(1).broadcast_to(shape)
                    dve.tensor_tensor(kd[:, lo:hi], kn[:, lo:hi, :].unsqueeze(2).broadcast_to(shape), g, ALU.mult).then_inc(kd_ready, 1)

                dve.wait_ge(krs_ready, 1)
                link(dve.tensor_tensor(kn[:, 0:16, :], kn[:, 0:16, :], krs[:, 0:16].unsqueeze(2).broadcast_to([P, 16, HD]), ALU.mult))
                duplicate(1, 0, 8)
                duplicate(2, 8, 16)

                def q_chunk(q):
                    return xn[:, :, q * CW:(q + 1) * CW].rearrange("p t (h d) -> p t h d", h=4)

                def q_squares(q):
                    dve.wait_ge(q_kept, q + 1)
                    mean_square(q_chunk(q), qsq[:], qss[:, 0, q, :].rearrange("p (t h) -> p t h", t=TT), qss[:, 1, q, :], qms_ready)

                def q_scale(q):
                    dve.wait_ge(qrs_ready, q + 1)
                    dve.tensor_tensor(q_chunk(q), q_chunk(q), qrs[:, q, :].rearrange("p (t h) -> p t h", t=TT).unsqueeze(3)
                                      .broadcast_to([P, TT, 4, HD]), ALU.mult).then_inc(qn_ready, 1)

                q_squares(0)
                split()
                dve.wait_ge(pairs_landed, 16 * 8)
                for a in range(2):
                    for half in range(2):
                        pos = cols[:, R_POS + 16 * a + 8 * half:R_POS + 16 * a + 8 * half + 8].unsqueeze(2).unsqueeze(3)
                        dve.tensor_tensor(blk[a][:, 8 * half:8 * half + 8, :].rearrange("p j (g n) -> p j g n", g=NG), windows(a, half),
                                          pos.broadcast_to([P, 8, NG, N_CMP]), ALU.add).then_inc(blocks_ready, 1)
                dve.wait_ge(blocks_ready, 4)
                link(dve.memset(cp[:], 0.0))
                q_squares(1)
                q_scale(0)
                q_squares(2)
                q_scale(1)
                q_squares(3)
                q_scale(2)
                q_scale(3)
                for _ in range(4):
                    at.take_direct()

                def gelu(a):
                    dve.wait_ge(chunk_used, first + 5 + 2 * (a + 1))
                    for n in range(2):
                        part = slice((2 * a + n) * NG * N_CMP, (2 * a + n + 1) * NG * N_CMP)
                        ins = dve.tensor_scalar(cz[:, part], ps[:, C_BANKS[2 * a + n], 0:NG * N_CMP],
                                                cols[:, R_B1 + 2 * a + n:R_B1 + 2 * a + n + 1], None, ALU.add)
                    link(ins)
                    part = slice(2 * a * NG * N_CMP, 2 * (a + 1) * NG * N_CMP)
                    link(dve.tensor_tensor(cz2[:, part], cz[:, part], cz[:, part], ALU.mult))
                    link(dve.tensor_scalar(cz2[:, part], cz2[:, part], 0.044715, 1.0, ALU.mult, ALU.add))
                    dve.tensor_tensor(cz2[:, part], cz2[:, part], cz[:, part], ALU.mult).then_inc(gelu_in, 1)
                    dve.wait_ge(gelu_sig, a + 1)
                    return part

                part = gelu(0)
                dve.tensor_tensor(cz[:, part], cz[:, part], csig[:, part], ALU.mult).then_inc(gelu_ready, 1)
                link(dve.memset(kn[:, 16, :], 1.0))
                dve.wait_ge(cmp_done, 1)
                dve.tensor_copy(kn[0:NG * N_CMP, 16, :], ps[0:NG * N_CMP, 1, 0:HD]).then_inc(kc_kept, 1)
                dve.wait_ge(kc_kept, 1)
                mean_square(kn[:, 16, :], kd[:, 16, 0, :], kss[:, 0, 16:17], kss[:, 1, 16:17], kms_ready)
                dve.wait_ge(krs_ready, 2)
                link(dve.tensor_tensor(kn[:, 16, :], kn[:, 16, :], krs[:, 16:17].broadcast_to([P, HD]), ALU.mult))
                duplicate(0, 16, 17)
                part = gelu(1)
                for k in range(2):
                    z, sg = (x[:, (2 + k) * NG * N_CMP:(3 + k) * NG * N_CMP].rearrange("p (g n) -> p g n", g=NG).unsqueeze(2)
                             .broadcast_to([P, NG, 4, N_CMP]) for x in (cz, csig))
                    ins = dve.tensor_tensor(czv[:, k, :, :, 0:N_CMP], z, sg, ALU.mult)
                ins.then_inc(gelu_ready, 1)
                split_ahead(3)
                dve.wait_ge(cmp_scored, 1)
                for t in range(TT):
                    c = slice(C_CMP + t * N_CMP, C_CMP + (t + 1) * N_CMP)
                    ins = dve.scalar_tensor_tensor(out=cl[:, t, :].rearrange("p (h n) -> p h n", n=N_CMP), op0=ALU.mult, op1=ALU.add,
                                                   in0=ps[:, 3 + t, 0:NH * N_CMP].rearrange("p (h n) -> p h n", n=N_CMP), scalar=HD ** -0.5,
                                                   in1=const[:, c].unsqueeze(1).broadcast_to([P, NH, N_CMP]))
                link(ins)
                every = cl[:].rearrange("p t (h n) -> p (t h) n", h=NH)
                wide = [P, TT * NH, N_CMP]
                link(dve.tensor_reduce(cmx[:], every, AX.X, ALU.max))
                dve.tensor_tensor(every, every, cmx[:].unsqueeze(2).broadcast_to(wide), ALU.subtract).then_inc(cmp_shifted, 1)
                dve.wait_ge(cmp_exp, 1)
                link(dve.tensor_reduce(csum[:, 0, :], every, AX.X, ALU.add))
                link(dve.reciprocal(csum[:, 1, :], csum[:, 0, :]))
                dve.wait_ge(gates_ready, 1)
                gate = gates[:].rearrange("p t (h b) -> p (t h) b", b=3)
                link(dve.tensor_tensor(csum[:, 0, :], csum[:, 1, :], gate[:, :, 0], ALU.mult))
                link(dve.tensor_tensor(every, every, csum[:, 0, :].unsqueeze(2).broadcast_to(wide), ALU.mult))
                for t in range(TT):
                    c = slice(C_VALID + t * N_CMP, C_VALID + (t + 1) * N_CMP)
                    dve.tensor_tensor(cp[:, t, :, 0:N_CMP], cl[:, t, :].rearrange("p (h n) -> p h n", h=NH),
                                      const[:, c].unsqueeze(1).broadcast_to([P, NH, N_CMP]), ALU.mult).then_inc(cmp_probs, 1)
                dve.wait_ge(cmp_done, 2)
                dve.tensor_copy(vc[:], ps[:, 1, 0:NG * HD].rearrange("p (g d) -> p g d", g=NG)).then_inc(vc_kept, 1)
                attention(NH // 2, 2, nsa_out, None, HD ** -0.5,
                          lambda u: gates[:].rearrange("p t (h b) -> p t h b", b=3)[:, :, 2 * (u // 2):2 * (u // 2) + 2, 1 + u % 2])
                out_product()

            for n, free_at_start in enumerate((bank_free[0], hid_ready, conv_done)):
                dve.memset(token[:, n:n + 1], 0.0).then_inc(free_at_start, 1)
            dve.memset(zero[:], 0.0).then_inc(zero_ready, 1)
            dve.memset(table[BUCKETS:BUCKETS + 1, :], NEG).then_inc(zero_ready, 1)
            for name in phases:
                at.last = name == weighty[-1]
                if name == "final":
                    normalise(turns=False)
                    at.h += 1
                elif name != "ffn4" or "kv" not in phases:
                    normalise()
                    if at.chunk == 0:
                        split_ahead(1)
                    x_low()
                if name == phases[0]:
                    split_ahead(3)
                    dve.wait_ge(cols_turned, 1)
                    dve.tensor_copy(cols[:], ps[:, 3, 0:ROWS]).then_inc(cols_ready, 1)
                    dve.wait_ge(cols_ready, 1)
                    dve.wait_ge(const_landed, 16)
                    dve.tensor_copy(ident_b[:], ident)
                    dve.tensor_copy(mask_b[:], causal[:, P:3 * P]).then_inc(zero_ready, 1)
                if name == "hgrn":
                    scale = hgrn()
                    dve.wait_ge(orms_ready, 1)
                    at.chunk -= 3
                    at.split = at.chunk + 3
                    out_product(scale)
                elif name.startswith("ffn"):
                    ffn(1.0 if name in ("ffn0", "ffn1") else 0.5)
                elif name != "final":
                    {"moba": moba, "conv": conv, "kv": shared_kv, "nsa": nsa}[name]()

        @block.tensor
        def _(pe):
            at = Place()

            def free(bank, i=0):
                n = at.fills[bank]
                at.fills[bank] += 1
                if not isinstance(i, int) or n + i > 0:
                    pe.wait_ge(bank_free[bank], i + n)

            def x_high(k, tiles=(0, 1)):
                if at.fresh and k % 4 == 0:
                    pe.wait_ge(xhi_ready, at.turned - 4 + 2 * tiles[-1] + k // 4 + 1)

            def x_low(k, tiles=(0, 1)):
                if at.fresh and k % 4 == 0:
                    for t in tiles:
                        bank = 4 + 2 * t + k // 4
                        pe.wait_ge(bank_free[bank], at.fills[bank])
                    if tiles[-1] == 1 and k == 4:
                        at.fresh = False

            def across(bank, i=0):
                c = at.chunk
                at.chunk += 1
                pe.wait_ge(split_lo, i * RING + (at.splits(c) + 1))
                hi, lo = thirds(whi[c % RING][:]), thirds(wlo[c % RING][:])
                for n in range(2):
                    out = ps[:, bank, n * S:(n + 1) * S]
                    tile = slice(n * P, (n + 1) * P)
                    for k in range(KT):
                        x_high(k)
                        pe.matmul(out, hi[:, k, tile], xhi[:, k, :], start=k == 0, stop=False)
                        pe.matmul(out, lo[:, k, tile], xhi[:, k, :], start=False, stop=False)
                    for k in range(KT):
                        x_low(k)
                        mm = pe.matmul(out, hi[:, k, tile], xlo[:, k, :], start=False, stop=k == KT - 1)
                mm.then_inc(chunk_used, 1)

            def along(bank, i=0, width=CW, piece=None):
                c = at.chunk
                at.chunk += 1
                pe.wait_ge(split_lo, i * RING + (at.splits(c) + 1))
                hi, lo = thirds(whi[c % RING][:, 0:KT * width]), thirds(wlo[c % RING][:, 0:KT * width])
                for t in range(TT):
                    out = ps[:, bank, t * width:(t + 1) * width]
                    tile = slice(t * P, (t + 1) * P)
                    if piece is not None:
                        for k in range(KT):
                            if t == 0:
                                piece(k)
                            pe.matmul(out, xhi[:, k, tile], hi[:, k, :], start=k == 0, stop=False)
                            pe.matmul(out, xhi[:, k, tile], lo[:, k, :], start=False, stop=False)
                            mm = pe.matmul(out, xlo[:, k, tile], hi[:, k, :], start=False, stop=k == KT - 1)
                        continue
                    for k in range(KT):
                        x_high(k, (t,))
                        pe.matmul(out, xhi[:, k, tile], hi[:, k, :], start=k == 0, stop=False)
                        pe.matmul(out, xhi[:, k, tile], lo[:, k, :], start=False, stop=False)
                    for k in range(KT):
                        x_low(k, (t,))
                        mm = pe.matmul(out, xlo[:, k, tile], hi[:, k, :], start=False, stop=k == KT - 1)
                mm.then_inc(chunk_used, 1)

            def keep_warm(n, bank=7):
                for _ in range(n):
                    pe.matmul(ps[:, bank, :], zero[:, 0:P], zero[:], start=True, stop=True)

            def norm(after):
                for g in range(4):
                    t, half = g // 2, g % 2
                    keep_warm(WARM[after][g])
                    pe.wait_ge(xn_ready, at.xn + g + 1)
                    free(4 + g)
                    for k in range(4):
                        kk = 4 * half + k
                        mm = pe.transpose(ps[:, 4 + g, k * P:(k + 1) * P], xn[:, t, kk * P:(kk + 1) * P], ident)
                    mm.then_inc(turned, 1)
                at.xn += 4
                at.turned += 4
                at.fresh = True

            def out_product(pieces=4, free_banks=None, sums=False):
                def piece(k):
                    if sums and k in (2, 4, 6):
                        keep_warm(3, bank=3)
                    if k % (KT // pieces) == 0:
                        pe.wait_ge(ylo_ready, at.y - pieces + k // (KT // pieces) + 1)

                if sums:
                    pe.wait_ge(bank_free[3], at.fills[3])
                    keep_warm(8, bank=3)
                for q in range(4):
                    if free_banks is not None:
                        pe.wait_ge(*free_banks[q])
                    elif at.fills[q]:
                        pe.wait_ge(bank_free[q], at.fills[q])
                    along(q, piece=piece if q == 0 else None)
                    if sums and q == 0:
                        pe.wait_ge(heads_summed, 3)
                        for t in range(TT):
                            mm = pe.matmul(ps[:, 4, t:t + 1], gq[:, 0, t * P:(t + 1) * P], one, start=True, stop=True)
                        mm.then_inc(o_summed, 1)

            def ffn(after_kv):
                pe.wait_ge(zero_ready, 1)

                def down(i=0, high=hhi, low=hlo, last=False):
                    c = at.chunk
                    at.chunk += 1
                    pe.wait_ge(split_lo, i * RING + (at.splits(c) + 1))
                    hi = whi[c % RING][:].rearrange("p (k n) -> p k n", k=2)
                    lo = wlo[c % RING][:].rearrange("p (k n) -> p k n", k=2)
                    for n, (t, half) in enumerate(halves(True)):
                        tile = slice(t * P, (t + 1) * P)
                        for k in range(2):
                            for a, b in ((high, hi), (high, lo), (low, hi)):
                                mm = pe.matmul(ps[:, 2 * t + half, :], a[:, k, tile], b[:, k, half * 512:(half + 1) * 512],
                                               start=False, stop=last and k == 1 and b is hi and a is low,
                                               skip_group_check=True)
                        if last and n < 3:
                            mm.then_inc(half_summed, 1)
                    mm.then_inc(chunk_used, 1)

                pe.wait_ge(bank_free[4], at.fills[4])
                across(4)
                across(5)
                for b in range(4):
                    if at.fills[b]:
                        pe.wait_ge(bank_free[b], at.fills[b])
                    if after_kv:
                        pe.wait_ge(kn_kept, 4)
                    pe.matmul(ps[:, b, :], zero[:, 0:P], zero[:], start=True, stop=False, skip_group_check=True)
                with pe.Fori(0, PAIRS - 2) as i:
                    pe.wait_ge(silu_ready, i + (at.hids + 1))
                    across(4, i)
                    pe.wait_ge(hlo_ready, i + (at.hids + 1))
                    down(i)
                    across(5, i)
                at.chunk += 3 * (PAIRS - 3)
                at.hids += PAIRS
                pe.wait_ge(silu_ready, at.hids - 1)
                across(4)
                pe.wait_ge(hid_ready, at.hids)
                across(5)
                pe.wait_ge(hlo_ready, at.hids - 1)
                down()
                pe.wait_ge(hlo_ready, at.hids)
                down(high=xhi, low=xlo, last=True)

            def rounds(kinds, n=4):
                for r in range(3):
                    free(r)
                    kinds[r](r)
                    if at.chunk == 1:
                        pe.wait_ge(rows_landed, 16 * 5)
                        pe.transpose(ps[:, 3, 0:ROWS], rows[:], ident[0:ROWS, 0:ROWS]).then_inc(cols_turned, 1)
                with pe.Fori(0, n - 1) as i:
                    for r in range(3):
                        free(r, i)
                        kinds[r](r, i)
                at.chunk += 3 * (n - 2)
                for r in range(3):
                    at.fills[r] += n - 2

            def hgrn():
                rounds((across, across, across))
                pe.wait_ge(small_landed, 16 * 7)
                pe.matmul(ps[0:HEADS, 7, :], table[:], places[:], start=True, stop=True).then_inc(bias_rowed, 1)
                pe.wait_ge(const_landed, 16)
                for s in range(LEVELS + 1):
                    for hg in range(2):
                        if s == 0:
                            pe.wait_ge(cols_ready, 1)
                            pe.wait_ge(bank_free[0], 5)
                            pe.wait_ge(fk_ready, 4)
                        else:
                            pe.wait_ge(q_ready, 2 * (s - 1) + hg + 1)
                        if s >= 2:
                            pe.wait_ge(k_ready, 2 * (s - 2) + hg + 1)
                        if s == LEVELS:
                            free(2 * hg)
                            for a in range(4):
                                hd = 4 * hg + a
                                mm = pe.matmul(ps[:, 2 * hg, a * P:(a + 1) * P], gk[:, hd, 0:P], gq[:, hd, P:2 * P], start=True, stop=True)
                            mm.then_inc(level_scored, 1)
                            continue
                        for t in range(TT):
                            tile = slice(t * P, (t + 1) * P)
                            free(2 * hg + t)
                            for a in range(4):
                                hd = 4 * hg + a
                                mm = pe.matmul(ps[:, 2 * hg + t, a * P:(a + 1) * P], gk[:, hd, tile], gq[:, hd, tile], start=True, stop=True)
                        mm.then_inc(level_scored, 1)
                    if s % 2 == 1:
                        free(4 + s // 2 % 2)
                        along(4 + s // 2 % 2)
                pe.wait_ge(bias_copied, 1)
                for p in range(4):
                    bank = 4 + p
                    hg = p // 2
                    pe.wait_ge(bank_free[2 * hg], at.fills[2 * hg])
                    pe.wait_ge(bank_free[bank], at.fills[bank])
                    for a in range(2):
                        hd = 2 * p + a
                        wide = slice(hd * P, (hd + 1) * P)
                        o = ps[:, bank, a * S:(a + 1) * S]
                        pe.matmul(o[:, 0:P], gin[:, 0, wide], gsc[:, hd, 0, :], start=True, stop=True)
                        pe.matmul(o[:, P:S], gin[:, 0, wide], gsc[:, hd, 2, :], start=True, stop=False)
                        mm = pe.matmul(o[:, P:S], gin[:, 1, wide], gsc[:, hd, 1, :], start=False, stop=True)
                    mm.then_inc(o_ready, 1)
                at.y += 4

            def attention(pairs, branches, q_of, k_of, pv, masked=False, warm=(0, 0)):
                units = pairs * branches
                for b in range(8):
                    if at.fills[b]:
                        pe.wait_ge(bank_free[b], at.fills[b])

                def logits(u):
                    if u >= 2:
                        pe.wait_ge(exp_ready if masked else max_ready, at.att + u - 1)
                    for a in range(2):
                        q, k = q_of(u, a), k_of(u, a)
                        bank = 2 * (u % 2) + a
                        mm = pe.matmul(ps[:, bank, 0:P], q[:, 0:P], k[:, 0:P], start=True, stop=not masked)
                        if masked:
                            mm = pe.matmul(ps[:, bank, 0:P], ident_b[:], mask_b[:, P:2 * P], start=False, stop=True)
                        mm = pe.matmul(ps[:, bank, P:3 * P], q[:, P:S], k, start=True, stop=not masked)
                        if masked:
                            mm = pe.matmul(ps[:, bank, P:3 * P], ident_b[:], mask_b[:], start=False, stop=True)
                    mm.then_inc(scored, 1)

                def turn(u):
                    pe.wait_ge(probs_ready, at.att + u + 1)
                    if u >= 1:
                        pe.wait_ge(pt_ready, at.att + u)
                    for a in range(2):
                        for n in range(3):
                            mm = pe.transpose(ps[:, 4 + a, n * P:(n + 1) * P], att_l[:, u % 2, a, n * P:(n + 1) * P], ident)
                    mm.then_inc(probs_turned, 1)

                def values(u):
                    pe.wait_ge(pt_ready, at.att + u + 1)
                    pair = u // branches
                    if pair and u % branches == 0:
                        pe.wait_ge(ylo_ready, at.y + pair)
                    pv(u, att_pt[:, u % 2]).then_inc(pv_done, 1)

                logits(0)
                for i in range(units + 2):
                    if i + 1 < units:
                        logits(i + 1)
                    if i == 0:
                        keep_warm(warm[0])
                    if i >= 2:
                        values(i - 2)
                        if i - 1 < units:
                            keep_warm(warm[1], bank=4)
                    if 0 <= i - 1 < units:
                        turn(i - 1)
                at.att += units
                at.y += pairs

            def moba():
                rounds((across, across, along))

                def pv(u, pt):
                    for a in range(2):
                        v = mv[:, :, (2 * u + a) * P:(2 * u + a + 1) * P]
                        part = slice(a * P, (a + 1) * P)
                        pe.matmul(ps[:, 6, part], v[:, 0, :], pt[:, a, 0:P], start=True, stop=True)
                        pe.matmul(ps[:, 7, part], v[:, 0, :], pt[:, a, P:2 * P], start=True, stop=False)
                        mm = pe.matmul(ps[:, 7, part], v[:, 1, :], pt[:, a, 2 * P:3 * P], start=False, stop=True)
                    return mm

                attention(HEADS // 2, 1, lambda u, a: mq[:, 2 * u + a, :], lambda u, a: mk[:, 2 * u + a, :], pv, warm=WARM_MOBA)
                out_product()

            def conv():
                for r in range(3):
                    if at.fills[r]:
                        pe.wait_ge(bank_free[r], at.fills[r])
                for r, kind in enumerate((across, across, across)):
                    kind(r)
                with pe.Fori(0, 3) as i:
                    for r in range(3):
                        pe.wait_ge((conv_done, conv_done, conv_round_done)[r], i + (2, 2, 1)[r])
                        across(r, i)
                at.chunk += 6
                at.y += 4
                keep_warm(6)
                out_product(free_banks=((conv_done, 5), (conv_done, 5), (conv_round_done, 4), (conv_round_done, 4)))

            def shared_kv():
                for slot in range(6):
                    bank = slot % 4
                    if slot < 4:
                        if at.fills[bank]:
                            pe.wait_ge(bank_free[bank], at.fills[bank])
                    else:
                        pe.wait_ge(raw_kept, slot - 3)
                    if slot == 5:
                        norm("kv")
                        at.fresh = False
                    (across if slot < 2 else along)(bank)
                at.fresh = True

            def nsa():
                c = at.chunk
                at.chunk += 1
                pe.wait_ge(split_lo, at.splits(c) + 1)
                hi, lo = thirds(whi[c % RING][:, 0:KT * TAIL]), thirds(wlo[c % RING][:, 0:KT * TAIL])
                out = ps[0:TAIL, 0, 0:S]
                for k in range(KT):
                    x_high(k)
                    pe.matmul(out, hi[:, k, :], xhi[:, k, :], start=k == 0, stop=False)
                    pe.matmul(out, lo[:, k, :], xhi[:, k, :], start=False, stop=False)
                for k in range(KT):
                    x_low(k)
                    mm = pe.matmul(out, hi[:, k, :], xlo[:, k, :], start=False, stop=k == KT - 1)
                mm.then_inc(chunk_used, 1)
                along(1)
                along(2)
                pe.wait_ge(gates_t_ready, 1)
                for t in range(TT):
                    mm = pe.transpose(ps[:, 0, t * TAIL:(t + 1) * TAIL], gates_t[:, t * P:(t + 1) * P], ident[0:TAIL, 0:TAIL])
                mm.then_inc(gates_turned, 1)
                along(3)
                pe.wait_ge(kd_ready, 2)
                for n in range(4):
                    if n == 3:
                        pe.wait_ge(gates_ready, 1)
                    for g in range(NG):
                        mm = pe.transpose(ps[:, KT_BANKS[n], g * P:(g + 1) * P], kd[:, 4 * n + g].rearrange("p a d -> p (a d)"), ident)
                    mm.then_inc(kt_turned, 1)
                along(4)

                def compress(a, half):
                    c = at.chunk
                    at.take_direct()
                    pe.wait_ge(landed[c % RING], 16 * (c // RING + 1))
                    pe.wait_ge(blocks_ready, 2 * a + half + 1)
                    if half == 0:
                        pe.wait_ge(kt_kept, 2 * a + 2)
                    for n in range(2):
                        for k in range(KT):
                            mm = pe.matmul(ps[:, C_BANKS[2 * a + n], 0:NG * N_CMP], thirds(raw[c % RING][:])[:, k, n * P:(n + 1) * P],
                                           blk[a][:, 8 * half + k, :], start=half == 0 and k == 0, stop=half == 1 and k == KT - 1)
                    mm.then_inc(chunk_used, 1)

                compress(0, 0)
                compress(0, 1)
                compress(1, 0)
                pe.wait_ge(gelu_ready, 1)
                pe.wait_ge(q_kept, 1)
                for k in range(2):
                    mm = pe.matmul(ps[0:NG * N_CMP, 1, 0:HD], cz[:, k * NG * N_CMP:(k + 1) * NG * N_CMP], w2sb[:, k, :], start=k == 0, stop=k == 1)
                mm.then_inc(cmp_done, 1)
                compress(1, 1)
                pe.wait_ge(q_kept, 4)
                for n in range(4):
                    t, half = n // 2, n % 2
                    pe.wait_ge(qn_ready, 4 if half else 2)
                    for k in range(4):
                        kk = 4 * half + k
                        mm = pe.transpose(ps[:, 3 + n, k * P:(k + 1) * P], xn[:, t, kk * P:(kk + 1) * P], ident)
                    mm.then_inc(q_turned, 1)
                pe.wait_ge(kd_ready, 3)
                c = NG * N_CMP
                pe.transpose(ps[:, 2, 0:c], kd[0:c, 16].rearrange("p a d -> p (a d)"), ident[0:c, 0:c]).then_inc(kt_turned, 1)
                pe.wait_ge(nq_ready, 4)
                pe.wait_ge(kct_ready, 2)
                for t in range(TT):
                    for pair in range(NH // 2):
                        mm = pe.matmul(ps[:, 3 + t, pair * 2 * N_CMP:(pair + 1) * 2 * N_CMP], nq[:, pair, t * P:(t + 1) * P],
                                       kct[:, pair // 2].rearrange("p a n -> p (a n)"), start=True, stop=True)
                mm.then_inc(cmp_scored, 1)
                pe.wait_ge(gelu_ready, 2)
                pe.wait_ge(kc_kept, 1)
                for g in range(NG):
                    for k in range(2):
                        mm = pe.matmul(ps[:, 1, g * HD:(g + 1) * HD], czv[:, k, g].rearrange("p h n -> p (h n)"), w2sb[:, 2 + k, :],
                                       start=k == 0, stop=k == 1)
                mm.then_inc(cmp_done, 1)
                pe.wait_ge(kct_ready, 2)
                keep_warm(WARM_CMP, bank=2)
                for t in range(TT):
                    pe.wait_ge(cmp_probs, t + 1)
                    for g in range(NG):
                        mm = pe.transpose(ps[:, 5 + t, g * P:(g + 1) * P], cp[:, t, 4 * g:4 * g + 4, :].rearrange("p h n -> p (h n)"), ident)
                    mm.then_inc(cmp_turned, 1)
                pe.wait_ge(cpt_ready, 2)
                pe.wait_ge(vc_kept, 1)

                def q_of(u, a):
                    return nq[a * HD:(a + 1) * HD, u // 2, :]

                def k_of(u, a):
                    return kt[a * HD:(a + 1) * HD, u % 2, u // 4, :]

                def pv(u, pt):
                    pair, branch = u // 2, u % 2
                    g = pair // 2
                    for a in range(2):
                        hd = 2 * pair + a
                        out = [ps[a * HD:(a + 1) * HD, 6 + t, 0:P] for t in range(TT)]
                        if branch == 0:
                            rows_c = slice(32 * (hd % 4), 32 * (hd % 4) + N_CMP)
                            for t in range(TT):
                                pe.matmul(out[t], vc[rows_c, g, :], cpt[rows_c, g, t * P:(t + 1) * P], start=True, stop=False)
                        v = vn[:, branch, :, g * HD:(g + 1) * HD]
                        last = branch == 1
                        pe.matmul(out[0], v[:, 0, :], pt[:, a, 0:P], start=False, stop=last)
                        pe.matmul(out[1], v[:, 0, :], pt[:, a, P:2 * P], start=False, stop=False)
                        mm = pe.matmul(out[1], v[:, 1, :], pt[:, a, 2 * P:3 * P], start=False, stop=last)
                    return mm

                pe.wait_ge(zero_ready, 3)
                attention(NH // 2, 2, q_of, k_of, pv, masked=True, warm=WARM_NSA)
                out_product(pieces=8)

            pe.wait_ge(zero_ready, 2)
            keep_warm(WARM_START)
            pe.wait_ge(ident_landed, 32)
            after = "start"
            for name in phases:
                if name == "final":
                    continue
                if name != "ffn4" or "kv" not in phases:
                    norm(after)
                if name == phases[0]:
                    keep_warm(WARM_FIRST, bank=3)
                after = ("final" if name == "ffn1" else "swiglu") if name.startswith("ffn") else "mixer"
                if name == "hgrn":
                    hgrn()
                    out_product(sums=True)
                elif name.startswith("ffn"):
                    ffn(name == "ffn4" and "kv" in phases)
                else:
                    {"moba": moba, "conv": conv, "kv": shared_kv, "nsa": nsa}[name]()


_INS = ['x', 'norm_mix', 'norm_ffn', 'hgrn_w_in', 'hgrn_lb_logits', 'hgrn_out_norm', 'hgrn_w_out', 'moba_w_in', 'moba_w_out', 'rel_bias_table', 'ffn_w13', 'ffn_w2', 'final_norm', 'ffn_norm_2', 'ffn_w_gate_up_2', 'ffn_w_down_2', 'mix_norm_2', 'conv_w_in_2', 'conv_w_2', 'conv_w_out_2', 'kv_norm_2', 'kv_w_2', 'cmp_pos_2', 'cmp_w1_2', 'cmp_b1_2', 'cmp_w2_2', 'k_norm_2', 'nsa_w_qg_2', 'q_norm_2', 'nsa_w_o_2']


def kernel(**inputs):
    import concourse.bacc as bacc
    from concourse.bass_utils import run_bass_kernel_spmd

    nc = bacc.Bacc("TRN2", target_bir_lowering=False, num_devices=1)
    masks, places = constants()
    arrays = {name: np.ascontiguousarray(inputs[name]) for name in _INS}
    arrays["masks"], arrays["places"] = masks, places
    w = {name: nc.dram_tensor(f"in_{name}", a.shape, mybir.dt.from_np(a.dtype), kind="ExternalInput").ap() for name, a in arrays.items()}
    out = nc.dram_tensor("out_0", (1, S, D), F32, kind="ExternalOutput").ap()
    build(nc, w, out)
    r = run_bass_kernel_spmd(nc, [{f"in_{name}": a for name, a in arrays.items()}], core_ids=[0])
    return r.results[0]["out_0"]
```
